# Optimizing a Trainium2 kernel written in Bass

```python
import math
import jax, jax.numpy as jnp
from jax import lax
import numpy as np

D_MODEL = 1024
BATCH = 1
SEQ = 512
DEPTH = 1
DEC_BATCH = 8
DEC_SEQ = 4
PAST_LEN = 1024
PAGE_SIZE = 128

NSA_HEADS = 16
NSA_GROUPS = 4
NSA_HPG = NSA_HEADS // NSA_GROUPS
NSA_DK = D_MODEL // NSA_HEADS
CMP_BLOCK = 32
CMP_STRIDE = 16
CMP_HID = 4 * NSA_DK
SEL_BLOCK = 64
N_SEL = 16
WINDOW = 512
FORCE_BONUS = 1e4
N_KV_SLOTS = 4
DIFF_HEADS = 8
DIFF_DD = D_MODEL // (2 * DIFF_HEADS)
DIFF_DV = 2 * DIFF_DD
D_FF = 4 * D_MODEL
NUM_BUCKETS = 32
MAX_DISTANCE = 128
Q_BLOCK = 128
EPS = 1e-6
NEG_INF = -1e30
TINY = 1e-30
SPLIT_SIZES = (NSA_HEADS * NSA_DK, 6 * NSA_GROUPS * NSA_DK, 3 * NSA_HEADS,
               2 * DIFF_HEADS * DIFF_DD, 2 * DIFF_HEADS * DIFF_DD, DIFF_HEADS * DIFF_DV,
               D_MODEL, D_MODEL)
SPLIT_POINTS = tuple(int(v) for v in np.cumsum(SPLIT_SIZES)[:-1])
N_IN = int(sum(SPLIT_SIZES))

kernel_name = "nsa_diffattn_gated_hybrid_step"

def rmsnorm(x, g):
    xf = x.astype(jnp.float32)
    y = xf * lax.rsqrt(jnp.mean(xf * xf, axis=-1, keepdims=True) + EPS)
    return (y * g.astype(jnp.float32)).astype(x.dtype)

def masked_softmax(s, mask):
    s = jnp.where(mask, s, NEG_INF)
    m = jnp.max(s, axis=-1, keepdims=True)
    p = jnp.where(mask, jnp.exp(s - m), 0.0)
    return p / jnp.maximum(jnp.sum(p, axis=-1, keepdims=True), TINY)

def t5_bucket(dist):
    n = jnp.maximum(dist, 0)
    max_exact = NUM_BUCKETS // 2
    nf = jnp.maximum(n, 1).astype(jnp.float32)
    log_ratio = jnp.log(nf / max_exact) / math.log(MAX_DISTANCE / max_exact)
    large = max_exact + (log_ratio * (NUM_BUCKETS - max_exact)).astype(jnp.int32)
    large = jnp.minimum(large, NUM_BUCKETS - 1)
    return jnp.where(n < max_exact, n, large)

def sweep_query_blocks(fn, T):
    qb = Q_BLOCK if T % Q_BLOCK == 0 else T
    starts = jnp.arange(T // qb, dtype=jnp.int32) * qb
    out = lax.map(lambda s: fn(s, qb), starts)
    out = jnp.moveaxis(out, 0, 1)
    return out.reshape((out.shape[0], T) + out.shape[3:])

def compress_rows(rows, pe, w1, w2):
    B, L = rows.shape[:2]
    R = CMP_BLOCK // CMP_STRIDE
    nch = -(-L // CMP_STRIDE)
    rows = jnp.pad(rows, ((0, 0), (0, nch * CMP_STRIDE - L), (0, 0), (0, 0)))
    chunks = rows.reshape(B, nch, CMP_STRIDE, NSA_GROUPS, NSA_DK)
    w1r = w1.reshape(R, CMP_STRIDE, NSA_DK, CMP_HID)
    nc = nch - R + 1
    h = jnp.einsum('ld,ldh->h', pe, w1.reshape(CMP_BLOCK, NSA_DK, CMP_HID))
    for r in range(R):
        part = jnp.einsum('bcjgd,jdh->bcgh', chunks, w1r[r])
        h = h + part[:, r:r + nc]
    return jnp.einsum('bcgh,hd->bcgd', jax.nn.gelu(h), w2)

def cmp_sel_weights(nc, n_slc):
    c0 = np.arange(nc)[:, None] * CMP_STRIDE
    s0 = np.arange(n_slc)[None, :] * SEL_BLOCK
    shared = np.clip(np.minimum(c0 + CMP_BLOCK, s0 + SEL_BLOCK) - np.maximum(c0, s0), 0, None)
    return jnp.asarray(shared / CMP_BLOCK, dtype=jnp.float32)

def nsa_mixer(q, gates, kv_all, win_all, tab_nsa, pe_k, w1_k, w2_k, pe_v, w1_v, w2_v, k_gain):
    B, T = q.shape[:2]
    L = kv_all.shape[1]
    t0 = L - T
    scale = NSA_DK ** -0.5
    kc = rmsnorm(compress_rows(kv_all[:, :, 0], pe_k, w1_k, w2_k), k_gain)
    vc = compress_rows(kv_all[:, :, 1], pe_v, w1_v, w2_v)
    nc = kc.shape[1]
    cmp_end = jnp.arange(nc, dtype=jnp.int32) * CMP_STRIDE + (CMP_BLOCK - 1)
    n_slc = -(-L // SEL_BLOCK)
    pad = n_slc * SEL_BLOCK - L

    def to_blocks(r):
        r = jnp.pad(r, ((0, 0), (0, pad), (0, 0), (0, 0)))
        return r.reshape(B, n_slc, SEL_BLOCK, NSA_GROUPS, NSA_DK).transpose(0, 3, 1, 2, 4)

    ksb = to_blocks(kv_all[:, :, 2])
    vsb = to_blocks(kv_all[:, :, 3])
    sel_w = cmp_sel_weights(nc, n_slc)
    n_top = min(N_SEL, n_slc)
    blk_ids = jnp.arange(n_slc, dtype=jnp.int32)
    tok_ids = jnp.arange(SEL_BLOCK, dtype=jnp.int32)
    k_win, v_win = win_all[:, :, 0], win_all[:, :, 1]
    qg = q.reshape(B, T, NSA_GROUPS, NSA_HPG, NSA_DK)
    gg = gates.reshape(B, T, NSA_GROUPS, NSA_HPG, 3)
    tab_g = tab_nsa.reshape(NUM_BUCKETS, NSA_GROUPS, NSA_HPG)
    gather = jax.vmap(jax.vmap(lambda blocks, ix: blocks[ix]))
    g_ids = jnp.arange(NSA_GROUPS)[None, :, None, None]

    def head_bias(dist):
        return tab_g[t5_bucket(dist)].astype(jnp.float32).transpose(2, 3, 0, 1)

    def block(s, qb):
        qbk = lax.dynamic_slice_in_dim(qg, s, qb, axis=1)
        gb = lax.dynamic_slice_in_dim(gg, s, qb, axis=1)
        tq = t0 + s + jnp.arange(qb, dtype=jnp.int32)
        dc = tq[:, None] - cmp_end[None, :]
        s_c = jnp.einsum('bqghd,bcgd->bghqc', qbk, kc).astype(jnp.float32) * scale + head_bias(dc)
        p_c = masked_softmax(s_c, dc >= 0)
        o_c = jnp.einsum('bghqc,bcgd->bqghd', p_c.astype(vc.dtype), vc)
        imp = jnp.einsum('bghqc,cn->bgqn', p_c, sel_w)
        cur = tq[:, None] // SEL_BLOCK
        forced = (blk_ids[None] == 0) | (blk_ids[None] == cur) | (blk_ids[None] == cur - 1)
        valid = blk_ids[None] * SEL_BLOCK <= tq[:, None]
        score = jnp.where(valid, imp + jnp.where(forced, FORCE_BONUS, 0.0), -FORCE_BONUS)
        _, idx = lax.top_k(score, n_top)
        nk = n_top * SEL_BLOCK
        kg = gather(ksb, idx).reshape(B, NSA_GROUPS, qb, nk, NSA_DK)
        vg = gather(vsb, idx).reshape(B, NSA_GROUPS, qb, nk, NSA_DK)
        pos = (idx[..., None] * SEL_BLOCK + tok_ids).reshape(B, NSA_GROUPS, qb, nk)
        ds = tq[None, None, :, None] - pos
        bias_s = tab_g[t5_bucket(ds), g_ids].astype(jnp.float32).transpose(0, 1, 4, 2, 3)
        s_s = jnp.einsum('bqghd,bgqkd->bghqk', qbk, kg).astype(jnp.float32) * scale + bias_s
        p_s = masked_softmax(s_s, (ds >= 0)[:, :, None])
        o_s = jnp.einsum('bghqk,bgqkd->bqghd', p_s.astype(vg.dtype), vg)
        lw = WINDOW + qb
        kw = lax.dynamic_slice_in_dim(k_win, s, lw, axis=1)
        vw = lax.dynamic_slice_in_dim(v_win, s, lw, axis=1)
        kpos = t0 - WINDOW + s + jnp.arange(lw, dtype=jnp.int32)
        dw = tq[:, None] - kpos[None, :]
        mask_w = (kpos[None, :] >= 0) & (dw >= 0) & (dw < WINDOW)
        s_w = jnp.einsum('bqghd,bkgd->bghqk', qbk, kw).astype(jnp.float32) * scale + head_bias(dw)
        p_w = masked_softmax(s_w, mask_w)
        o_w = jnp.einsum('bghqk,bkgd->bqghd', p_w.astype(vw.dtype), vw)
        return gb[..., 0:1] * o_c + gb[..., 1:2] * o_s + gb[..., 2:3] * o_w

    o = sweep_query_blocks(block, T)
    return o.reshape(B, T, NSA_HEADS * NSA_DK)

def diff_mixer(q1, q2, k1, k2, v, lam, lam_init, subln_g, tab_diff):
    B, T = q1.shape[:2]
    L = k1.shape[1]
    t0 = L - T
    scale = DIFF_DD ** -0.5
    kpos = jnp.arange(L, dtype=jnp.int32)

    def block(s, qb):
        q1b = lax.dynamic_slice_in_dim(q1, s, qb, axis=1)
        q2b = lax.dynamic_slice_in_dim(q2, s, qb, axis=1)
        tq = t0 + s + jnp.arange(qb, dtype=jnp.int32)
        dist = tq[:, None] - kpos[None, :]
        bias = tab_diff[t5_bucket(dist)].astype(jnp.float32).transpose(2, 0, 1)
        mask = dist >= 0
        s1 = jnp.einsum('bqhd,bkhd->bhqk', q1b, k1).astype(jnp.float32) * scale + bias
        s2 = jnp.einsum('bqhd,bkhd->bhqk', q2b, k2).astype(jnp.float32) * scale + bias
        a = masked_softmax(s1, mask) - lam * masked_softmax(s2, mask)
        return jnp.einsum('bhqk,bkhd->bqhd', a.astype(v.dtype), v)

    o = sweep_query_blocks(block, T)
    o = rmsnorm(o, subln_g) * (1.0 - lam_init)
    return o.reshape(B, T, DIFF_HEADS * DIFF_DV)

def decoder_layer(x, past_nsa, past_diff, past_win, win_keep, lam_init, lam, tab,
                  attn_g, w_in, q_g, k_g, pe_k, w1_k, w2_k, pe_v, w1_v, w2_v,
                  dq_g, dk_g, subln_g, w_o, mlp_g, w_up, w_down):
    B, T, _ = x.shape
    xn = rmsnorm(x, attn_g)
    proj = jnp.einsum('btd,de->bte', xn, w_in)
    q_n, kv_n, g_n, q_d, k_d, v_d, ga, gb = jnp.split(proj, SPLIT_POINTS, axis=-1)
    q = rmsnorm(q_n.reshape(B, T, NSA_HEADS, NSA_DK), q_g)
    kv = kv_n.reshape(B, T, 6, NSA_GROUPS, NSA_DK)
    k_sel = rmsnorm(kv[:, :, 2], k_g)
    k_win = rmsnorm(kv[:, :, 4], k_g)
    new_nsa = jnp.stack([kv[:, :, 0], kv[:, :, 1], k_sel, kv[:, :, 3]], axis=2)
    new_win = jnp.stack([k_win, kv[:, :, 5]], axis=2)
    gates = jax.nn.sigmoid(g_n.reshape(B, T, NSA_HEADS, 3))
    kv_all = jnp.concatenate([past_nsa, new_nsa], axis=1)
    win_all = jnp.concatenate([past_win, new_win], axis=1)
    o_a = nsa_mixer(q, gates, kv_all, win_all, tab[:, :NSA_HEADS],
                    pe_k, w1_k, w2_k, pe_v, w1_v, w2_v, k_g)
    qd = rmsnorm(q_d.reshape(B, T, DIFF_HEADS, 2, DIFF_DD), dq_g)
    kd = rmsnorm(k_d.reshape(B, T, DIFF_HEADS, 2, DIFF_DD), dk_g)
    vd = v_d.reshape(B, T, DIFF_HEADS, DIFF_DV)
    new_diff = jnp.stack([kd.reshape(B, T, DIFF_HEADS, 2 * DIFF_DD), vd], axis=2)
    diff_all = jnp.concatenate([past_diff, new_diff], axis=1)
    L = diff_all.shape[1]
    k_all = diff_all[:, :, 0].reshape(B, L, DIFF_HEADS, 2, DIFF_DD)
    o_b = diff_mixer(qd[:, :, :, 0], qd[:, :, :, 1], k_all[:, :, :, 0], k_all[:, :, :, 1],
                     diff_all[:, :, 1], lam, lam_init, subln_g, tab[:, NSA_HEADS:])
    o = jax.nn.sigmoid(ga) * o_a + jax.nn.sigmoid(gb) * o_b
    h = x + jnp.einsum('bte,ed->btd', o, w_o)
    hn = rmsnorm(h, mlp_g)
    y = h + jnp.einsum('btf,fd->btd', jnp.square(jax.nn.relu(jnp.einsum('btd,df->btf', hn, w_up))), w_down)
    return y, new_nsa, new_diff, win_all[:, win_all.shape[1] - win_keep:]

def setup_inputs(seed: int = 0) -> dict:
    key = jax.random.key(seed)
    ks = jax.random.split(key, 32)
    n_pages = PAST_LEN // PAGE_SIZE
    in_use = DEC_BATCH * n_pages
    n_phys = in_use + max(1, in_use // 4)
    win_buf = min(WINDOW, PAST_LEN)
    f32 = jnp.float32

    def nrm(k, shape, s):
        return jax.random.normal(k, shape, f32) * s

    def gain(k, shape):
        return 1.0 + 0.05 * jax.random.normal(k, shape, f32)

    page_table = jax.random.permutation(ks[3], n_phys)[:in_use].reshape(DEC_BATCH, n_pages).astype(jnp.int32)
    return {
        'x_prompt': nrm(ks[0], (BATCH, SEQ, D_MODEL), 1.0),
        'x_sample': nrm(ks[1], (DEC_BATCH, DEC_SEQ, D_MODEL), 1.0),
        'cache_nsa_kv': nrm(ks[2], (DEPTH, n_phys, PAGE_SIZE, N_KV_SLOTS, NSA_GROUPS, NSA_DK), 1.0),
        'cache_diff_kv': nrm(ks[4], (DEPTH, n_phys, PAGE_SIZE, 2, DIFF_HEADS, DIFF_DV), 1.0),
        'cache_nsa_win': nrm(ks[5], (DEPTH, DEC_BATCH, win_buf, 2, NSA_GROUPS, NSA_DK), 1.0),
        'page_table': page_table,
        'rel_bias_table': nrm(ks[6], (NUM_BUCKETS, NSA_HEADS + DIFF_HEADS), 0.2),
        'attn_norm': gain(ks[7], (DEPTH, D_MODEL)),
        'w_in': nrm(ks[8], (DEPTH, D_MODEL, N_IN), D_MODEL ** -0.5),
        'nsa_q_gain': gain(ks[9], (DEPTH, NSA_DK)),
        'nsa_k_gain': gain(ks[10], (DEPTH, NSA_DK)),
        'cmp_pe_k': nrm(ks[11], (DEPTH, CMP_BLOCK, NSA_DK), 0.1),
        'cmp_w1_k': nrm(ks[12], (DEPTH, CMP_BLOCK * NSA_DK, CMP_HID), (CMP_BLOCK * NSA_DK) ** -0.5),
        'cmp_w2_k': nrm(ks[13], (DEPTH, CMP_HID, NSA_DK), CMP_HID ** -0.5),
        'cmp_pe_v': nrm(ks[14], (DEPTH, CMP_BLOCK, NSA_DK), 0.1),
        'cmp_w1_v': nrm(ks[15], (DEPTH, CMP_BLOCK * NSA_DK, CMP_HID), (CMP_BLOCK * NSA_DK) ** -0.5),
        'cmp_w2_v': nrm(ks[16], (DEPTH, CMP_HID, NSA_DK), CMP_HID ** -0.5),
        'diff_q_gain': gain(ks[17], (DEPTH, DIFF_DD)),
        'diff_k_gain': gain(ks[18], (DEPTH, DIFF_DD)),
        'lambda_q1': nrm(ks[19], (DEPTH, DIFF_DD), 0.1),
        'lambda_k1': nrm(ks[20], (DEPTH, DIFF_DD), 0.1),
        'lambda_q2': nrm(ks[21], (DEPTH, DIFF_DD), 0.1),
        'lambda_k2': nrm(ks[22], (DEPTH, DIFF_DD), 0.1),
        'diff_subln': gain(ks[23], (DEPTH, DIFF_DV)),
        'w_o': nrm(ks[24], (DEPTH, D_MODEL, D_MODEL), D_MODEL ** -0.5),
        'mlp_norm': gain(ks[25], (DEPTH, D_MODEL)),
        'w_up': nrm(ks[26], (DEPTH, D_MODEL, D_FF), D_MODEL ** -0.5),
        'w_down': nrm(ks[27], (DEPTH, D_FF, D_MODEL), D_FF ** -0.5),
    }

def reference(x_prompt, x_sample, cache_nsa_kv, cache_diff_kv, cache_nsa_win, page_table,
              rel_bias_table, attn_norm, w_in, nsa_q_gain, nsa_k_gain,
              cmp_pe_k, cmp_w1_k, cmp_w2_k, cmp_pe_v, cmp_w1_v, cmp_w2_v,
              diff_q_gain, diff_k_gain, lambda_q1, lambda_k1, lambda_q2, lambda_k2, diff_subln,
              w_o, mlp_norm, w_up, w_down):
    B, T = x_prompt.shape[:2]
    DB = x_sample.shape[0]
    n_pages = page_table.shape[1]
    past_len = n_pages * cache_nsa_kv.shape[2]
    win_buf = cache_nsa_win.shape[2]
    yp, ys = x_prompt, x_sample
    nsa_p_l, diff_p_l, win_p_l, nsa_s_l, diff_s_l, win_s_l = [], [], [], [], [], []
    for l in range(DEPTH):
        lam_init = 0.8 - 0.6 * math.exp(-0.3 * l)
        lam = (jnp.exp(jnp.sum(lambda_q1[l].astype(jnp.float32) * lambda_k1[l].astype(jnp.float32)))
               - jnp.exp(jnp.sum(lambda_q2[l].astype(jnp.float32) * lambda_k2[l].astype(jnp.float32)))
               + lam_init)
        lw = (lam_init, lam, rel_bias_table, attn_norm[l], w_in[l], nsa_q_gain[l], nsa_k_gain[l],
              cmp_pe_k[l], cmp_w1_k[l], cmp_w2_k[l], cmp_pe_v[l], cmp_w1_v[l], cmp_w2_v[l],
              diff_q_gain[l], diff_k_gain[l], diff_subln[l], w_o[l], mlp_norm[l], w_up[l], w_down[l])
        p_nsa0 = jnp.zeros((B, 0, N_KV_SLOTS, NSA_GROUPS, NSA_DK), x_prompt.dtype)
        p_diff0 = jnp.zeros((B, 0, 2, DIFF_HEADS, DIFF_DV), x_prompt.dtype)
        p_win0 = jnp.zeros((B, WINDOW, 2, NSA_GROUPS, NSA_DK), x_prompt.dtype)
        yp, nsa_p, diff_p, win_p = decoder_layer(yp, p_nsa0, p_diff0, p_win0, min(WINDOW, T), *lw)
        s_nsa = cache_nsa_kv[l][page_table].reshape(DB, past_len, N_KV_SLOTS, NSA_GROUPS, NSA_DK)
        s_diff = cache_diff_kv[l][page_table].reshape(DB, past_len, 2, DIFF_HEADS, DIFF_DV)
        s_win = jnp.pad(cache_nsa_win[l], ((0, 0), (WINDOW - win_buf, 0), (0, 0), (0, 0), (0, 0)))
        ys, nsa_s, diff_s, win_s = decoder_layer(ys, s_nsa, s_diff, s_win, win_buf, *lw)
        nsa_p_l.append(nsa_p); diff_p_l.append(diff_p); win_p_l.append(win_p)
        nsa_s_l.append(nsa_s); diff_s_l.append(diff_s); win_s_l.append(win_s)
    return (yp, ys, jnp.stack(nsa_p_l, 0), jnp.stack(diff_p_l, 0), jnp.stack(win_p_l, 0),
            jnp.stack(nsa_s_l, 0), jnp.stack(diff_s_l, 0), jnp.stack(win_s_l, 0))


_drawn_inputs = setup_inputs


def setup_inputs(seed=0):
    import zlib

    import numpy as np

    out = dict(_drawn_inputs(seed))
    spreads = {}
    factors = {'nsa_q_gain': 8.0,
     'cmp_pe_k': 8.0,
     'cmp_pe_v': 3.515,
     'lambda_q1': 5.506,
     'lambda_k1': 8.0,
     'lambda_q2': 4.359,
     'lambda_k2': 7.469}
    for name, (base, spread) in spreads.items():
        noise = np.random.default_rng([zlib.crc32(name.encode()), seed]).standard_normal(out[name].shape)
        drawn = base * np.exp(spread * noise) if base else spread * noise
        out[name] = __import__('jax').numpy.asarray(drawn.astype(out[name].dtype))
    for name, factor in factors.items():
        out[name] = (out[name] * factor).astype(out[name].dtype)
    return out
```

```python
import math
from contextlib import ExitStack

import numpy as np
import concourse.bass as bass
from concourse import mybir
from concourse.alu_op_type import AluOpType as ALU

F32 = mybir.dt.float32
F32R = mybir.dt.float32r
I32 = mybir.dt.int32
ACT = mybir.ActivationFunctionType
AX = mybir.AxisListType

P = 128
D_MODEL = 1024
SEQ = 512
DEC_B, DEC_T = 8, 4
N_DEC = DEC_B * DEC_T
TOKENS = SEQ + N_DEC
PAST = 1024
PAGE = 128
N_PAGES = PAST // PAGE
HEADS, GROUPS, DK = 16, 4, 64
HPG = HEADS // GROUPS
KVW = GROUPS * DK
CMP_BLOCK, CMP_STRIDE, CMP_HID = 32, 16, 256
SEL_BLOCK = 64
N_SLC = -(-(PAST + DEC_T) // SEL_BLOCK)
WINDOW = 512
DHEADS, DD, DV = 8, 64, 128
D_FF = 4 * D_MODEL
BUCKETS, MAX_DIST = 32, 128
EPS = 1e-6
NEG = -1e30
TINY = 1e-30
SCALE = DK ** -0.5
N_IN = 7728

KT = D_MODEL // P
QT = SEQ // P
TT = QT + 1
CW = 512
BROW = 1556
BTOP = PAST + DEC_T - 1
STRIP = 912
DECW = 1040


class Chain:

    def __init__(self, eng, sem, base=0):
        self.eng, self.sem, self.base, self.n = eng, sem, base, 0

    def __call__(self, ins):
        self.n += 1
        ins.then_inc(self.sem, 1)
        self.eng.wait_ge(self.sem, self.base + self.n)


class Space:

    def __init__(self, nc, ctx, stage):
        self.nc, self.ctx, self.stage, self.sems = nc, ctx, stage, []
        ctx.callback(self.clear)

    def sb(self, name, shape, dt=F32):
        return self.ctx.enter_context(self.nc.sbuf_tensor(f"{self.stage}_{name}", shape, dt))

    def ps(self, name, shape):
        return self.ctx.enter_context(self.nc.psum_tensor(f"{self.stage}_{name}", shape, F32))

    def sem(self, name):
        self.sems.append(self.nc.alloc_semaphore(f"{self.stage}_{name}"))
        return self.sems[-1]

    def clear(self):
        self.nc.clear_and_free_semaphores(self.sems)
        self.nc.all_engine_barrier()


def spread(ap, n):
    return bass.AP(tensor=ap.tensor, offset=ap.offset, ap=[[0, n]] + [list(x) for x in ap.ap][-1:])


Q_N, KV_N, G_N = 0, 1024, 2560
Q_D, K_D, V_D, GA, GB = 2608, 3632, 4656, 5680, 6704
CHUNKS = (
    [(Q_N + CW * j, "query", "q", CW * j) for j in range(2)]
    + [(Q_D + CW * j, "query", "qd", CW * j) for j in range(2)]
    + [(K_D + CW * j, "key", "diff", CW * j) for j in range(2)]
    + [(KV_N + 2 * CW, "key_value", "win", 0), (KV_N + CW, "key_value", "nsa", CW), (KV_N, "plain", "nsa", 0)]
    + [(V_D + CW * j, "plain", "diff", 1024 + CW * j) for j in range(2)]
    + [(GA + CW * j, "gate", "ga", CW * j) for j in range(2)]
    + [(GB + CW * j, "gate", "gb", CW * j) for j in range(2)]
)
NC = len(CHUNKS)


def project(nc, d):
    with ExitStack() as ctx:
        s = Space(nc, ctx, "pj")
        x = s.sb("x", [P, TT, D_MODEL])
        xh = s.sb("xh", [P, KT, SEQ], F32R)
        xl = s.sb("xl", [P, KT, SEQ], F32R)
        xf = s.sb("xf", [P, 2, CW])
        xsam = s.sb("xsam", [P, KT, N_DEC])
        ident = s.sb("ident", [P, P])
        gain = s.sb("gain", [P, KT])
        ssum = s.sb("ssum", [P, TT])
        rstd = s.sb("rstd", [P, TT])
        w = s.sb("w", [P, 2, KT, CW])
        wh = s.sb("wh", [P, 2, KT, CW], F32R)
        wl = s.sb("wl", [P, 2, KT, CW], F32R)
        wg = s.sb("wg", [P, KT, 48])
        wgh = s.sb("wgh", [P, KT, 48], F32R)
        wgl = s.sb("wgl", [P, KT, 48], F32R)
        heads_gain = s.sb("heads_gain", [P, 4, DK])
        sq = s.sb("sq", [P, 2, CW])
        stat = s.sb("stat", [P, 2, 3, 8])
        y = s.sb("y", [P, 3, CW])
        tab = s.sb("tab", [BUCKETS + 1, 24])
        hot = s.sb("hot", [BUCKETS + 1, BROW])
        brow = s.sb("brow", [24, BROW])
        ps = s.ps("ps", [P, TT, CW])
        pt = s.ps("pt", [P, 2, CW])

        ssum_set = s.sem("ssum_set")
        x_in, gains_in, table_in = s.sem("x_in"), s.sem("gains_in"), s.sem("table_in")
        x_sq, x_rstd, x_scaled = s.sem("x_sq"), s.sem("x_rstd"), s.sem("x_scaled")
        x_turned, x_copied, x_hi, x_ready = s.sem("x_turned"), s.sem("x_copied"), s.sem("x_hi"), s.sem("x_ready")
        mask_row, bias_mm, bias_row, bias_out = s.sem("mask_row"), s.sem("bias_mm"), s.sem("bias_row"), s.sem("bias_out")
        w_in = [s.sem(f"w_in{u}") for u in range(2)]
        wg_in = s.sem("wg_in")
        w_hi, w_split = s.sem("w_hi"), s.sem("w_split")
        tile_done = s.sem("tile_done")
        bank_free = [s.sem(f"bank_free{t}") for t in range(TT)]
        squared, summed, rooted = s.sem("squared"), s.sem("summed"), s.sem("rooted")
        y_ready = s.sem("y_ready")
        stored = [s.sem(f"stored{k}") for k in range(3)]
        dve_step, act_step = s.sem("dve_step"), s.sem("act_step")
        block = ctx.enter_context(nc.Block())

        rows = lambda t: P if t < QT else N_DEC
        units = [(c, t) for c in range(NC + 1) for t in range(TT)]

        def dests(c, t):
            name, at = (CHUNKS[c][2], CHUNKS[c][3]) if c < NC else ("g", 0)
            k = (c * TT + t) % 3
            if c == NC:
                n = rows(t)
                return [(d["g"][t * P:t * P + n, :], y[0:n, k, 0:48])]
            if t < QT:
                out = d[name if name in ("q", "qd", "ga", "gb") else name + "_p"]
                return [(out[t * P:(t + 1) * P, at:at + CW], y[:, k, :])]
            if name == "win":
                return [(d["win_s"][:, WINDOW - DEC_T:WINDOW, P * j:P * (j + 1)], y[32 * j:32 * j + 32, k, 0:P])
                        for j in range(4)]
            out = d[name][SEQ:TOKENS, :] if name in ("q", "qd", "ga", "gb") else d[name + "_s"]
            return [(out[:, at + P * j:at + P * (j + 1)], y[32 * j:32 * j + 32, k, 0:P]) for j in range(4)]

        stores = [0] * 3
        store_level = []
        for n, (c, t) in enumerate(units):
            stores[n % 3] += 16 * len(dests(c, t))
            store_level.append(stores[n % 3])

        @block.sync
        def _(sp):
            for t in range(TT):
                src = d["x_prompt"][t * P:(t + 1) * P, :] if t < QT else d["x_sample"]
                sp.dma_start(x[0:rows(t), t, :], src).then_inc(x_in, 16)
            sp.dma_start(ident[:], d["ident"]).then_inc(gains_in, 16)
            with nc.allow_non_contiguous_dma("a column of gains"):
                sp.dma_start(gain[:], d["attn_norm"].rearrange("(k p) -> p k", p=P)).then_inc(gains_in, 16)
            for j, name in enumerate(("nsa_q_gain", "diff_q_gain", "diff_k_gain", "nsa_k_gain")):
                sp.dma_start(heads_gain[:, j, :], spread(d[name], P)).then_inc(gains_in, 16)
            sp.dma_start(tab[0:BUCKETS, :], d["rel_bias_table"]).then_inc(table_in, 16)
            sp.dma_start(hot[:], d["bucket_hot"]).then_inc(table_in, 16)
            w_view = d["w_in"].rearrange("(k p) n -> p k n", p=P)
            for c in range(2):
                sp.dma_start(w[:, c, :, :], w_view[:, :, CHUNKS[c][0]:CHUNKS[c][0] + CW]).then_inc(w_in[c], 16)
            sp.dma_start(wg[:], w_view[:, :, G_N:G_N + 48]).then_inc(wg_in, 16)
            sp.wait_ge(bias_row, 4)
            for h in range(24):
                sp.dma_start(d["toep"][h:h + 1, :, :],
                             bass.AP(tensor=brow, offset=h * BROW + BTOP - 384, ap=[[BROW, 1], [-1, P], [1, STRIP]])
                             ).then_inc(bias_out, 16)
            sp.dma_start(d["decb"], bass.AP(tensor=brow, offset=DEC_T - 1, ap=[[BROW, 24], [-1, DEC_T], [1, DECW]])
                         ).then_inc(bias_out, 16)
            n_normed = 0
            for n, (c, t) in enumerate(units):
                if t == QT and c + 2 < NC:
                    sp.wait_ge(tile_done, TT * (c + 1))
                    at = CHUNKS[c + 2][0]
                    sp.dma_start(w[:, c % 2, :, :], w_view[:, :, at:at + CW]).then_inc(w_in[c % 2], 16)
                if c < NC and CHUNKS[c][1] in ("query", "key", "key_value"):
                    n_normed += 1
                    sp.wait_ge(y_ready, n_normed)
                else:
                    sp.wait_ge(bank_free[t], c + 2)
                for dst, src in dests(c, t):
                    sp.dma_start(dst, src).then_inc(stored[n % 3], 16)
            sp.wait_ge(bias_out, 16 * 25)
            for k in range(3):
                sp.wait_ge(stored[k], stores[k])

        def x_tile(sc, t):
            return x[0:rows(t), t, :]

        @block.scalar
        def _(act):
            act.wait_ge(x_in, 16 * TT)
            act.wait_ge(ssum_set, 1)
            for t in range(TT):
                if t:
                    act.wait_ge(x_sq, t)
                nc.scalar.activation(xf[0:rows(t), :, :].rearrange("p a b -> p (a b)"), x[0:rows(t), t, :], ACT.Square,
                                     accum_out=ssum[0:rows(t), t:t + 1]).then_inc(x_sq, 1)
            act.wait_ge(x_rstd, 1)
            nc.scalar.activation(rstd[:], ssum[:], ACT.Sqrt).then_inc(x_sq, 1)
            act.wait_ge(x_rstd, 2)
            for t in range(TT):
                nc.scalar.activation(x[0:rows(t), t, :], x[0:rows(t), t, :], ACT.Copy,
                                     scale=rstd[0:rows(t), t:t + 1]).then_inc(x_scaled, 1)
            for k in range(KT):
                act.wait_ge(x_copied, k + 1)
                nc.scalar.activation(xh[:, k, :], xf[:, k % 2, :], ACT.Copy).then_inc(x_hi, 1)

            def split(c):
                act.wait_ge(w_in[c % 2], 16 * (c // 2 + 1))
                if c >= 2:
                    act.wait_ge(tile_done, TT * (c - 1))
                nc.scalar.activation(wh[:, c % 2, :, :], w[:, c % 2, :, :], ACT.Copy).then_inc(w_hi, 1)

            split(0)
            split(1)
            act.wait_ge(wg_in, 16)
            nc.scalar.activation(wgh[:], wg[:], ACT.Copy).then_inc(w_hi, 1)
            n_sq = 0
            for n, (c, t) in enumerate(units):
                kind = CHUNKS[c][1] if c < NC else "gate"
                cols = 48 if c == NC else (CW if t < QT else P)
                rws = rows(t) if c == NC else P
                if kind in ("query", "key", "key_value"):
                    a, b = (rws, cols) if kind != "key_value" else ((P, KVW) if t < QT else (64, P))
                    act.wait_ge(tile_done, n + 1)
                    if n_sq >= 2:
                        act.wait_ge(summed, 2 * (n_sq - 1))
                    nc.scalar.activation(sq[0:a, n_sq % 2, 0:b], ps[0:a, t, 0:b], ACT.Square).then_inc(squared, 1)
                    act.wait_ge(summed, 2 * n_sq + 2)
                    nc.scalar.activation(stat[0:a, n_sq % 2, 1, 0:b // DK], stat[0:a, n_sq % 2, 0, 0:b // DK],
                                         ACT.Sqrt).then_inc(rooted, 1)
                    n_sq += 1
                if kind == "gate":
                    act.wait_ge(tile_done, n + 1)
                    if n >= 3:
                        act.wait_ge(stored[n % 3], store_level[n - 3])
                    nc.scalar.activation(y[0:rws, n % 3, 0:cols], ps[0:rws, t, 0:cols],
                                         ACT.Sigmoid).then_inc(bank_free[t], 1)
                if t == TT - 1 and c + 2 < NC:
                    split(c + 2)

        @block.vector
        def _(dve):
            step = Chain(dve, dve_step)
            for t in range(TT):
                nc.vector.nop().then_inc(bank_free[t], 1)
            nc.vector.memset(ssum[:], 1.0).then_inc(ssum_set, 1)
            nc.vector.memset(tab[BUCKETS:BUCKETS + 1, :], NEG).then_inc(mask_row, 1)
            dve.wait_ge(x_sq, TT)
            nc.vector.tensor_scalar(ssum[:], ssum[:], 1.0 / D_MODEL, EPS, ALU.mult, ALU.add).then_inc(x_rstd, 1)
            dve.wait_ge(x_sq, TT + 1)
            nc.vector.reciprocal(rstd[:], rstd[:]).then_inc(x_rstd, 1)
            dve.wait_ge(gains_in, 16 * 6)
            for k in range(KT):
                dve.wait_ge(x_turned, k + 1)
                if k >= 2:
                    dve.wait_ge(x_ready, k - 1)
                nc.vector.tensor_scalar(xf[:, k % 2, :], pt[:, k % 2, :], gain[:, k:k + 1], None,
                                        ALU.mult).then_inc(x_copied, 1)
                dve.wait_ge(x_hi, k + 1)
                nc.vector.tensor_tensor(xl[:, k, :], xf[:, k % 2, :], xh[:, k, :].bitcast(F32),
                                        ALU.subtract).then_inc(x_ready, 1)
            dve.wait_ge(x_turned, KT + 1)
            for k in range(KT):
                ins = nc.vector.tensor_scalar(xsam[:, k, :], pt[:, 0, N_DEC * k:N_DEC * (k + 1)], gain[:, k:k + 1], None,
                                              ALU.mult)
            ins.then_inc(x_ready, 1)
            for j in range(4):
                dve.wait_ge(bias_mm, j + 1)
                nc.vector.tensor_copy(brow[:, 389 * j:389 * (j + 1)], ps[0:24, j, 0:389]).then_inc(bias_row, 1)
            for j in range(2):
                step(nc.vector.tensor_scalar(heads_gain[:, j, :], heads_gain[:, j, :], SCALE, None, ALU.mult))

            def split(c):
                dve.wait_ge(w_hi, c + 1 + (c >= 2))
                nc.vector.tensor_tensor(wl[:, c % 2, :, :], w[:, c % 2, :, :], wh[:, c % 2, :, :].bitcast(F32),
                                        ALU.subtract).then_inc(w_split, 1)

            split(0)
            split(1)
            dve.wait_ge(w_hi, 3)
            nc.vector.tensor_tensor(wgl[:], wg[:], wgh[:].bitcast(F32), ALU.subtract).then_inc(w_split, 1)
            n_sq = 0
            for n, (c, t) in enumerate(units):
                kind = CHUNKS[c][1] if c < NC else "gate"
                cols = CW if t < QT else P
                k = n % 3
                if kind != "gate":
                    dve.wait_ge(tile_done, n + 1)
                    if n >= 3:
                        dve.wait_ge(stored[k], store_level[n - 3])
                if kind in ("query", "key", "key_value"):
                    a, b = (P, cols) if kind != "key_value" else ((P, KVW) if t < QT else (64, P))
                    g = b // DK
                    m = n_sq % 2
                    dve.wait_ge(squared, n_sq + 1)
                    nc.vector.tensor_reduce(stat[0:a, m, 0, 0:g], sq[0:a, m, 0:b].rearrange("p (g e) -> p g e", e=DK),
                                            AX.X, ALU.add).then_inc(summed, 1)
                    dve.wait_ge(summed, 2 * n_sq + 1)
                    nc.vector.tensor_scalar(stat[0:a, m, 0, 0:g], stat[0:a, m, 0, 0:g], 1.0 / DK, EPS,
                                            ALU.mult, ALU.add).then_inc(summed, 1)
                    if kind == "key_value":
                        raw = (slice(0, P), slice(KVW, CW)) if t < QT else (slice(64, P), slice(0, P))
                        nc.vector.tensor_copy(y[raw[0], k, raw[1]], ps[raw[0], t, raw[1]]).then_inc(dve_step, 1)
                        step.n += 1
                    dve.wait_ge(rooted, n_sq + 1)
                    step(nc.vector.reciprocal(stat[0:a, m, 2, 0:g], stat[0:a, m, 1, 0:g]))
                    row = {"q": 0, "qd": 1, "diff": 2, "nsa": 3, "win": 3}[CHUNKS[c][2]]
                    yv = y[0:a, k, 0:b].rearrange("p (g e) -> p g e", e=DK)
                    nc.vector.tensor_tensor(yv, ps[0:a, t, 0:b].rearrange("p (g e) -> p g e", e=DK),
                                                   stat[0:a, m, 2, 0:g].unsqueeze(2).to_broadcast([a, g, DK]),
                                            ALU.mult).then_inc(bank_free[t], 1)
                    dve.wait_ge(bank_free[t], c + 2)
                    nc.vector.tensor_tensor(yv, yv, heads_gain[0:a, row:row + 1, :].to_broadcast([a, g, DK]),
                                            ALU.mult).then_inc(y_ready, 1)
                    n_sq += 1
                elif kind == "plain":
                    nc.vector.tensor_copy(y[:, k, 0:cols], ps[:, t, 0:cols]).then_inc(bank_free[t], 1)
                if t == TT - 1 and c + 2 < NC:
                    split(c + 2)

        @block.tensor
        def _(pe):
            pe.wait_ge(gains_in, 16 * 6)
            pe.wait_ge(x_scaled, TT)
            for k in range(KT):
                if k >= 2:
                    pe.wait_ge(x_copied, k - 1)
                for t in range(QT):
                    ins = pe.transpose(pt[:, k % 2, P * t:P * (t + 1)], x[:, t, P * k:P * (k + 1)], ident[:])
                ins.then_inc(x_turned, 1)
            pe.wait_ge(x_copied, KT)
            for k in range(KT):
                ins = pe.transpose(pt[:, 0, N_DEC * k:N_DEC * (k + 1)], x[0:N_DEC, QT, P * k:P * (k + 1)],
                                   ident[0:N_DEC, 0:N_DEC])
            ins.then_inc(x_turned, 1)
            pe.wait_ge(table_in, 32)
            pe.wait_ge(mask_row, 1)
            for j in range(4):
                pe.matmul(ps[0:24, j, 0:389], tab[:], hot[:, 389 * j:389 * (j + 1)], start=True, stop=True).then_inc(bias_mm, 1)
            pe.wait_ge(bias_row, 4)
            pe.wait_ge(x_ready, KT + 1)

            def chunk(u, c, width, hi, lo, raw):
                for t in range(QT):
                    pe.wait_ge(bank_free[t], c + 1)
                    for k in range(KT):
                        xk = slice(P * t, P * (t + 1))
                        pe.matmul(ps[:, t, 0:width], xh[:, k, xk], hi(k), start=k == 0, stop=False)
                        pe.matmul(ps[:, t, 0:width], xh[:, k, xk], lo(k), start=False, stop=False)
                        ins = pe.matmul(ps[:, t, 0:width], xl[:, k, xk], hi(k), start=False, stop=k == KT - 1)
                    ins.then_inc(tile_done, 1)
                pe.wait_ge(bank_free[QT], c + 1)
                for k in range(KT):
                    for j in range(4 if width == CW else 1):
                        n = P if width == CW else width
                        ins = pe.matmul(ps[32 * j:32 * j + 32, QT, 0:n], xsam[:, k, :], raw(k)[:, n * j:n * (j + 1)],
                                        start=k == 0, stop=k == KT - 1)
                ins.then_inc(tile_done, 1)

            def full(u, c):
                chunk(u, c, CW, lambda k: wh[:, u, k, :], lambda k: wl[:, u, k, :], lambda k: w[:, u, k, :])


            pe.wait_ge(w_split, 3)
            with pe.Fori(0, NC // 2) as i:
                for u in range(2):
                    pe.wait_ge(w_split, 2 * i + u + 2)
                    full(u, 2 * i + u)
            pe.wait_ge(w_split, NC + 1)
            full(0, NC - 1)
            chunk(0, NC, 48, lambda k: wgh[:, k, :], lambda k: wgl[:, k, :], lambda k: wg[:, k, :])


def bucket_of(dist):
    exact = BUCKETS // 2
    if dist < exact:
        return dist
    return min(exact + int(math.log(dist / exact) / math.log(MAX_DIST / exact) * (BUCKETS - exact)), BUCKETS - 1)


def bucket_hot():
    hot = np.zeros((BUCKETS + 1, BROW), np.float32)
    for i in range(BROW):
        dist = BTOP - i
        hot[BUCKETS if dist < 0 else bucket_of(dist), i] = 1.0
    return hot


CH = 64
CHP = SEQ // CMP_STRIDE
JP = CMP_STRIDE // 2
CHUNKS_PER_PAGE = PAGE // CMP_STRIDE
XW = GROUPS * P + 2


def compress(nc, d):
    with ExitStack() as ctx:
        s = Space(nc, ctx, "cm")
        raw = s.sb("raw", [P, 2, CMP_STRIDE, 2 * KVW])
        laid = s.sb("laid", [P, 2, GROUPS, CMP_STRIDE * DK])
        xh = s.sb("xh", [P, JP, XW], F32R)
        xl = s.sb("xl", [P, JP, XW], F32R)
        w1h = s.sb("w1h", [P, 2, 2 * JP, CMP_HID], F32R)
        w1l = s.sb("w1l", [P, 2, 2 * JP, CMP_HID], F32R)
        w2 = s.sb("w2", [P, 2, 2, DK])
        pe_t = s.sb("pe_t", [P, 2, 2 * JP])
        pe_h = s.sb("pe_h", [P, 4])
        hid = s.sb("hid", [P, 2, 2, CW])
        ident = s.sb("ident", [P, P])
        gain = s.sb("gain", [P, DK])
        table = s.sb("table", [1, DEC_B * N_PAGES], I32)
        sq = s.sb("sq", [P, KVW])
        stat = s.sb("stat", [P, 3, GROUPS])
        out = s.sb("out", [P, 2, KVW])
        pt = s.ps("pt", [P, 4, CW])
        ph = s.ps("ph", [P, 2, CW])
        pc = s.ps("pc", [P, 2, CW])

        consts_in, table_in = s.sem("consts_in"), s.sem("table_in")
        w1_in = [s.sem(f"w1_in{k}") for k in range(2)]
        w1_hi, w1_lo, pe_mm, pe_ready, pads = (s.sem(n) for n in ("w1_hi", "w1_lo", "pe_mm", "pe_ready", "pads"))
        raw_in = [s.sem(f"raw_in{u}") for u in range(2)]
        laid_out = s.sem("laid_out")
        turned, x_hi, x_lo = s.sem("turned"), s.sem("x_hi"), s.sem("x_lo")
        hid_mm, hid_ready, row_mm = s.sem("hid_mm"), s.sem("hid_ready"), s.sem("row_mm")
        squared, summed, rooted, step_sem, out_ready = (
            s.sem(n) for n in ("squared", "summed", "rooted", "dve_step", "out_ready"))
        stored = [s.sem(f"stored{k}") for k in range(2)]
        block = ctx.enter_context(nc.Block())

        T_UNIT = 2 * GROUPS
        N_UNITS = DEC_B
        w1 = [d[f"cmp_w1_{x}"].rearrange("(k p) n -> p k n", p=P) for x in "kv"]
        raw_w1 = [raw[:, k, :, :].rearrange("p j c -> p (j c)")[:, 0:2 * JP * CMP_HID]
                  .rearrange("p (k n) -> p k n", n=CMP_HID) for k in range(2)]
        nsa_chunks = d["cache_nsa"].rearrange("n (c j) e -> n c j e", j=CMP_STRIDE)
        nsa_p_chunks = d["nsa_p"].rearrange("(c j) e -> c j e", j=CMP_STRIDE)

        @block.sync
        def _(sp):
            sp.dma_start(table[:], d["page_table"]).then_inc(table_in, 16)
            for k in range(2):
                sp.dma_start(raw_w1[k], w1[k]).then_inc(w1_in[k], 16)
            sp.dma_start(ident[:], d["ident"]).then_inc(consts_in, 16)
            sp.dma_start(gain[:], spread(d["nsa_k_gain"], P)).then_inc(consts_in, 16)
            for k, x in enumerate("kv"):
                sp.dma_start(w2[:, k, :, :], d[f"cmp_w2_{x}"].rearrange("(h p) n -> p h n", p=P)).then_inc(consts_in, 16)
                with nc.allow_non_contiguous_dma("the position embedding, by contraction row"):
                    sp.dma_start(pe_t[:, k, :], d[f"cmp_pe_{x}"].rearrange("l e -> (l e)").rearrange("(k p) -> p k", p=P)
                                 ).then_inc(consts_in, 16)
            sp.wait_ge(table_in, 16)
            sp.wait_ge(w1_lo, 2)
            sp.wait_ge(pe_mm, 1)

            def store(n, k, kn):
                sp.wait_ge(out_ready, n + 3)
                sp.dma_start(d["kc_s" if k == 0 else "vc_s"][bass.ds(kn * P, P), :], out[:, k, :]).then_inc(stored[k], 16)

            def load(pair, u):
                if pair >= 2:
                    sp.wait_ge(laid_out, 2 * (pair - 1))
                for b in range(2):
                    for pg in range(N_PAGES):
                        page = sp.value_load(table[0:1, bass.ds((2 * pair + b) * N_PAGES + pg, 1)],
                                             min_val=0, max_val=d["cache_nsa"].shape[0] - 1)
                        at = CH * b + CHUNKS_PER_PAGE * pg
                        sp.dma_start(raw[at:at + CHUNKS_PER_PAGE, u, :, :],
                                     nsa_chunks[bass.ds(page, 1), :, :, 0:2 * KVW].rearrange("n c j e -> (n c) j e")).then_inc(raw_in[u], 16)

            load(0, 0)
            load(1, 1)
            for pair in range(DEC_B // 2):
                for k in range(2):
                    store(2 * pair + k, k, pair)
                if pair + 2 < DEC_B // 2:
                    load(pair + 2, pair % 2)
                elif pair + 2 == DEC_B // 2:
                    sp.wait_ge(laid_out, 2 * (pair + 1))
                    sp.dma_start(raw[0:CHP, 0, :, :], nsa_p_chunks[:, :, 0:2 * KVW]).then_inc(raw_in[0], 16)
            for k, name in enumerate(("kc_p", "vc_p")):
                sp.wait_ge(out_ready, N_UNITS + k + 3)
                sp.dma_start(d[name], out[0:CHP, k, :]).then_inc(stored[k], 16)
            for k in range(2):
                sp.wait_ge(stored[k], 16 * (DEC_B // 2 + 2))

        FILL = 16 * 2 * N_PAGES
        PROMPT = [(N_UNITS + k, 0, k, CHP) for k in range(2)]

        def loop_units(i):
            return [(4 * i + 2 * u + k, u, k, P) for u in range(2) for k in range(2)]

        @block.scalar
        def _(act):
            for k in range(2):
                act.wait_ge(w1_in[k], 16)
                nc.scalar.activation(w1h[:, k, :, :], raw_w1[k], ACT.Copy).then_inc(w1_hi, 1)
            act.wait_ge(pe_ready, 1)
            act.wait_ge(pads, 2)

            def high_parts(n, r, jh):
                for g in range(GROUPS):
                    m = GROUPS * jh + g
                    act.wait_ge(turned, T_UNIT * n + m + 1)
                    if m == 0:
                        act.wait_ge(hid_mm, 2 * n + 1)
                    nc.scalar.activation(xh[:, 4 * jh:4 * jh + 4, r * g:r * (g + 1)],
                                         pt[:, m % 4, 0:4 * r].rearrange("p (j c) -> p j c", j=4), ACT.Copy).then_inc(x_hi, 1)

            def gelu(n, k, r):
                for ht in range(2):
                    act.wait_ge(hid_mm, 2 * n + ht + 2)
                    nc.scalar.activation(hid[:, k, ht, 0:4 * r], ph[:, ht, 0:4 * r], ACT.Gelu_apprx_tanh,
                                         bias=pe_h[:, 2 * k + ht:2 * k + ht + 1]).then_inc(hid_ready, 1)

            def norm(n, kn, r):
                act.wait_ge(row_mm, n + 1)
                nc.scalar.activation(sq[0:r, :], pc[0:r, 0, 0:KVW], ACT.Square).then_inc(squared, 1)
                act.wait_ge(summed, 2 * kn + 2)
                nc.scalar.activation(stat[0:r, 1, :], stat[0:r, 0, :], ACT.Sqrt).then_inc(rooted, 1)

            def run(units, key_no):
                for n, u, k, r in units:
                    high_parts(n, r, 0)
                    if k == 1:
                        norm(n - 1, key_no(u), r)
                    high_parts(n, r, 1)
                    gelu(n, k, r)

            with act.Fori(0, 2) as i:
                run(loop_units(i), lambda u: 2 * i + u)
            run(PROMPT, lambda u: DEC_B // 2)

        @block.vector
        def _(dve):
            nc.vector.nop().then_inc(x_lo, 1)
            for k in range(2):
                nc.vector.nop().then_inc(out_ready, 1)
                nc.vector.nop().then_inc(stored[k], 16)
            nc.vector.memset(xh[:, :, GROUPS * P:XW].bitcast(F32), 0.0).then_inc(pads, 1)
            nc.vector.memset(xl[:, :, GROUPS * P:XW].bitcast(F32), 0.0).then_inc(pads, 1)
            for k in range(2):
                dve.wait_ge(w1_hi, k + 1)
                nc.vector.tensor_tensor(w1l[:, k, :, :], raw_w1[k], w1h[:, k, :, :].bitcast(F32),
                                        ALU.subtract).then_inc(w1_lo, 1)
            dve.wait_ge(pe_mm, 1)
            nc.vector.tensor_copy(pe_h[:], pc[:, 0, 0:4]).then_inc(pe_ready, 1)

            def lay_out(n, u, k, r, level):
                if k == 0:
                    dve.wait_ge(raw_in[u], level)
                nc.vector.tensor_copy(laid[0:r, k, :, :].rearrange("p g (j e) -> p g j e", e=DK),
                                      raw[0:r, u, :, KVW * k:KVW * (k + 1)].rearrange("p j (g e) -> p g j e", e=DK)
                                      ).then_inc(laid_out, 1)

            def low_parts(n, r, jh):
                for g in range(GROUPS):
                    m = GROUPS * jh + g
                    dve.wait_ge(x_hi, T_UNIT * n + m + 1)
                    view = (slice(None), slice(4 * jh, 4 * jh + 4), slice(r * g, r * (g + 1)))
                    nc.vector.tensor_tensor(xl[view], pt[:, m % 4, 0:4 * r].rearrange("p (j c) -> p j c", j=4),
                                            xh[view].bitcast(F32), ALU.subtract).then_inc(x_lo, 1)

            def rows(n, k, kn, r, step):
                dve.wait_ge(row_mm, n + 1)
                dve.wait_ge(stored[k], 16 * kn + 16)
                if k == 1:
                    nc.vector.tensor_copy(out[0:r, 1, :], pc[0:r, 1, 0:KVW]).then_inc(out_ready, 1)
                    return
                dve.wait_ge(squared, kn + 1)
                nc.vector.tensor_reduce(stat[0:r, 0, :], sq[0:r, :].rearrange("p (g e) -> p g e", e=DK),
                                        AX.X, ALU.add).then_inc(summed, 1)
                dve.wait_ge(summed, 2 * kn + 1)
                nc.vector.tensor_scalar(stat[0:r, 0, :], stat[0:r, 0, :], 1.0 / DK, EPS, ALU.mult, ALU.add).then_inc(summed, 1)
                dve.wait_ge(rooted, kn + 1)
                step(nc.vector.reciprocal(stat[0:r, 2, :], stat[0:r, 1, :]))
                view = out[0:r, 0, :].rearrange("p (g e) -> p g e", e=DK)
                step(nc.vector.tensor_tensor(view, pc[0:r, 0, 0:KVW].rearrange("p (g e) -> p g e", e=DK),
                                             stat[0:r, 2, :].unsqueeze(2).to_broadcast([r, GROUPS, DK]), ALU.mult))
                nc.vector.tensor_tensor(view, view, gain[0:r, :].unsqueeze(1).to_broadcast([r, GROUPS, DK]),
                                        ALU.mult).then_inc(out_ready, 1)

            def run(units, key_no, step, level):
                for j, (n, u, k, r) in enumerate(units):
                    lay_out(n, u, k, r, level)
                    low_parts(n, r, 0)
                    if j:
                        rows(n - 1, 1 - k, kn, r, step)
                    kn = key_no(u)
                    low_parts(n, r, 1)
                rows(n, k, kn, r, step)

            dve.wait_ge(consts_in, 16 * 6)
            with dve.Fori(0, 2) as i:
                run(loop_units(i), lambda u: 2 * i + u, Chain(dve, step_sem, 4 * i), FILL * i + FILL)
            run(PROMPT, lambda u: DEC_B // 2, Chain(dve, step_sem, 8), 2 * FILL + 16)

        @block.tensor
        def _(pe):
            pe.nop().then_inc(hid_mm, 1)
            pe.wait_ge(consts_in, 16 * 6)
            for k in range(2):
                pe.wait_ge(w1_in[k], 16)
                for ht in range(2):
                    for kt in range(2 * JP):
                        ins = pe.matmul(pc[:, 0, 2 * k + ht:2 * k + ht + 1], raw_w1[k][:, kt, P * ht:P * (ht + 1)],
                                        pe_t[:, k, kt:kt + 1], start=kt == 0, stop=kt == 2 * JP - 1)
            ins.then_inc(pe_mm, 1)
            pe.wait_ge(pe_ready, 1)
            pe.wait_ge(w1_lo, 2)

            def turn(n, u, k, r, jh):
                for g in range(GROUPS):
                    m = GROUPS * jh + g
                    if jh:
                        pe.wait_ge(x_lo, T_UNIT * n + m - 4 + 2)
                    for j in range(4):
                        jp = 4 * jh + j
                        ins = pe.transpose(pt[:, m % 4, r * j:r * (j + 1)],
                                           laid[0:r, k, g, P * jp:P * (jp + 1)],
                                           ident[0:r, 0:r])
                    ins.then_inc(turned, 1)

            def hidden(n, k, r):
                for ht in range(2):
                    col = slice(P * ht, P * (ht + 1))
                    for jp in range(JP):
                        if ht == 0 and jp % 4 == 0:
                            pe.wait_ge(x_lo, T_UNIT * n + GROUPS * (jp // 4 + 1) + 1)
                        for half in range(2):
                            mh, ml = xh[:, jp, half:half + 4 * r], xl[:, jp, half:half + 4 * r]
                            kt = JP * half + jp
                            o = ph[:, ht, 0:4 * r]
                            pe.matmul(o, w1h[:, k, kt, col], mh, start=jp == 0 and half == 0, stop=False)
                            pe.matmul(o, w1h[:, k, kt, col], ml, start=False, stop=False)
                            ins = pe.matmul(o, w1l[:, k, kt, col], mh, start=False, stop=jp == JP - 1 and half == 1)
                    ins.then_inc(hid_mm, 1)

            def second(n, k, r):
                pe.wait_ge(hid_ready, 2 * n + 2)
                pe.wait_ge(out_ready, n + 1)
                for g in range(GROUPS):
                    for ht in range(2):
                        ins = pe.matmul(pc[0:r, k, DK * g:DK * (g + 1)], hid[:, k, ht, r * g:r * (g + 1)], w2[:, k, ht, :],
                                        start=ht == 0, stop=ht == 1)
                ins.then_inc(row_mm, 1)

            def run(units):
                for j, (n, u, k, r) in enumerate(units):
                    if j == 0:
                        pe.wait_ge(x_lo, T_UNIT * n + 1)
                    pe.wait_ge(laid_out, n + 1)
                    turn(n, u, k, r, 0)
                    if j:
                        second(*prev)
                    turn(n, u, k, r, 1)
                    hidden(n, k, r)
                    prev = (n, k, r)
                second(*prev)

            with pe.Fori(0, 2) as i:
                run(loop_units(i))
            run(PROMPT)


CHP = SEQ // CMP_STRIDE
LAM_INIT = 0.8 - 0.6 * math.exp(-0.3 * 0)


def lambda_steps(nc, dve, act_exp_done, lam, lv, step, ready):
    for j in range(2):
        step(nc.vector.tensor_tensor(lv[:, j, :], lv[:, 2 * j, :] if j == 0 else lv[:, 2, :],
                                     lv[:, 1, :] if j == 0 else lv[:, 3, :], ALU.mult))
    nc.vector.tensor_reduce(lam[:, 1:3], lv[:, 0:2, :], AX.X, ALU.add).then_inc(ready, 1)
    dve.wait_ge(act_exp_done, 1)
    step(nc.vector.tensor_tensor(lam[:, 0:1], lam[:, 2:3], lam[:, 1:2], ALU.subtract))
    step(nc.vector.tensor_scalar(lam[:, 0:1], lam[:, 0:1], -LAM_INIT, None, ALU.add))


def prompt_attention(nc, d):
    with ExitStack() as ctx:
        s = Space(nc, ctx, "pa")
        q = s.sb("q", [P, 2, QT, HPG * DK])
        ks = s.sb("ks", [P, 2, QT, 2, DK])
        kw = s.sb("kw", [P, 2, QT, 2, DK])
        kc = s.sb("kc", [CHP, 2, 2, DK])
        vs = s.sb("vs", [P, 2, QT, DK])
        vw = s.sb("vw", [P, 2, QT, DK])
        vc = s.sb("vc", [CHP, 2, DK])
        strip = s.sb("strip", [P, 2, HPG, STRIP])
        gates = s.sb("gates", [P, 2, QT, HPG * 3])
        dq = s.sb("dq", [P, 2, QT, P])
        dk = s.sb("dk", [P, 2, QT, P])
        dv = s.sb("dv", [P, 2, QT, DV])
        dstrip = s.sb("dstrip", [P, 2, SEQ])
        q_t = s.sb("q_t", [P, 2, SEQ])
        ks_t = s.sb("ks_t", [P, SEQ])
        kw_t = s.sb("kw_t", [P, SEQ])
        kc_t = s.sb("kc_t", [P, CHP])
        sc = s.sb("sc", [P, 4, SEQ])
        p_t = s.sb("p_t", [P, 2, SEQ])
        nmax = s.sb("nmax", [P, 4])
        rsum = s.sb("rsum", [P, 4, 4])
        coef = s.sb("coef", [P, 2, 4])
        part = s.sb("part", [P, 2 * DV])
        oa = s.sb("oa", [P, 2, QT, HPG * DK])
        ob = s.sb("ob", [P, QT, DHEADS, DV])
        osq = s.sb("osq", [P, DHEADS, DV])
        ssum = s.sb("ssum", [P, QT * DHEADS])
        ident = s.sb("ident", [P, P])
        lam = s.sb("lam", [P, 4])
        lv = s.sb("lv", [P, 4, DD])
        gain = s.sb("gain", [P, DV])
        ps_s, ps_t, ps_o, ps_k = (s.ps(n, [P, 2, CW]) for n in ("ps_s", "ps_t", "ps_o", "ps_k"))

        consts_in, begun, begun_keys = s.sem("consts_in"), s.sem("begun"), s.sem("begun_keys")
        g_in = [s.sem(f"g_in{u}") for u in range(2)]
        h_in = [s.sem(f"h_in{u}") for u in range(2)]
        keys_mm, q_copied, k_copied = s.sem("keys_mm"), s.sem("q_copied"), s.sem("k_copied")
        scores_mm, scored, probs, turned, values_mm = (
            s.sem(n) for n in ("scores_mm", "scored", "probs", "turned", "values_mm"))
        p_copied = [s.sem(f"p_copied{k}") for k in range(2)]
        combined, step_sem, lam_dot, lam_exp = s.sem("combined"), s.sem("dve_step"), s.sem("lam_dot"), s.sem("lam_exp")
        oa_out = [s.sem(f"oa_out{u}") for u in range(2)]
        window_kept = s.sem("window_kept")
        o_sq, o_root, ob_ready, ob_out = s.sem("o_sq"), s.sem("o_root"), s.sem("ob_ready"), s.sem("ob_out")
        block = ctx.enter_context(nc.Block())

        NU = HPG * QT * 3
        DU = QT * 2
        N_BASE = GROUPS * NU
        M_BASE = GROUPS * HPG * QT
        G_LOADS, H_LOADS = 12, 4

        class Unit:
            def __init__(self, lhs, rhs, bias, width, values, out, clamp, m, br, nbr):
                self.lhs, self.rhs, self.bias, self.width, self.values, self.out = lhs, rhs, bias, width, values, out
                self.clamp, self.m, self.br, self.nbr = clamp, m, br, nbr

        def group_units(u):
            out = []
            for hh in range(HPG):
                half = slice(DK * (hh % 2), DK * (hh % 2) + DK)
                for t in range(QT):
                    m = HPG * hh + t
                    lhs = q_t[half, hh // 2, P * t:P * (t + 1)]
                    n = P * (t + 1)
                    first = P * (QT - 1 - t)
                    c0 = first + CMP_BLOCK - 1
                    cb = strip[:, u, hh, c0:c0 + CMP_STRIDE * (CHP - 1) + 1:CMP_STRIDE]
                    o = lambda br: ps_o[:, m % 2, DK * br:DK * (br + 1)]
                    out.append(Unit(lhs, kc_t[half, :], cb, CHP, [vc[:, u, :]], o(0), 1e29, m, 0, 3))
                    sb = strip[:, u, hh, first:SEQ]
                    out.append(Unit(lhs, ks_t[half, 0:n], sb, n, [vs[:, u, k, :] for k in range(t + 1)], o(1), 3e38, m, 1, 3))
                    out.append(Unit(lhs, kw_t[half, 0:n], sb, n, [vw[:, u, k, :] for k in range(t + 1)], o(2), 3e38, m, 2, 3))
            return out

        def head_units(u):
            out = []
            for t in range(QT):
                n = P * (t + 1)
                for mp in range(2):
                    half = slice(DD * mp, DD * (mp + 1))
                    out.append(Unit(q_t[half, 0, P * t:P * (t + 1)], ks_t[half, 0:n], dstrip[:, u, P * (QT - 1 - t):SEQ], n,
                                    [dv[:, u, k, :] for k in range(t + 1)], ps_o[:, t % 2, DV * mp:DV * (mp + 1)],
                                    3e38, t, mp, 2))
            return out

        @block.sync
        def _(sp):
            sp.dma_start(ident[:], d["ident"]).then_inc(consts_in, 16)
            for j, name in enumerate(("lambda_q1", "lambda_k1", "lambda_q2", "lambda_k2")):
                sp.dma_start(lv[:, j, :], spread(d[name], P)).then_inc(consts_in, 16)
            sp.dma_start(gain[:], spread(d["diff_subln"], P)).then_inc(consts_in, 16)

            def tok(ap):
                return ap.rearrange("(t p) c -> p t c", p=P)

            def load_group(g, u):
                q_cols, cols = bass.ds(g * HPG * DK, HPG * DK), lambda slot: bass.ds(g * DK + slot * KVW, DK)
                pairs = [(q[:, u, :, :], tok(d["q"][0:SEQ, q_cols])), (vs[:, u, :, :], tok(d["nsa_p"][:, cols(3)])),
                         (vw[:, u, :, :], tok(d["win_p"][:, cols(1)])), (vc[:, u, :], d["vc_p"][:, cols(0)]),
                         (strip[:, u, :, :], d["toep"][bass.ds(g * HPG, HPG), :, :].rearrange("h p x -> p h x")),
                         (gates[:, u, :, :], tok(d["g"][0:SEQ, bass.ds(g * HPG * 3, HPG * 3)]))]
                for k in range(2):
                    pairs += [(ks[:, u, :, k, :], tok(d["nsa_p"][:, cols(2)])), (kw[:, u, :, k, :], tok(d["win_p"][:, cols(0)])),
                              (kc[:, u, k, :], d["kc_p"][:, cols(0)])]
                assert len(pairs) == G_LOADS
                for dst, src in pairs:
                    sp.dma_start(dst, src).then_inc(g_in[u], 16)

            def load_head(h, u):
                cols = lambda slot: bass.ds(h * P + slot * 1024, P)
                for dst, src in ((dq[:, u, :, :], tok(d["qd"][0:SEQ, cols(0)])), (dk[:, u, :, :], tok(d["diff_p"][:, cols(0)])),
                                 (dv[:, u, :, :], tok(d["diff_p"][:, cols(1)])),
                                 (dstrip[:, u, :], d["toep"][bass.ds(h + HEADS, 1), :, 0:SEQ].rearrange("h p x -> (h p) x"))):
                    sp.dma_start(dst, src).then_inc(h_in[u], 16)

            load_group(0, 0)
            load_group(1, 1)
            for u in range(2):
                load_head(u, u)
            for g in range(GROUPS):
                sp.wait_ge(combined, HPG * QT * (g + 1) + 2)
                sp.dma_start(tok(d["oa"][0:SEQ, HPG * DK * g:HPG * DK * (g + 1)]), oa[:, g % 2, :, :]).then_inc(oa_out[g % 2], 16)
                if g + 2 < GROUPS:
                    load_group(g + 2, g % 2)
            for h in range(2, DHEADS):
                sp.wait_ge(combined, M_BASE + QT * (h - 1) + 2)
                load_head(h, h % 2)
            for u in range(2):
                sp.wait_ge(oa_out[u], 48)
            for t in range(QT):
                sp.wait_ge(ob_ready, t + 1)
                sp.dma_start(d["ob"][P * t:P * (t + 1), :], ob[:, t, :, :].rearrange("p h e -> p (h e)")).then_inc(ob_out, 16)
            sp.wait_ge(ob_out, 16 * QT)

        @block.gpsimd
        def _(pool):
            pool.dma_start(d["win_s"][:, 0:WINDOW - DEC_T, :], d["cache_win"][:, DEC_T:WINDOW, :]).then_inc(window_kept, 16)
            pool.wait_ge(window_kept, 16)

        @block.tensor
        def _(pe):
            pe.wait_ge(consts_in, 96)

            def turn_group(u, g, level):
                pe.wait_ge(g_in[u], level)
                for hp in range(2):
                    for t in range(QT):
                        ins = pe.transpose(ps_k[:, 0, P * t:P * (t + 1)], q[:, u, t, P * hp:P * (hp + 1)], ident[:])
                    ins.then_inc(keys_mm, 1)
                    for t in range(QT):
                        k = (ks, kw)[hp][:, u, t, :, :].rearrange("p a e -> p (a e)")
                        ins = pe.transpose(ps_k[:, 1, P * t:P * (t + 1)], k, ident[:])
                    ins.then_inc(keys_mm, 1)
                    pe.wait_ge(q_copied, 2 * g + hp + 1)
                    pe.wait_ge(k_copied, 3 * g + hp + 1)
                pe.sem_inc(begun_keys, 1)
                pe.transpose(ps_k[:, 1, 0:CHP], kc[:, u, :, :].rearrange("p a e -> p (a e)"),
                             ident[0:CHP, 0:CHP]).then_inc(keys_mm, 1)
                pe.wait_ge(k_copied, 3 * g + 3)

            def turn_head(u, h, level):
                pe.wait_ge(h_in[u], level)
                for t in range(QT):
                    ins = pe.transpose(ps_k[:, 0, P * t:P * (t + 1)], dq[:, u, t, :], ident[:])
                ins.then_inc(keys_mm, 1)
                for t in range(QT):
                    ins = pe.transpose(ps_k[:, 1, P * t:P * (t + 1)], dk[:, u, t, :], ident[:])
                ins.then_inc(keys_mm, 1)
                pe.wait_ge(q_copied, 2 * GROUPS + h + 1)
                pe.wait_ge(k_copied, 3 * GROUPS + h + 1)

            def scores(x, j, n):
                pe.wait_ge(scored, n + 1)
                pe.matmul(ps_s[:, j % 2, 0:x.width], x.lhs, x.rhs, start=True, stop=True).then_inc(scores_mm, 1)

            def turn(x, j, n):
                pe.wait_ge(probs, n + 1)
                pe.wait_ge(p_copied[j % 2], half_count(n, j))
                for k, v in enumerate(x.values):
                    r = v.shape[0]
                    ins = pe.transpose(ps_t[0:r, j % 2, P * k:P * (k + 1)], sc[:, j % 4, P * k:P * k + r], ident[:])
                ins.then_inc(turned, 1)

            def values(x, j, n, m):
                pe.wait_ge(p_copied[j % 2], half_count(n, j) + 1)
                if x.br == 0:
                    pe.wait_ge(combined, m + 1)
                for k, v in enumerate(x.values):
                    r = v.shape[0]
                    ins = pe.matmul(x.out, p_t[0:r, j % 2, P * k:P * (k + 1)], v, start=k == 0, stop=k == len(x.values) - 1)
                ins.then_inc(values_mm, 1)

            def half_count(n, j):
                return base_half[0] + j // 2 + 1

            base_half = [None]

            def run(units, n0, h0, m0):
                base_half[0] = h0
                for j in range(len(units) + 3):
                    if j < len(units):
                        scores(units[j], j, n0 + j)
                    if 2 <= j < len(units) + 2:
                        turn(units[j - 2], j - 2, n0 + (j - 2))
                    if j >= 3:
                        values(units[j - 3], j - 3, n0 + (j - 3), m0 + units[j - 3].m)

            with pe.Fori(0, GROUPS // 2) as i:
                for u in range(2):
                    turn_group(u, 2 * i + u, 16 * G_LOADS * i + 16 * G_LOADS)
                    run(group_units(u), NU * (2 * i + u), NU // 2 * (2 * i + u), HPG * QT * (2 * i + u))
            with pe.Fori(0, DHEADS // 2) as i:
                for u in range(2):
                    h = 2 * i + u
                    turn_head(u, h, 16 * H_LOADS * i + 16 * H_LOADS)
                    run(head_units(u), N_BASE + DU * h, N_BASE // 2 + DU // 2 * h, M_BASE + QT * h)

        @block.scalar
        def _(act):
            act.wait_ge(lam_dot, 1)
            nc.scalar.activation(lam[:, 1:3], lam[:, 1:3], ACT.Exp).then_inc(lam_exp, 1)

            def exps(x, j, n, m):
                act.wait_ge(scored, n + 3)
                nc.scalar.activation(sc[:, j % 4, 0:x.width], sc[:, j % 4, 0:x.width], ACT.Exp, scale=-1.0,
                                     bias=nmax[:, j % 4:j % 4 + 1], accum_out=rsum[:, x.m % 4, x.br:x.br + 1]
                                     ).then_inc(probs, 1)

            def copy(x, j, n):
                act.wait_ge(turned, n + 5)
                act.wait_ge(values_mm, n + 1)
                r, w = x.values[0].shape[0], P * len(x.values)
                nc.scalar.activation(p_t[0:r, 0, 0:w], ps_t[0:r, 0, 0:w], ACT.Copy).then_inc(p_copied[0], 1)

            def run(units, n0, m0):
                for j in range(len(units) + 2):
                    if j < len(units):
                        exps(units[j], j, n0 + j, m0)
                    if j >= 2 and (j - 2) % 2 == 0:
                        copy(units[j - 2], j - 2, n0 + (j - 2))

            with act.Fori(0, GROUPS // 2) as i:
                for u in range(2):
                    g = 2 * i + u
                    for hp in range(2):
                        act.wait_ge(keys_mm, 5 * g + 2 * hp + 1)
                        nc.scalar.activation(q_t[:, hp, :], ps_k[:, 0, :], ACT.Copy).then_inc(q_copied, 1)
                    run(group_units(u), NU * g, HPG * QT * g)
            with act.Fori(0, DHEADS // 2) as i:
                for u in range(2):
                    h = 2 * i + u
                    act.wait_ge(keys_mm, 5 * GROUPS + 2 * h + 1)
                    nc.scalar.activation(q_t[:, 0, :], ps_k[:, 0, :], ACT.Copy).then_inc(q_copied, 1)
                    run(head_units(u), N_BASE + DU * h, M_BASE + QT * h)
            act.wait_ge(o_sq, QT + 1)
            nc.scalar.activation(ssum[:], ssum[:], ACT.Sqrt).then_inc(o_root, 1)

        @block.vector
        def _(dve):
            nc.vector.nop().then_inc(scored, 2)
            nc.vector.nop().then_inc(combined, 2)
            nc.vector.nop().then_inc(turned, 4)
            nc.vector.nop().then_inc(values_mm, 2)
            for k in range(2):
                nc.vector.nop().then_inc(p_copied[k], 1)
                nc.vector.nop().then_inc(oa_out[k], 16)
            step = Chain(dve, step_sem)
            dve.wait_ge(consts_in, 96)
            lambda_steps(nc, dve, lam_exp, lam, lv, step, lam_dot)
            step(nc.vector.tensor_scalar(gain[:], gain[:], 1.0 - LAM_INIT, None, ALU.mult))
            done = step.n

            def score(x, j, n):
                dve.wait_ge(scores_mm, n + 1)
                dve.wait_ge(turned, n + 1)
                dve.sem_inc(begun, 1)
                nc.vector.tensor_tensor_reduce(out=sc[:, j % 4, 0:x.width], in0=ps_s[:, j % 2, 0:x.width], in1=x.bias,
                                               scale=-1.0, scalar=x.clamp, op0=ALU.add, op1=ALU.min,
                                               accum_out=nmax[:, j % 4:j % 4 + 1]).then_inc(scored, 1)

            def copy(x, j, n):
                dve.wait_ge(turned, n + 5)
                dve.wait_ge(values_mm, n + 1)
                r, w = x.values[0].shape[0], P * len(x.values)
                nc.vector.tensor_copy(p_t[0:r, 1, 0:w], ps_t[0:r, 1, 0:w]).then_inc(p_copied[1], 1)

            def combine_group(x, n, u, chain):
                k, hh, t = x.m % 2, x.m // QT, x.m % QT
                dve.wait_ge(values_mm, n + 3)
                chain(nc.vector.tensor_scalar(coef[:, k, 0:3], rsum[:, x.m % 4, 0:3], TINY, None, ALU.max))
                chain(nc.vector.reciprocal(coef[:, k, 0:3], coef[:, k, 0:3]))
                chain(nc.vector.tensor_tensor(coef[:, k, 0:3], coef[:, k, 0:3], gates[:, u, t, 3 * hh:3 * hh + 3], ALU.mult))
                pv = part[:, 0:3 * DK].rearrange("p (b e) -> p b e", e=DK)
                chain(nc.vector.tensor_tensor(pv, ps_o[:, k, 0:3 * DK].rearrange("p (b e) -> p b e", e=DK),
                                              coef[:, k, 0:3].unsqueeze(2).to_broadcast([P, 3, DK]), ALU.mult))
                nc.vector.tensor_reduce(oa[:, u, t, DK * hh:DK * (hh + 1)], part[:, 0:3 * DK].rearrange("p (b e) -> p e b", e=DK),
                                        AX.X, ALU.add).then_inc(combined, 1)

            def combine_head(x, n, h, chain):
                k, t = x.m % 2, x.m % QT
                dve.wait_ge(values_mm, n + 3)
                chain(nc.vector.tensor_scalar(coef[:, k, 0:2], rsum[:, x.m % 4, 0:2], TINY, None, ALU.max))
                chain(nc.vector.reciprocal(coef[:, k, 0:2], coef[:, k, 0:2]))
                chain(nc.vector.tensor_tensor(coef[:, k, 1:2], coef[:, k, 1:2], lam[:, 0:1], ALU.mult))
                chain(nc.vector.tensor_scalar(part[:, 0:DV], ps_o[:, k, DV:2 * DV], coef[:, k, 1:2], None, ALU.mult))
                out = ob[:, t, bass.ds(h, 1), :].rearrange("p a e -> p (a e)")
                nc.vector.scalar_tensor_tensor(out=out, in0=ps_o[:, k, 0:DV], scalar=coef[:, k, 0:1],
                                               in1=part[:, 0:DV], op0=ALU.mult, op1=ALU.add).then_inc(combined, 1)

            def run(units, n0, combine):
                LAG = 5
                for j in range(len(units) + LAG):
                    if j < len(units):
                        score(units[j], j, n0 + j)
                    if 2 <= j < len(units) + 2 and j % 2 == 1:
                        copy(units[j - 2], j - 2, n0 + (j - 2))
                    if j >= LAG:
                        x = units[j - LAG]
                        if x.br == x.nbr - 1:
                            combine(x, n0 + (j - LAG))

            with dve.Fori(0, GROUPS // 2) as i:
                chain = Chain(dve, step_sem, 2 * HPG * QT * 4 * i + done)
                for u in range(2):
                    g = 2 * i + u
                    for k, dst in enumerate((ks_t, kw_t)):
                        dve.wait_ge(keys_mm, 5 * g + 2 * k + 2)
                        nc.vector.tensor_copy(dst[:], ps_k[:, 1, :]).then_inc(k_copied, 1)
                    dve.wait_ge(keys_mm, 5 * g + 5)
                    nc.vector.tensor_copy(kc_t[:], ps_k[:, 1, 0:CHP]).then_inc(k_copied, 1)
                    dve.wait_ge(oa_out[u], 16 * i + 16)
                    run(group_units(u), NU * g, lambda x, n: combine_group(x, n, u, chain))
            done += GROUPS * HPG * QT * 4
            with dve.Fori(0, DHEADS // 2) as i:
                chain = Chain(dve, step_sem, 2 * QT * 4 * i + done)
                for u in range(2):
                    h = 2 * i + u
                    dve.wait_ge(keys_mm, 5 * GROUPS + 2 * h + 2)
                    nc.vector.tensor_copy(ks_t[:], ps_k[:, 1, :]).then_inc(k_copied, 1)
                    run(head_units(u), N_BASE + DU * h, lambda x, n: combine_head(x, n, h, chain))
            done += DHEADS * QT * 4
            step = Chain(dve, step_sem, done)
            for t in range(QT):
                step(nc.vector.tensor_tensor(osq[:], ob[:, t, :, :], ob[:, t, :, :], ALU.mult))
                nc.vector.tensor_reduce(ssum[:, DHEADS * t:DHEADS * (t + 1)], osq[:], AX.X, ALU.add).then_inc(o_sq, 1)
                dve.wait_ge(o_sq, t + 1)
            nc.vector.tensor_scalar(ssum[:], ssum[:], 1.0 / DV, EPS, ALU.mult, ALU.add).then_inc(o_sq, 1)
            dve.wait_ge(o_root, 1)
            step(nc.vector.reciprocal(ssum[:], ssum[:]))
            for t in range(QT):
                step(nc.vector.tensor_tensor(ob[:, t, :, :], ob[:, t, :, :],
                                             ssum[:, DHEADS * t:DHEADS * (t + 1)].unsqueeze(2).to_broadcast([P, DHEADS, DV]),
                                             ALU.mult))
                nc.vector.tensor_tensor(ob[:, t, :, :], ob[:, t, :, :], gain[:].unsqueeze(1).to_broadcast([P, DHEADS, DV]),
                                        ALU.mult).then_inc(ob_ready, 1)


PAIRS = DEC_B // 2
ROWS = P // 2
NCOL = PAST + DEC_T
CMPS = ROWS

C_GROUP, C_STACK, C_IDX, C_WIN, C_MAP, C_NSA, C_DIFF = 0, 128, 192, 209, 213, 215, 471
C_ALL = 983


def decode_constants():
    c = np.zeros((P, C_ALL), np.float32)
    for r in range(P):
        b, x = divmod(r, ROWS)
        h, t = divmod(x, DEC_T)
        for y in range(ROWS):
            c[r, C_GROUP + ROWS * b + y] = float(x // (HPG * DEC_T) == y // (HPG * DEC_T) and y % DEC_T == t)
        c[r, C_STACK + 32 * b + x % 32] = 1.0
        c[r, C_IDX:C_IDX + N_SLC] = np.arange(N_SLC)
        c[r, C_WIN:C_WIN + DEC_T] = [NEG if j <= t else 0.0 for j in range(DEC_T)]
        c[r, C_MAP + x // 32] = 1.0
        g = h // HPG
        c[r, C_NSA + DK * g:C_NSA + DK * (g + 1)] = 1.0
        half, dh = (r // 32) % 2, (r % 32) // DEC_T
        if dh // 4 == half:
            c[r, C_DIFF + DV * (dh % 4):C_DIFF + DV * (dh % 4 + 1)] = 1.0
    return c


def select_weights():
    c0 = np.arange(CMPS)[:, None] * CMP_STRIDE
    s0 = np.arange(N_SLC)[None, :] * SEL_BLOCK
    shared = np.clip(np.minimum(c0 + CMP_BLOCK, s0 + SEL_BLOCK) - np.maximum(c0, s0), 0, None)
    return (shared / CMP_BLOCK).astype(np.float32)


CHAIN = 24


def decode_attention(nc, d):
    with ExitStack() as ctx:
        s = Space(nc, ctx, "de")
        sel = s.sb("sel", [P, 2, N_PAGES, 2 * KVW])
        win = s.sb("win", [P, 2, WINDOW // P, 2 * KVW])
        dk = s.sb("dk", [P, 2, 2, DHEADS * P])
        dv = s.sb("dv", [P, 2, N_PAGES, DHEADS * DV])
        sel_n = s.sb("sel_n", [DEC_T, 2, 2 * KVW])
        win_n = s.sb("win_n", [DEC_T, 2, 2 * KVW])
        dk_n = s.sb("dk_n", [DEC_T, 2, DHEADS * P])
        dv_n = s.sb("dv_n", [DEC_T, 2, DHEADS * DV])
        kc = s.sb("kc", [P, KVW])
        vc = s.sb("vc", [P, KVW])
        qn = s.sb("qn", [2 * DEC_T, D_MODEL])
        qd = s.sb("qd", [2 * DEC_T, D_MODEL])
        gates = s.sb("gates", [P, 3])
        qb = s.sb("qb", [P, 2, 2, ROWS])
        qdb = s.sb("qdb", [P, DHEADS, 2, ROWS])
        slot = s.sb("slot", [P, 3, CW])
        s_cmp = s.sb("s_cmp", [P, CMPS])
        s_sel = s.sb("s_sel", [P, NCOL])
        s_win = s.sb("s_win", [P, WINDOW + DEC_T])
        s_dif = s.sb("s_dif", [P, NCOL])
        qp = s_dif[0:2 * DEC_T, 0:D_MODEL]
        b_nsa = s.sb("b_nsa", [P, DECW])
        b_win = s.sb("b_win", [P, WINDOW + DEC_T])
        b_dif = s.sb("b_dif", [P, NCOL])
        con = s.sb("con", [P, C_ALL])
        selw = s.sb("selw", [CMPS, N_SLC])
        nm = s.sb("nm", [P, 4, 4])
        rs = s.sb("rs", [P, 4])
        rr = s.sb("rr", [P, 8])
        cm = s.sb("cm", [P, 3, P])
        cd = s.sb("cd", [P, 64])
        gm = s.sb("gm", [P, P])
        pg = s.sb("pg", [CMPS, P])
        pick = s.sb("pick", [P, 3, N_SLC])
        part = s.sb("part", [P, CW])
        o_n = s.sb("o_n", [P, DK])
        o_d = s.sb("o_d", [P, DV])
        table = s.sb("table", [1, DEC_B * N_PAGES], I32)
        ident = s.sb("ident", [P, P])
        lam = s.sb("lam", [P, 4])
        lv = part[:, 0:4 * DD].rearrange("p (v e) -> p v e", e=DD)
        gain = s.sb("gain", [P, DV])
        ps_t = s.ps("ps_t", [P, 3, CW])
        ps_s = s.ps("ps_s", [P, 2, CW])
        ps_n = s.ps("ps_n", [P, CW])
        ps_d = s.ps("ps_d", [P, CW])
        Q_AT, PG_AT, IMP_AT = 256, 384, 256

        consts_in, table_in, b_ready, begun, begun_pe = (
            s.sem(n) for n in ("consts_in", "table_in", "b_ready", "begun", "begun_pe"))
        begun_sp, begun_pool = s.sem("begun_sp"), s.sem("begun_pool")
        q_in, new_in = s.sem("q_in"), s.sem("new_in")
        sel_in = [s.sem(f"sel_in{k}") for k in range(N_PAGES)]
        win_in = [s.sem(f"win_in{k}") for k in range(WINDOW // P)]
        dk_in = [s.sem(f"dk_in{k}") for k in range(2)]
        dv_in = [s.sem(f"dv_in{k}") for k in range(N_PAGES)]
        q_laid, q_turned, q_ready = s.sem("q_laid"), s.sem("q_turned"), s.sem("q_ready")
        turned, scores_mm, scored = s.sem("turned"), s.sem("scores_mm"), s.sem("scored")
        copied = [s.sem(f"copied{k}") for k in range(2)]
        max_ready, probs, coef_ready = s.sem("max_ready"), s.sem("probs"), s.sem("coef_ready")
        pg_mm, pg_copied, imp_mm = s.sem("pg_mm"), s.sem("pg_copied"), s.sem("imp_mm")
        nsa_mm, diff_mm, nsa_read, diff_read = s.sem("nsa_mm"), s.sem("diff_mm"), s.sem("nsa_read"), s.sem("diff_read")
        o_sq, o_root, nsa_out, diff_out = s.sem("o_sq"), s.sem("o_root"), s.sem("nsa_out"), s.sem("diff_out")
        nsa_stored, diff_stored = s.sem("nsa_stored"), s.sem("diff_stored")
        o_n_free, o_d_free = s.sem("o_n_free"), s.sem("o_d_free")
        step_sem, lam_dot, lam_exp = s.sem("dve_step"), s.sem("lam_dot"), s.sem("lam_exp")
        block = ctx.enter_context(nc.Block())

        STEPS = ([("sel", k, 0) for k in range(N_PAGES)] + [("win", k, 0) for k in range(WINDOW // P)]
                 + [("sel_n", 0, 0), ("win_n", 0, 0), ("cmp", 0, 0)] + [("dif_n", 0, k) for k in range(4)]
                 + [("dif", k, m) for k in range(N_PAGES) for m in range(4)]
                 + [("p_sel", 0, 0), ("p_sel", 1, 0), ("p_few", 0, 0), ("p_win", 0, 0), ("p_dif", 0, 0), ("p_dif_n", 0, 0)])
        N = len(STEPS)
        assert N % 3 == 0
        EVEN, ODD = (N + 1) // 2, N // 2
        AT = {x: k for k, x in reversed(list(enumerate(STEPS)))}
        SEL0, SEL1, WIN0, FEW, DIF0, DIF1 = range(6)
        LAST = [AT["sel", 3, 0], AT["sel", 7, 0], AT["win", 3, 0], AT["dif_n", 0, 3], AT["dif", 3, 3], AT["dif", 7, 3]]
        GROUP_OF = {}
        for g, (kind, a, b) in enumerate((("sel", 0, 4), ("sel", 4, 8), ("win", 0, 4), (None, 0, 0), ("dif", 0, 4), ("dif", 4, 8))):
            for k in range(a, b):
                GROUP_OF[kind, k] = g
        F_CMP, F_SEL, F_WIN, F_DIF = 0, 64, 68, 72
        TURN_CREDIT = N
        IMP_1, IMP_2 = LAST[FEW] + 6, LAST[FEW] + 9
        READ_AT = {last + 2 + (last + 1) % 2: g for g, last in enumerate(LAST)}
        GROUP_AT, SHARE_AT, CHOOSE_AT, SCALE_AT, SCALE_D_AT = IMP_1 - 1, IMP_1 + 1, IMP_2 + 2, IMP_2 + 6, LAST[DIF1] + 3
        assert all(x % 2 for x in (GROUP_AT, SHARE_AT, CHOOSE_AT, SCALE_AT, SCALE_D_AT, *READ_AT))

        def score_place(kind, k):
            if kind in ("sel", "win", "dif"):
                return GROUP_OF[kind, k] % 2, P * (k % 4)
            return FEW % 2, {"cmp": F_CMP, "sel_n": F_SEL, "win_n": F_WIN, "dif_n": F_DIF}[kind]

        def pieces(j):
            kind = STEPS[j][0]
            if kind in ("sel_n", "win_n", "dif_n"):
                return [(slice(0, P), slice(0, 4 * DEC_T))]
            if kind == "cmp":
                return [(slice(0, P), slice(0, 2 * P))]
            if kind == "p_few":
                return [(slice(0, DEC_T), slice(0, 4 * ROWS)), (slice(0, ROWS), slice(4 * ROWS, 5 * ROWS)),
                        (slice(ROWS, P), slice(5 * ROWS, 6 * ROWS))]
            if kind == "p_dif_n":
                return [(slice(0, DEC_T), slice(0, 64))]
            return [(slice(0, P), slice(0, CW))]

        @block.sync
        def _(sp):
            sp.dma_start(table[:], d["page_table"]).then_inc(table_in, 16)
            sp.dma_start(ident[:], d["ident"]).then_inc(consts_in, 16)
            for j, name in enumerate(("lambda_q1", "lambda_k1", "lambda_q2", "lambda_k2")):
                sp.dma_start(lv[:, j, :], spread(d[name], P)).then_inc(consts_in, 16)
            sp.dma_start(gain[:], spread(d["diff_subln"], P)).then_inc(consts_in, 16)
            sp.dma_start(con[:], d["decode_constants"]).then_inc(consts_in, 16)
            sp.dma_start(selw[:], d["select_weights"]).then_inc(consts_in, 16)
            for b in range(2):
                rows = slice(ROWS * b, ROWS * (b + 1))
                sp.dma_start(b_nsa[rows, :], d["decb"][0:HEADS].rearrange("h t k -> (h t) k")).then_inc(consts_in, 16)
                sp.dma_start(b_win[rows, :], d["decb"][0:HEADS, :, PAST - WINDOW:NCOL].rearrange("h t k -> (h t) k")
                             ).then_inc(consts_in, 16)
                for m in range(2):
                    sp.dma_start(b_dif[rows.start + 32 * m:rows.start + 32 * m + 32, :],
                                 d["decb"][HEADS:24, :, 0:NCOL].rearrange("h t k -> (h t) k")).then_inc(consts_in, 16)
            sp.wait_ge(table_in, 16)
            n_phys = d["cache_nsa"].shape[0]

            with sp.Fori(0, PAIRS) as i:
                def page(b, k):
                    return sp.value_load(table[0:1, bass.ds((2 * i + b) * N_PAGES + k, 1)], min_val=0, max_val=n_phys - 1)

                tok = bass.ds(2 * DEC_T * i + SEQ, 2 * DEC_T)
                new = bass.ds(2 * DEC_T * i, 2 * DEC_T)
                sp.wait_ge(turned, N * i + LAST[FEW] + 1)
                for dst, src in ((qn[:], d["q"][tok, :]), (qd[:], d["qd"][tok, :]), (kc[:], d["kc_s"][bass.ds(P * i, P), :])):
                    sp.dma_start(dst, src).then_inc(q_in, 16)
                sp.wait_ge(nsa_mm, i + 1)
                sp.sem_inc(begun_sp, 1)
                for k in range(N_PAGES):
                    for b in range(2):
                        sp.dma_start(sel[:, b, k, :], d["cache_nsa"][bass.ds(page(b, k), 1), :, 2 * KVW:4 * KVW]
                                     .rearrange("n p e -> (n p) e")).then_inc(sel_in[k], 16)
                for k in range(WINDOW // P):
                    for b in range(2):
                        sp.dma_start(win[:, b, k, :], d["cache_win"][bass.ds(2 * i + b, 1), P * k:P * (k + 1), :]
                                     .rearrange("n p e -> (n p) e")).then_inc(win_in[k], 16)
                sp.wait_ge(diff_mm, i + 1)
                sp.dma_start(vc[:], d["vc_s"][bass.ds(P * i, P), :]).then_inc(new_in, 16)
                for dst, src in ((sel_n, d["nsa_s"][new, 2 * KVW:4 * KVW]), (dk_n, d["diff_s"][new, 0:1024]),
                                 (dv_n, d["diff_s"][new, 1024:2048])):
                    sp.dma_start(dst[:], src.rearrange("(b t) e -> t b e", b=2)).then_inc(new_in, 16)
                sp.dma_start(win_n[:], d["win_s"][bass.ds(2 * i, 2), WINDOW - DEC_T:WINDOW, :].rearrange("b t e -> t b e")
                             ).then_inc(new_in, 16)
                with nc.allow_non_contiguous_dma("three gates of a head"):
                    for b in range(2):
                        sp.dma_start(gates[ROWS * b:ROWS * (b + 1), :],
                                     d["g"][bass.ds(2 * DEC_T * i + SEQ + DEC_T * b, DEC_T), :]
                                     .rearrange("t (h c) -> h t c", c=3)).then_inc(new_in, 16)

                def load_k(k):
                    first = N * i + AT["dif", k - 2, 3] + 1 + TURN_CREDIT if k >= 2 else N * i + AT["dif", k + 6, 3] + 1
                    sp.wait_ge(turned, first)
                    sp.sem_inc(begun_sp, 1)
                    for b in range(2):
                        sp.dma_start(dk[:, k % 2, b, :], d["cache_diff"][bass.ds(page(b, k), 1), :, 0:1024]
                                     .rearrange("n p e -> (n p) e")).then_inc(dk_in[k % 2], 16)

                def load_v(k):
                    for b in range(2):
                        sp.dma_start(dv[:, b, k, :], d["cache_diff"][bass.ds(page(b, k), 1), :, 1024:2048]
                                     .rearrange("n p e -> (n p) e")).then_inc(dv_in[k], 16)

                load_k(0)
                load_k(1)
                for k in range(N_PAGES):
                    load_v(k)
                    if k + 2 < N_PAGES:
                        load_k(k + 2)

        @block.gpsimd
        def _(pool):
            with pool.Fori(0, PAIRS) as i:
                pool.wait_ge(nsa_out, i + 2)
                pool.sem_inc(begun_pool, 1)
                for b in range(2):
                    pool.dma_start(d["oa"][bass.ds(2 * DEC_T * i + SEQ + DEC_T * b, DEC_T), :].rearrange("t (h e) -> h t e", e=DK),
                                   o_n[ROWS * b:ROWS * (b + 1), :]).then_inc(nsa_stored, 16)
                pool.wait_ge(diff_out, i + 2)
                pool.sem_inc(begun_pool, 1)
                for b in range(2):
                    for half in range(2):
                        at = ROWS * b + 32 * half + 16 * half
                        pool.dma_start(d["ob"][bass.ds(2 * DEC_T * i + SEQ + DEC_T * b, DEC_T), 512 * half:512 * (half + 1)]
                                       .rearrange("t (h e) -> h t e", e=DV), o_d[at:at + 16, :]).then_inc(diff_stored, 16)
                pool.wait_ge(nsa_stored, 32 * i + 32)
                pool.sem_inc(o_n_free, 1)
                pool.wait_ge(diff_stored, 64 * i + 64)
                pool.sem_inc(o_d_free, 1)
            pool.wait_ge(nsa_stored, 32 * PAIRS)
            pool.wait_ge(diff_stored, 64 * PAIRS)

        @block.tensor
        def _(pe):
            pe.wait_ge(consts_in, 16 * 16)

            def stand():
                pe.sem_inc(begun_pe, 1)

            def turn(i, j):
                kind, k, m = STEPS[j]
                bank = ps_t[:, j % 3, :]
                if kind in ("sel", "win"):
                    src, arrived = (sel, sel_in) if kind == "sel" else (win, win_in)
                    pe.wait_ge(arrived[k], 32 * i + 32)
                    for b in range(2):
                        for g in range(2):
                            c = 2 * b + g
                            ins = pe.transpose(bank[:, P * c:P * (c + 1)], src[:, b, k, P * g:P * (g + 1)], ident[:])
                elif kind in ("sel_n", "win_n", "dif_n"):
                    src = {"sel_n": sel_n, "win_n": win_n, "dif_n": dk_n}[kind]
                    if kind == "sel_n":
                        pe.wait_ge(new_in, 112 * i + 112)
                        stand()
                    for b in range(2):
                        for g in range(2):
                            c = 2 * b + g
                            ins = pe.transpose(bank[:, DEC_T * c:DEC_T * (c + 1)],
                                               src[:, b, P * (2 * m + g):P * (2 * m + g + 1)], ident[0:DEC_T, 0:DEC_T])
                elif kind == "cmp":
                    for g in range(2):
                        ins = pe.transpose(bank[:, P * g:P * (g + 1)], kc[:, P * g:P * (g + 1)], ident[:])
                elif kind == "dif":
                    if m == 0:
                        pe.wait_ge(dk_in[k % 2], 128 * i + 32 * (k // 2) + 32)
                    for b in range(2):
                        for g in range(2):
                            c, h = 2 * b + g, 2 * m + g
                            ins = pe.transpose(bank[:, P * c:P * (c + 1)], dk[:, k % 2, b, P * h:P * (h + 1)], ident[:])
                elif kind == "p_sel" or kind == "p_win":
                    pr, which = (s_sel, 1) if kind == "p_sel" else (s_win, 2)
                    if kind == "p_sel" and k == 0:
                        pe.wait_ge(coef_ready, 5 * i + 4)
                    for x in range(4):
                        cols = slice(P * (4 * k + x), P * (4 * k + x + 1))
                        ins = pe.matmul(bank[:, P * x:P * (x + 1)], pr[:, cols], cm[:, which, :], start=True, stop=True)
                elif kind == "p_few":
                    for x, (pr, which, first) in enumerate(((s_sel, 1, PAST), (s_win, 2, WINDOW))):
                        pe.matmul(bank[0:DEC_T, P * x:P * (x + 1)], pr[:, first:first + DEC_T], cm[:, which, :], start=True, stop=True)
                    for b in range(2):
                        rows = slice(ROWS * b, ROWS * (b + 1))
                        ins = pe.matmul(bank[rows, 2 * P + ROWS * b:2 * P + ROWS * (b + 1)], s_cmp[:], cm[:, 0, rows],
                                        start=True, stop=True)
                elif kind == "p_dif":
                    pe.wait_ge(coef_ready, 5 * i + 5)
                    for x in range(N_PAGES):
                        ins = pe.matmul(bank[:, 64 * x:64 * (x + 1)], s_dif[:, P * x:P * (x + 1)], cd[:], start=True, stop=True)
                else:
                    ins = pe.matmul(bank[0:DEC_T, 0:64], s_dif[:, PAST:NCOL], cd[:], start=True, stop=True)
                ins.then_inc(turned, 1)

            def multiply(i, j):
                kind, k, m = STEPS[j]
                tile = slot[:, j % 3, :]
                pe.wait_ge(copied[j % 2], (ODD if j % 2 else EVEN) * i + j // 2 + 1)
                ins = None
                if kind in ("sel", "win", "sel_n", "win_n", "cmp", "dif", "dif_n"):
                    bank, at = score_place(kind, k)
                    n = {"cmp": CMPS, "sel_n": DEC_T, "win_n": DEC_T, "dif_n": DEC_T}.get(kind, P)
                    group = {("sel", 0): SEL0, ("sel", 4): SEL1, ("win", 0): WIN0, ("sel_n", 0): FEW, ("dif", 0): DIF0,
                             ("dif", 4): DIF1}.get((kind, k))
                    if group is not None and m == 0:
                        pe.wait_ge(scored, 6 * i + group + 1)
                    for g in range(2):
                        for b in range(2):
                            lhs = qdb[:, 2 * m + g, b, :] if kind in ("dif", "dif_n") else qb[:, g, b, :]
                            c = (2 * b + g) * n
                            if kind == "cmp":
                                c = P * g + CMPS * b
                            first = g == 0 and m == 0
                            last = g == 1 and (kind not in ("dif", "dif_n") or m == 3)
                            ins = pe.matmul(ps_s[ROWS * b:ROWS * (b + 1), bank, at:at + n], lhs, tile[:, c:c + n],
                                            start=first, stop=last)
                    if j in LAST:
                        ins.then_inc(scores_mm, 1)
                elif kind in ("p_sel", "p_win"):
                    if kind == "p_sel" and k == 0:
                        pe.wait_ge(nsa_read, i + 1)
                    for x in range(4):
                        v = sel[:, :, 4 * k + x, KVW:2 * KVW] if kind == "p_sel" else win[:, :, x, KVW:2 * KVW]
                        for b in range(2):
                            ins = pe.matmul(ps_n[ROWS * b:ROWS * (b + 1), 0:KVW], tile[:, P * x + ROWS * b:P * x + ROWS * (b + 1)],
                                            v[:, b, :], start=kind == "p_sel" and k == 0 and x == 0,
                                            stop=kind == "p_win" and x == 3)
                    if kind == "p_win":
                        ins.then_inc(nsa_mm, 1)
                elif kind == "p_few":
                    for x in range(3):
                        for b in range(2):
                            rows = slice(ROWS * b, ROWS * (b + 1)) if x == 2 else slice(0, DEC_T)
                            v = (sel_n[:, b, KVW:2 * KVW], win_n[:, b, KVW:2 * KVW], vc[rows, :])[x]
                            ins = pe.matmul(ps_n[ROWS * b:ROWS * (b + 1), 0:KVW], tile[rows, P * x + ROWS * b:P * x + ROWS * (b + 1)],
                                            v, start=False, stop=False)
                elif kind == "p_dif":
                    pe.wait_ge(diff_read, i + 1)
                    for x in range(N_PAGES):
                        pe.wait_ge(dv_in[x], 32 * i + 32)
                        for b in range(2):
                            for half in range(2):
                                o = 64 * b + 32 * half
                                ins = pe.matmul(ps_d[o:o + 32, :], tile[:, 64 * x + 32 * b:64 * x + 32 * b + 32],
                                                dv[:, b, x, CW * half:CW * (half + 1)], start=x == 0, stop=False)
                else:
                    stand()
                    for b in range(2):
                        for half in range(2):
                            o = 64 * b + 32 * half
                            ins = pe.matmul(ps_d[o:o + 32, :], tile[0:DEC_T, 32 * b:32 * b + 32],
                                            dv_n[:, b, CW * half:CW * (half + 1)], start=False, stop=True)
                    ins.then_inc(diff_mm, 1)

            with pe.Fori(0, PAIRS) as i:
                pe.wait_ge(q_in, 48 * i + 48)
                pe.wait_ge(q_laid, i + 1)
                stand()
                for x in range(16):
                    src = qp if x < 8 else qd
                    ins = pe.transpose(ps_n[:, Q_AT + 8 * x:Q_AT + 8 * x + 8], src[:, P * (x % 8):P * (x % 8 + 1)],
                                       ident[0:2 * DEC_T, 0:2 * DEC_T])
                ins.then_inc(q_turned, 1)
                pe.wait_ge(q_ready, i + 1)
                for j in range(N + 2):
                    if j < N:
                        turn(i, j)
                    if j >= 2:
                        multiply(i, j - 2)
                    if j - 2 == IMP_1:
                        pe.wait_ge(coef_ready, 5 * i + 1)
                        stand()
                        pe.matmul(ps_n[0:CMPS, PG_AT:PG_AT + P], s_cmp[:], gm[:], start=True, stop=True).then_inc(pg_mm, 1)
                    if j - 2 == IMP_2:
                        pe.wait_ge(pg_copied, i + 1)
                        stand()
                        pe.matmul(ps_n[:, IMP_AT:IMP_AT + N_SLC], pg[:], selw[:], start=True, stop=True).then_inc(imp_mm, 1)

        @block.scalar
        def _(act):
            act.wait_ge(lam_dot, 1)
            nc.scalar.activation(lam[:, 1:3], lam[:, 1:3], ACT.Exp).then_inc(lam_exp, 1)
            with act.Fori(0, PAIRS) as i:
                def exp(kind, tile, level):
                    act.wait_ge(max_ready, 4 * i + level)
                    nc.scalar.activation(tile, tile, ACT.Exp, scale=-1.0, bias=nm[:, kind, 3:4],
                                         accum_out=rs[:, kind:kind + 1]).then_inc(probs, 1)

                for j in range(0, N, 2):
                    act.wait_ge(turned, N * i + j + 1 + TURN_CREDIT)
                    todo = pieces(j)
                    for x, (rows, cols) in enumerate(todo):
                        ins = nc.scalar.activation(slot[rows, j % 3, cols], ps_t[rows, j % 3, cols], ACT.Copy)
                    ins.then_inc(copied[0], 1)
                    if j == LAST[FEW] + 2:
                        exp(0, s_cmp[:], 1)
                        exp(2, s_win[:], 2)
                    if j == LAST[FEW] + 12:
                        exp(1, s_sel[:], 3)
                    if j == LAST[DIF1] + 2:
                        exp(3, s_dif[:], 4)
                act.wait_ge(o_sq, 2 * i + 2)
                nc.scalar.activation(rr[:, 7:8], rr[:, 6:7], ACT.Sqrt).then_inc(o_root, 1)

        @block.vector
        def _(dve):
            def stand():
                dve.sem_inc(begun, 1)

            nc.vector.nop().then_inc(turned, TURN_CREDIT)
            nc.vector.nop().then_inc(scored, 2)
            for x in (nsa_mm, diff_mm, nsa_read, diff_read, nsa_out, diff_out, o_n_free, o_d_free):
                nc.vector.nop().then_inc(x, 1)
            step = Chain(dve, step_sem)
            step(nc.vector.memset(qb[:], 0.0))
            step(nc.vector.memset(qdb[:], 0.0))
            dve.wait_ge(consts_in, 16 * 16)
            lambda_steps(nc, dve, lam_exp, lam, lv, step, lam_dot)
            step(nc.vector.tensor_scalar(gain[:], gain[:], 1.0 - LAM_INIT, None, ALU.mult))
            step(nc.vector.scalar_tensor_tensor(out=lam[:, 3:4], in0=con[:, C_MAP + 1:C_MAP + 2], scalar=lam[:, 0:1],
                                                in1=con[:, C_MAP:C_MAP + 1], op0=ALU.mult, op1=ALU.add))
            step(nc.vector.tensor_tensor(b_win[:, 0:DEC_T], b_win[:, 0:DEC_T], con[:, C_WIN:C_WIN + DEC_T], ALU.add))
            done = step.n

            with dve.Fori(0, PAIRS) as i:
                chain = Chain(dve, step_sem, CHAIN * i + done)

                def lowest(kind, piece, out, in0, in1, last=None):
                    stand()
                    ins = nc.vector.tensor_tensor_reduce(out=out, in0=in0, in1=in1, scale=-1.0, scalar=3e38 if kind else 1e29,
                                                         op0=ALU.add, op1=ALU.min,
                                                         accum_out=nm[:, kind, piece:piece + 1])
                    if last is None:
                        chain(ins)
                    else:
                        ins.then_inc(last, 1)

                def least(kind, n):
                    nc.vector.tensor_reduce(nm[:, kind, 3:4], nm[:, kind, 0:n], AX.X, ALU.min).then_inc(max_ready, 1)

                def read(group):
                    dve.wait_ge(scores_mm, 6 * i + group + 1)
                    bank = ps_s[:, group % 2, :]
                    if group in (SEL0, SEL1):
                        cols = slice(CW * group, CW * (group + 1))
                        nc.vector.tensor_tensor(s_sel[:, cols], bank, b_nsa[:, cols], ALU.add).then_inc(scored, 1)
                    elif group == WIN0:
                        lowest(2, 0, s_win[:, 0:WINDOW], bank, b_win[:, 0:WINDOW], scored)
                    elif group == FEW:
                        dve.wait_ge(scored, 6 * i + 2 + WIN0 + 1)
                        c0 = CMP_BLOCK - 1
                        lowest(0, 3, s_cmp[:], bank[:, F_CMP:F_CMP + CMPS], b_nsa[:, c0:c0 + CMP_STRIDE * (CMPS - 1) + 1:CMP_STRIDE])
                        nc.vector.nop().then_inc(max_ready, 1)
                        lowest(2, 1, s_win[:, WINDOW:], bank[:, F_WIN:F_WIN + DEC_T], b_win[:, WINDOW:])
                        least(2, 2)
                        lowest(3, 2, s_dif[:, PAST:], bank[:, F_DIF:F_DIF + DEC_T], b_dif[:, PAST:])
                        nc.vector.tensor_tensor(s_sel[:, PAST:], bank[:, F_SEL:F_SEL + DEC_T], b_nsa[:, PAST:NCOL],
                                                ALU.add).then_inc(scored, 1)
                    else:
                        k = group - DIF0
                        cols = slice(CW * k, CW * (k + 1))
                        lowest(3, k, s_dif[:, cols], bank, b_dif[:, cols], scored)

                def inverse(kind):
                    chain(nc.vector.tensor_scalar(rr[:, kind:kind + 1], rs[:, kind:kind + 1], TINY, None, ALU.max))
                    chain(nc.vector.reciprocal(rr[:, kind:kind + 1], rr[:, kind:kind + 1]))

                dve.wait_ge(q_in, 48 * i + 48)
                for gp in range(2):
                    ins = nc.vector.tensor_copy(qp[:, 512 * gp:512 * (gp + 1)].rearrange("p (h g e) -> p h g e", h=HPG, g=2),
                                                qn[:, 512 * gp:512 * (gp + 1)].rearrange("p (g h e) -> p h g e", g=2, h=HPG))
                ins.then_inc(q_laid, 1)
                dve.wait_ge(q_turned, i + 1)
                for gp in range(2):
                    for g2 in range(2):
                        half, g = slice(DK * g2, DK * (g2 + 1)), 2 * gp + g2
                        nc.vector.tensor_copy(
                            qb[half, gp, :, 16 * g:16 * (g + 1)].rearrange("p b (h t) -> p h b t", t=DEC_T),
                            ps_n[half, Q_AT + 32 * gp:Q_AT + 32 * (gp + 1)].rearrange("p (h b t) -> p h b t", h=HPG, t=DEC_T))
                for m in range(2):
                    half = slice(DD * m, DD * (m + 1))
                    base = qdb[half, 0, 0, 32 * m:32 * m + 1]
                    out = bass.AP(tensor=base.tensor, offset=base.offset,
                                  ap=[list(base.ap[0]), [2 * ROWS + DEC_T, DHEADS], [ROWS, 2], [1, DEC_T]])
                    ins = nc.vector.tensor_copy(out, ps_n[half, Q_AT + 64:Q_AT + 128].rearrange("p (h b t) -> p h b t", h=DHEADS, t=DEC_T))
                ins.then_inc(q_ready, 1)

                for j in range(1, N, 2):
                    dve.wait_ge(turned, N * i + j + 1 + TURN_CREDIT)
                    for rows, cols in pieces(j):
                        ins = nc.vector.tensor_copy(slot[rows, j % 3, cols], ps_t[rows, j % 3, cols])
                    ins.then_inc(copied[1], 1)
                    if j in READ_AT:
                        read(READ_AT[j])
                    if j == GROUP_AT:
                        dve.wait_ge(probs, 4 * i + 1)
                        inverse(0)
                        nc.vector.tensor_scalar(gm[:], con[:, C_GROUP:C_GROUP + P], rr[:, 0:1], None, ALU.mult).then_inc(coef_ready, 1)
                    if j == SHARE_AT:
                        dve.wait_ge(pg_mm, i + 1)
                        nc.vector.tensor_copy(pg[:], ps_n[0:CMPS, PG_AT:PG_AT + P]).then_inc(pg_copied, 1)
                    if j == CHOOSE_AT:
                        dve.wait_ge(imp_mm, i + 1)
                        dve.wait_ge(scored, 6 * i + 2 + FEW + 1)
                        free = slice(1, N_SLC - 2)
                        imp = ps_n[:, IMP_AT:IMP_AT + N_SLC]
                        idx = con[:, C_IDX:C_IDX + N_SLC]
                        chain(nc.vector.tensor_reduce(rr[:, 4:5], imp[:, free], AX.X, ALU.min))
                        chain(nc.vector.scalar_tensor_tensor(out=pick[:, 0, free], in0=imp[:, free], scalar=rr[:, 4:5],
                                                             in1=idx[:, free], op0=ALU.is_equal, op1=ALU.mult))
                        chain(nc.vector.tensor_reduce(rr[:, 5:6], pick[:, 0, free], AX.X, ALU.max))
                        chain(nc.vector.tensor_scalar(pick[:, 1, :], idx, rr[:, 5:6], NEG, ALU.is_equal, ALU.mult))
                        view = s_sel[:, 0:PAST].rearrange("p (n e) -> p n e", e=SEL_BLOCK)
                        lowest(1, 0, view, view, pick[:, 1, 0:N_SLC - 1].unsqueeze(2).to_broadcast([P, N_SLC - 1, SEL_BLOCK]))
                        lowest(1, 1, s_sel[:, PAST:], s_sel[:, PAST:], pick[:, 1, N_SLC - 1:N_SLC].to_broadcast([P, DEC_T]))
                        least(1, 2)
                    if j == SCALE_AT:
                        dve.wait_ge(probs, 4 * i + 3)
                        dve.wait_ge(new_in, 112 * i + 112)
                        dve.wait_ge(coef_ready, 5 * i + 1)
                        inverse(1)
                        inverse(2)
                        chain(nc.vector.tensor_tensor(rr[:, 0:3], rr[:, 0:3], gates[:], ALU.mult))
                        for k in range(3):
                            nc.vector.tensor_scalar(cm[:, k, :], ident[:], rr[:, k:k + 1], None,
                                                    ALU.mult).then_inc(coef_ready, 1)
                    if j == SCALE_D_AT:
                        dve.wait_ge(scored, 6 * i + 2 + DIF1 + 1)
                        least(3, 3)
                        dve.wait_ge(probs, 4 * i + 4)
                        inverse(3)
                        chain(nc.vector.tensor_tensor(rr[:, 3:4], rr[:, 3:4], lam[:, 3:4], ALU.mult))
                        nc.vector.tensor_scalar(cd[:], con[:, C_STACK:C_STACK + 64], rr[:, 3:4], None, ALU.mult).then_inc(coef_ready, 1)
                dve.wait_ge(nsa_mm, i + 2)
                chain(nc.vector.tensor_tensor(part[:, 0:KVW], ps_n[:, 0:KVW], con[:, C_NSA:C_NSA + KVW], ALU.mult))
                nc.vector.nop().then_inc(nsa_read, 1)
                dve.wait_ge(o_n_free, i + 1)
                nc.vector.tensor_reduce(o_n[:], part[:, 0:KVW].rearrange("p (g e) -> p e g", e=DK), AX.X, ALU.add).then_inc(nsa_out, 1)
                dve.wait_ge(nsa_out, i + 2)
                dve.wait_ge(diff_mm, i + 2)
                chain(nc.vector.tensor_tensor(part[:], ps_d[:], con[:, C_DIFF:C_DIFF + CW], ALU.mult))
                nc.vector.nop().then_inc(diff_read, 1)
                dve.wait_ge(o_d_free, i + 1)
                chain(nc.vector.tensor_reduce(o_d[:], part[:].rearrange("p (h e) -> p e h", e=DV), AX.X, ALU.add))
                chain(nc.vector.tensor_tensor(part[:, 0:DV], o_d[:], o_d[:], ALU.mult))
                nc.vector.tensor_reduce(rr[:, 6:7], part[:, 0:DV], AX.X, ALU.add).then_inc(o_sq, 1)
                dve.wait_ge(o_sq, 2 * i + 1)
                nc.vector.tensor_scalar(rr[:, 6:7], rr[:, 6:7], 1.0 / DV, EPS, ALU.mult, ALU.add).then_inc(o_sq, 1)
                dve.wait_ge(o_root, i + 1)
                chain(nc.vector.reciprocal(rr[:, 7:8], rr[:, 7:8]))
                nc.vector.scalar_tensor_tensor(out=o_d[:], in0=o_d[:], scalar=rr[:, 7:8], in1=gain[:],
                                               op0=ALU.mult, op1=ALU.mult).then_inc(diff_out, 1)
                assert chain.n == CHAIN, chain.n


HALF = D_FF // 2
FT = HALF // P
WS = 2048
PAIR = TOKENS // 2


def finish(nc, d):
    with ExitStack() as ctx:
        s = Space(nc, ctx, "fi")
        h = s.sb("h", [P, TT, D_MODEL])
        th = s.sb("th", [P, KT, TOKENS], F32R)
        tl = s.sb("tl", [P, KT, TOKENS], F32R)
        fh = s.sb("fh", [P, FT, TOKENS], F32R)
        fl = s.sb("fl", [P, FT, TOKENS], F32R)
        yt = s.sb("yt", [P, KT, TOKENS])
        w = s.sb("w", [P, 2, WS])
        wh = s.sb("wh", [P, 2, WS], F32R)
        wl = s.sb("wl", [P, 2, WS], F32R)
        buf = s.sb("buf", [P, 2, 4, CW])
        relu = buf[:, 0, 0:2, :].rearrange("p a b -> p (a b)")[:, 0:TOKENS]
        sqr = buf[:, 1, 0:2, :].rearrange("p a b -> p (a b)")[:, 0:TOKENS]
        ident = s.sb("ident", [P, P])
        gain = s.sb("gain", [P, D_MODEL])
        ssum = s.sb("ssum", [P, TT])
        rstd = s.sb("rstd", [P, TT])
        ps = s.ps("ps", [P, 8, CW])

        h_in, consts_in = s.sem("h_in"), s.sem("consts_in")
        o_in = [s.sem(f"o_in{k}") for k in range(2)]
        w_in = [s.sem(f"w_in{k}") for k in range(2)]
        w_hi, w_split = s.sem("w_hi"), s.sem("w_split")
        merged, turned, t_hi, t_lo = s.sem("merged"), s.sem("turned"), s.sem("t_hi"), s.sem("t_lo")
        o_done, up_done, down_done, h_added = s.sem("o_done"), s.sem("up_done"), s.sem("down_done"), s.sem("h_added")
        h_sq, h_rstd = s.sem("h_sq"), s.sem("h_rstd")
        relued, f_hi, f_lo, y_added = (s.sem(n) for n in ("relued", "f_hi", "f_lo", "y_added"))
        f_made = [s.sem(f"f_made{f}") for f in range(2)]
        y_turned, y_ready, y_out = s.sem("y_turned"), s.sem("y_ready"), s.sem("y_out")
        step_sem, zeroed = s.sem("dve_step"), s.sem("zeroed")
        block = ctx.enter_context(nc.Block())

        rows = lambda t: P if t < QT else N_DEC
        units = [(t, k) for t in range(TT) for k in range(2)]
        NO = 4
        NU = HALF // 256
        w_o = d["w_o"].rearrange("(k p) n -> p k n", p=P)
        w_up = d["w_up"].rearrange("(k p) n -> p k n", p=P)
        w_down = d["w_down"].rearrange("(k p) n -> p k n", p=P)

        def piece(n):
            if n < NO:
                return w_o[:, :, 256 * n:256 * (n + 1)], KT
            half, c = divmod(n - NO, 2 * NU)
            if c < NU:
                return w_up[:, :, HALF * half + 256 * c:HALF * half + 256 * (c + 1)], KT
            return w_down[:, FT * half:FT * (half + 1), P * (c - NU):P * (c - NU + 1)], FT

        N_ALL = NO + 4 * NU

        @block.sync
        def _(sp):
            def load(n):
                if n >= 2:
                    sp.wait_ge(w_split, n - 1)
                src, k = piece(n)
                sp.dma_start(w[:, n % 2, :].rearrange("p (k c) -> p k c", k=k), src).then_inc(w_in[n % 2], 16)

            for u, (t, k) in enumerate(units):
                if u >= 2:
                    sp.wait_ge(turned, u - 1)
                cols = slice(CW * k, CW * (k + 1))
                for j, name in enumerate(("ga", "oa", "gb", "ob")):
                    sp.dma_start(buf[0:rows(t), u % 2, j, :], d[name][P * t:P * t + rows(t), cols]).then_inc(o_in[u % 2], 16)
                if u == 1:
                    sp.dma_start(ident[:], d["ident"]).then_inc(consts_in, 16)
                    sp.dma_start(gain[:], spread(d["mlp_norm"], P)).then_inc(consts_in, 16)
                    load(0)
                    load(1)
            for t in range(TT):
                src = d["x_prompt"][P * t:P * (t + 1), :] if t < QT else d["x_sample"]
                sp.dma_start(h[0:rows(t), t, :], src).then_inc(h_in, 16)
            for n in range(2, N_ALL):
                load(n)
            for t in range(TT):
                sp.wait_ge(y_ready, t + 1)
                dst = d["y_prompt"][P * t:P * (t + 1), :] if t < QT else d["y_sample"]
                sp.dma_start(dst, h[0:rows(t), t, :]).then_inc(y_out, 16)
            sp.wait_ge(y_out, 16 * TT)

        @block.scalar
        def _(act):
            def split(n):
                act.wait_ge(w_in[n % 2], 16 * (n // 2 + 1))
                if n >= 2:
                    act.wait_ge(o_done, TT * (n - 1))
                nc.scalar.activation(wh[:, n % 2, :], w[:, n % 2, :], ACT.Copy).then_inc(w_hi, 1)

            def split_ahead(u, n, done, level):
                act.wait_ge(w_in[u], 8 * n + (16 if u == 0 else 8))
                act.wait_ge(done, level)
                nc.scalar.activation(wh[:, u, :], w[:, u, :], ACT.Copy).then_inc(w_hi, 1)

            def high_parts(u):
                t, k = units[u % len(units)]
                act.wait_ge(turned, u + 1)
                nc.scalar.activation(th[:, 4 * k:4 * k + 4, P * t:P * t + rows(t)],
                                     ps[:, 6 + u % 2, 0:4 * rows(t)].rearrange("p (k c) -> p k c", k=4),
                                     ACT.Copy).then_inc(t_hi, 1)

            split(0)
            split(1)
            for u in range(len(units)):
                high_parts(u)
            split(2)
            split(3)
            for t in range(TT):
                act.wait_ge(h_added, TT * (NO - 1) + t + 1)
                if t == 0:
                    act.wait_ge(zeroed, 1)
                else:
                    act.wait_ge(h_sq, t)
                nc.scalar.activation(buf[0:rows(t), 0, 0:2, :].rearrange("p a b -> p (a b)"), h[0:rows(t), t, :],
                                     ACT.Square, accum_out=ssum[0:rows(t), t:t + 1]).then_inc(h_sq, 1)
            act.wait_ge(h_rstd, 1)
            nc.scalar.activation(rstd[:], ssum[:], ACT.Sqrt).then_inc(h_sq, 1)
            for u in range(len(units)):
                high_parts(len(units) + u)
            split(4)
            split(5)
            for half in range(2):
                first = NO + 2 * NU * half
                with act.Fori(0, NU // 2) as i:
                    for u in range(2):
                        at = NU * half + 2 * i + u
                        for f in range(2):
                            act.wait_ge(up_done, 2 * at + f + 1)
                            nc.scalar.activation(relu.rearrange("p (a c) -> p a c", a=2), ps[:, 2 * f:2 * f + 2, 0:PAIR],
                                                 ACT.Relu).then_inc(relued, 1)
                            act.wait_ge(f_made[f], at + 2)
                            nc.scalar.activation(fh[:, bass.ds(4 * i + 2 * u + f, 1), :].rearrange("p a c -> p (a c)"),
                                                 sqr, ACT.Copy).then_inc(f_hi, 1)
                        split_ahead(u, first + 2 * i + u + 2, up_done, 2 * at + 2)
                last = 1 if half else 0
                with act.Fori(0, NU // 2 - last) as i:
                    for u in range(2):
                        split_ahead(u, first + NU + 2 * i + u + 2, down_done, NU * half + 2 * i + u + 1)

        @block.vector
        def _(dve):
            step = Chain(dve, step_sem)

            def split(n):
                dve.wait_ge(w_hi, n + 1)
                nc.vector.tensor_tensor(wl[:, n % 2, :], w[:, n % 2, :], wh[:, n % 2, :].bitcast(F32),
                                        ALU.subtract).then_inc(w_split, 1)

            def low_parts(u):
                t, k = units[u % len(units)]
                dve.wait_ge(t_hi, u + 1)
                view = (slice(None), slice(4 * k, 4 * k + 4), slice(P * t, P * t + rows(t)))
                nc.vector.tensor_tensor(tl[view], ps[:, 6 + u % 2, 0:4 * rows(t)].rearrange("p (k c) -> p k c", k=4),
                                        th[view].bitcast(F32), ALU.subtract).then_inc(t_lo, 1)

            nc.vector.memset(ssum[:], 1.0).then_inc(zeroed, 1)
            nc.vector.memset(yt[:], 0.0).then_inc(zeroed, 1)
            nc.vector.nop().then_inc(f_lo, 1)
            for f in range(2):
                nc.vector.nop().then_inc(f_made[f], 1)
                nc.vector.nop().then_inc(y_added, 1)
            for u, (t, k) in enumerate(units):
                b = buf[0:rows(t), u % 2]
                dve.wait_ge(o_in[u % 2], 64 * (u // 2 + 1))
                nc.vector.tensor_tensor(b[:, 0, :], b[:, 0, :], b[:, 1, :], ALU.mult)
                step(nc.vector.tensor_tensor(b[:, 2, :], b[:, 2, :], b[:, 3, :], ALU.mult))
                nc.vector.tensor_tensor(b[:, 0, :], b[:, 0, :], b[:, 2, :], ALU.add).then_inc(merged, 1)
                if u == 1:
                    split(0)
                    split(1)
                if u >= 1:
                    low_parts(u - 1)
            low_parts(len(units) - 1)
            dve.wait_ge(h_in, 16 * TT)
            for n in range(NO):
                for t in range(TT):
                    dve.wait_ge(o_done, TT * n + t + 1)
                    hv = h[0:rows(t), t, 256 * n:256 * (n + 1)]
                    nc.vector.tensor_tensor(hv, ps[0:rows(t), t, 0:256], hv, ALU.add).then_inc(h_added, 1)
                if n + 2 < NO:
                    split(n + 2)
            dve.wait_ge(h_sq, TT)
            nc.vector.tensor_scalar(ssum[:], ssum[:], 1.0 / D_MODEL, EPS, ALU.mult, ALU.add).then_inc(h_rstd, 1)
            dve.wait_ge(h_sq, TT + 1)
            step(nc.vector.reciprocal(rstd[:], rstd[:]))
            for u, (t, k) in enumerate(units):
                n = len(units) + u
                if u >= 2:
                    dve.wait_ge(turned, n - 1)
                nc.vector.scalar_tensor_tensor(out=buf[0:rows(t), u % 2, 0, :], in0=h[0:rows(t), t, CW * k:CW * (k + 1)],
                                               scalar=rstd[0:rows(t), t:t + 1], in1=gain[0:rows(t), CW * k:CW * (k + 1)],
                                               op0=ALU.mult, op1=ALU.mult).then_inc(merged, 1)
                if u >= 1:
                    low_parts(n - 1)
            low_parts(2 * len(units) - 1)
            split(4)
            split(5)

            def split_dyn(u, n):
                dve.wait_ge(w_hi, n + 1)
                nc.vector.tensor_tensor(wl[:, u, :], w[:, u, :], wh[:, u, :].bitcast(F32), ALU.subtract).then_inc(w_split, 1)

            for half in range(2):
                first = NO + 2 * NU * half
                with dve.Fori(0, NU // 2) as i:
                    for u in range(2):
                        for f in range(2):
                            at = 2 * (NU * half + 2 * i + u) + f
                            dve.wait_ge(relued, at + 1)
                            dve.wait_ge(f_lo, at + 1)
                            nc.vector.scalar_tensor_tensor(out=sqr.rearrange("p (a c) -> p a c", a=2),
                                                           in0=ps[:, 2 * f:2 * f + 2, 0:PAIR], scalar=0.0,
                                                           in1=relu.rearrange("p (a c) -> p a c", a=2),
                                                           op0=ALU.max, op1=ALU.mult).then_inc(f_made[f], 1)
                            dve.wait_ge(f_hi, at + 1)
                            ft = bass.ds(4 * i + 2 * u + f, 1)
                            nc.vector.tensor_tensor(fl[:, ft, :].rearrange("p a c -> p (a c)"), sqr,
                                                    fh[:, ft, :].rearrange("p a c -> p (a c)").bitcast(F32),
                                                    ALU.subtract).then_inc(f_lo, 1)
                        split_dyn(u, first + 2 * i + u + 2)

                def add_y(i, u):
                    dve.wait_ge(down_done, NU * half + 2 * i + u + 1)
                    y = yt[:, bass.ds(2 * i + u, 1), :].rearrange("p b (a c) -> p (b a) c", a=2)
                    nc.vector.tensor_tensor(y, ps[:, 4 + 2 * u:6 + 2 * u, 0:PAIR], y, ALU.add).then_inc(y_added, 1)

                last = 1 if half else 0
                with dve.Fori(0, NU // 2 - last) as i:
                    for u in range(2):
                        add_y(i, u)
                        split_dyn(u, first + NU + 2 * i + u + 2)
                if half:
                    for u in range(2):
                        add_y(NU // 2 - 1, u)
            for t in range(TT):
                for k in range(2):
                    dve.wait_ge(y_turned, 2 * t + k + 1)
                    hv = h[0:rows(t), t, CW * k:CW * (k + 1)]
                    ins = nc.vector.tensor_tensor(hv, ps[0:rows(t), k + 2 * (t % 2), :], hv, ALU.add)
                    if k == 0:
                        ins.then_inc(step_sem, 1)
                ins.then_inc(y_ready, 1)

        @block.tensor
        def _(pe):
            pe.wait_ge(consts_in, 32)

            def turn(u):
                t, k = units[u % len(units)]
                pe.wait_ge(merged, u + 1)
                if u >= 2:
                    pe.wait_ge(t_lo, u - 1)
                n = rows(t)
                for j in range(4):
                    ins = pe.transpose(ps[:, 6 + u % 2, n * j:n * (j + 1)], buf[0:n, u % 2, 0, P * j:P * (j + 1)],
                                       ident[0:n, 0:n])
                ins.then_inc(turned, 1)

            for u in range(len(units)):
                turn(u)
            pe.wait_ge(t_lo, len(units))
            for n in range(NO):
                pe.wait_ge(w_split, n + 1)
                hi = wh[:, n % 2, :].rearrange("p (k c) -> p k c", k=KT)
                lo = wl[:, n % 2, :].rearrange("p (k c) -> p k c", k=KT)
                for t in range(TT):
                    if n:
                        pe.wait_ge(h_added, TT * (n - 1) + t + 1)
                    tok = slice(P * t, P * t + rows(t))
                    out = ps[0:rows(t), t, 0:256]
                    for k in range(KT):
                        pe.matmul(out, th[:, k, tok], hi[:, k, :], start=k == 0, stop=False)
                        pe.matmul(out, th[:, k, tok], lo[:, k, :], start=False, stop=False)
                        ins = pe.matmul(out, tl[:, k, tok], hi[:, k, :], start=False, stop=k == KT - 1)
                    ins.then_inc(o_done, 1)
            for u in range(len(units)):
                turn(len(units) + u)
            pe.wait_ge(t_lo, 2 * len(units))

            def product(out, kts, hi, lo, a_hi, a_lo):
                for k in range(kts):
                    for b in range(2):
                        tok = slice(PAIR * b, PAIR * (b + 1))
                        o = out[:, b, 0:PAIR]
                        pe.matmul(o, hi[:, k, :], a_hi[:, k, tok], start=k == 0, stop=False)
                        pe.matmul(o, hi[:, k, :], a_lo[:, k, tok], start=False, stop=False)
                        ins = pe.matmul(o, lo[:, k, :], a_hi[:, k, tok], start=False, stop=k == kts - 1)
                return ins

            for half in range(2):
                first = NO + 2 * NU * half
                with pe.Fori(0, NU // 2) as i:
                    for u in range(2):
                        at = NU * half + 2 * i + u
                        pe.wait_ge(w_split, first + 2 * i + u + 1)
                        hi = wh[:, u, :].rearrange("p (k c) -> p k c", k=KT)
                        lo = wl[:, u, :].rearrange("p (k c) -> p k c", k=KT)
                        for f in range(2):
                            pe.wait_ge(f_made[f], at + 1)
                            col = slice(P * f, P * (f + 1))
                            product(ps[:, 2 * f:2 * f + 2, :], KT, hi[:, :, col], lo[:, :, col], th, tl).then_inc(up_done, 1)
                pe.wait_ge(f_lo, 2 * NU * (half + 1) + 1)
                with pe.Fori(0, NU // 2) as i:
                    for u in range(2):
                        at = NU * half + 2 * i + u
                        pe.wait_ge(w_split, first + NU + 2 * i + u + 1)
                        pe.wait_ge(y_added, at + 1)
                        hi = wh[:, u, :].rearrange("p (k c) -> p k c", k=FT)
                        lo = wl[:, u, :].rearrange("p (k c) -> p k c", k=FT)
                        product(ps[:, 4 + 2 * u:6 + 2 * u, :], FT, hi, lo, fh, fl).then_inc(down_done, 1)
            pe.wait_ge(y_added, 2 * NU + 2)
            for t in range(TT):
                if t >= 2:
                    pe.wait_ge(y_ready, t - 1)
                for k in range(2):
                    for j in range(4):
                        ins = pe.transpose(ps[0:rows(t), k + 2 * (t % 2), P * j:P * (j + 1)],
                                           yt[:, 4 * k + j, P * t:P * t + rows(t)], ident[:])
                    ins.then_inc(y_turned, 1)


def build(nc, d):
    project(nc, d)
    compress(nc, d)
    prompt_attention(nc, d)
    decode_attention(nc, d)
    finish(nc, d)


VIEWS = {
    "x_prompt": ("x_prompt", (SEQ, D_MODEL)), "x_sample": ("x_sample", (N_DEC, D_MODEL)),
    "cache_nsa_kv": ("cache_nsa", (-1, PAGE, 4 * KVW)), "cache_diff_kv": ("cache_diff", (-1, PAGE, 2 * D_MODEL)),
    "cache_nsa_win": ("cache_win", (DEC_B, WINDOW, 2 * KVW)), "page_table": ("page_table", (1, DEC_B * N_PAGES)),
    "rel_bias_table": ("rel_bias_table", (BUCKETS, HEADS + DHEADS)),
    "w_in": ("w_in", (D_MODEL, N_IN)), "w_o": ("w_o", (D_MODEL, D_MODEL)),
    "w_up": ("w_up", (D_MODEL, D_FF)), "w_down": ("w_down", (D_FF, D_MODEL)),
    **{f"cmp_pe_{x}": (f"cmp_pe_{x}", (CMP_BLOCK, DK)) for x in "kv"},
    **{f"cmp_w1_{x}": (f"cmp_w1_{x}", (CMP_BLOCK * DK, CMP_HID)) for x in "kv"},
    **{f"cmp_w2_{x}": (f"cmp_w2_{x}", (CMP_HID, DK)) for x in "kv"},
    **{x: (x, (-1,)) for x in ("attn_norm", "nsa_q_gain", "nsa_k_gain", "diff_q_gain", "diff_k_gain", "lambda_q1",
                               "lambda_k1", "lambda_q2", "lambda_k2", "diff_subln", "mlp_norm")},
}
SCRATCH = {
    **{x: (TOKENS, D_MODEL) for x in ("q", "qd", "ga", "gb", "oa", "ob")}, "g": (TOKENS, 3 * HEADS),
    "toep": (HEADS + DHEADS, P, STRIP), "decb": (HEADS + DHEADS, DEC_T, DECW),
    "kc_s": (DEC_B * PAST // CMP_STRIDE, KVW), "vc_s": (DEC_B * PAST // CMP_STRIDE, KVW), "kc_p": (CHP, KVW), "vc_p": (CHP, KVW),
}
OUTPUTS = (
    ("y_prompt", (SEQ, D_MODEL), (1, SEQ, D_MODEL)), ("y_sample", (N_DEC, D_MODEL), (DEC_B, DEC_T, D_MODEL)),
    ("nsa_p", (SEQ, 4 * KVW), (1, 1, SEQ, 4, GROUPS, DK)), ("diff_p", (SEQ, 2 * D_MODEL), (1, 1, SEQ, 2, DHEADS, DV)),
    ("win_p", (SEQ, 2 * KVW), (1, 1, SEQ, 2, GROUPS, DK)),
    ("nsa_s", (N_DEC, 4 * KVW), (1, DEC_B, DEC_T, 4, GROUPS, DK)), ("diff_s", (N_DEC, 2 * D_MODEL), (1, DEC_B, DEC_T, 2, DHEADS, DV)),
    ("win_s", (DEC_B, WINDOW, 2 * KVW), (1, DEC_B, WINDOW, 2, GROUPS, DK)),
)


def kernel(**inputs):
    import concourse.bacc as bacc
    from concourse.bass_utils import run_bass_kernel_spmd

    nc = bacc.Bacc("TRN2", target_bir_lowering=False, num_devices=1)
    arrays, d = {}, {}

    def give(name, a):
        arrays[f"in_{name}"] = np.ascontiguousarray(a)
        d[name] = nc.dram_tensor(f"in_{name}", a.shape, mybir.dt.from_np(a.dtype), kind="ExternalInput").ap()

    for source, (name, shape) in VIEWS.items():
        give(name, np.asarray(inputs[source]).reshape(shape))
    for name, a in (("ident", np.eye(P, dtype=np.float32)), ("bucket_hot", bucket_hot()),
                    ("decode_constants", decode_constants()), ("select_weights", select_weights())):
        give(name, a)
    for name, shape in SCRATCH.items():
        d[name] = nc.dram_tensor(f"scratch_{name}", shape, F32, kind="Internal").ap()
    for name, shape, _ in OUTPUTS:
        d[name] = nc.dram_tensor(f"out_{name}", shape, F32, kind="ExternalOutput").ap()
    build(nc, d)
    result = run_bass_kernel_spmd(nc, [arrays], core_ids=[0]).results[0]
    return tuple(result[f"out_{name}"].reshape(shape) for name, _, shape in OUTPUTS)
```

```python
import math
from contextlib import ExitStack

import numpy as np
import concourse.bass as bass
from concourse import mybir
from concourse.alu_op_type import AluOpType as ALU

F32 = mybir.dt.float32
F32R = mybir.dt.float32r
I32 = mybir.dt.int32
ACT = mybir.ActivationFunctionType
AX = mybir.AxisListType

P = 128
D_MODEL = 1024
SEQ = 512
DEC_B, DEC_T = 8, 4
N_DEC = DEC_B * DEC_T
TOKENS = SEQ + N_DEC
PAST = 1024
PAGE = 128
N_PAGES = PAST // PAGE
HEADS, GROUPS, DK = 16, 4, 64
HPG = HEADS // GROUPS
KVW = GROUPS * DK
CMP_BLOCK, CMP_STRIDE, CMP_HID = 32, 16, 256
SEL_BLOCK = 64
N_SLC = -(-(PAST + DEC_T) // SEL_BLOCK)
WINDOW = 512
DHEADS, DD, DV = 8, 64, 128
D_FF = 4 * D_MODEL
BUCKETS, MAX_DIST = 32, 128
EPS = 1e-6
NEG = -1e30
TINY = 1e-30
SCALE = DK ** -0.5
N_IN = 7728

KT = D_MODEL // P
QT = SEQ // P
TT = QT + 1
CW = 512
BROW = 1556
BTOP = PAST + DEC_T - 1
STRIP = 912
DECW = 1040


class Chain:

    def __init__(self, eng, sem, base=0):
        self.eng, self.sem, self.base, self.n = eng, sem, base, 0

    def __call__(self, ins):
        self.n += 1
        ins.then_inc(self.sem, 1)
        self.eng.wait_ge(self.sem, self.base + self.n)


class Space:

    def __init__(self, nc, ctx, stage):
        self.nc, self.ctx, self.stage, self.sems = nc, ctx, stage, []
        ctx.callback(self.clear)

    def sb(self, name, shape, dt=F32):
        return self.ctx.enter_context(self.nc.sbuf_tensor(f"{self.stage}_{name}", shape, dt))

    def ps(self, name, shape):
        return self.ctx.enter_context(self.nc.psum_tensor(f"{self.stage}_{name}", shape, F32))

    def sem(self, name):
        self.sems.append(self.nc.alloc_semaphore(f"{self.stage}_{name}"))
        return self.sems[-1]

    def clear(self):
        self.nc.clear_and_free_semaphores(self.sems)
        self.nc.all_engine_barrier()


def spread(ap, n):
    return bass.AP(tensor=ap.tensor, offset=ap.offset, ap=[[0, n]] + [list(x) for x in ap.ap][-1:])


Q_N, KV_N, G_N = 0, 1024, 2560
Q_D, K_D, V_D, GA, GB = 2608, 3632, 4656, 5680, 6704
CHUNKS = (
    [(Q_N + CW * j, "query", "q", CW * j) for j in range(2)]
    + [(Q_D + CW * j, "query", "qd", CW * j) for j in range(2)]
    + [(K_D + CW * j, "key", "diff", CW * j) for j in range(2)]
    + [(KV_N + 2 * CW, "key_value", "win", 0), (KV_N + CW, "key_value", "nsa", CW), (KV_N, "plain", "nsa", 0)]
    + [(V_D + CW * j, "plain", "diff", 1024 + CW * j) for j in range(2)]
    + [(GA + CW * j, "gate", "ga", CW * j) for j in range(2)]
    + [(GB + CW * j, "gate", "gb", CW * j) for j in range(2)]
)
NC = len(CHUNKS)


def project(nc, d):
    with ExitStack() as ctx:
        s = Space(nc, ctx, "pj")
        x = s.sb("x", [P, TT, D_MODEL])
        xh = s.sb("xh", [P, KT, SEQ], F32R)
        xl = s.sb("xl", [P, KT, SEQ], F32R)
        xf = s.sb("xf", [P, 2, CW])
        xsam = s.sb("xsam", [P, KT, N_DEC])
        ident = s.sb("ident", [P, P])
        gain = s.sb("gain", [P, KT])
        ssum = s.sb("ssum", [P, TT])
        rstd = s.sb("rstd", [P, TT])
        w = s.sb("w", [P, 2, KT, CW])
        wh = s.sb("wh", [P, 2, KT, CW], F32R)
        wl = s.sb("wl", [P, 2, KT, CW], F32R)
        wg = s.sb("wg", [P, KT, 48])
        wgh = s.sb("wgh", [P, KT, 48], F32R)
        wgl = s.sb("wgl", [P, KT, 48], F32R)
        heads_gain = s.sb("heads_gain", [P, 4, DK])
        sq = s.sb("sq", [P, 2, CW])
        stat = s.sb("stat", [P, 2, 3, 8])
        y = s.sb("y", [P, 3, CW])
        tab = s.sb("tab", [BUCKETS + 1, 24])
        hot = s.sb("hot", [BUCKETS + 1, BROW])
        brow = s.sb("brow", [24, BROW])
        ps = s.ps("ps", [P, TT, CW])
        pt = s.ps("pt", [P, 2, CW])

        ssum_set = s.sem("ssum_set")
        gains_in, table_in, heads_in = s.sem("gains_in"), s.sem("table_in"), s.sem("heads_in")
        x_in = [s.sem(f"x_in{t}") for t in range(TT)]
        x_sq, x_rstd, x_scaled = s.sem("x_sq"), s.sem("x_rstd"), s.sem("x_scaled")
        x_turned, x_copied, x_hi, x_ready = s.sem("x_turned"), s.sem("x_copied"), s.sem("x_hi"), s.sem("x_ready")
        mask_row, bias_mm, bias_row, bias_out = s.sem("mask_row"), s.sem("bias_mm"), s.sem("bias_row"), s.sem("bias_out")
        w_in = [s.sem(f"w_in{u}") for u in range(2)]
        wg_in = s.sem("wg_in")
        w_hi, w_split = s.sem("w_hi"), s.sem("w_split")
        first_hi, first_split, gates_split = s.sem("first_hi"), s.sem("first_split"), s.sem("gates_split")
        tile_done = s.sem("tile_done")
        bank_free = [s.sem(f"bank_free{t}") for t in range(TT)]
        squared, summed, rooted = s.sem("squared"), s.sem("summed"), s.sem("rooted")
        y_ready = s.sem("y_ready")
        stored = [s.sem(f"stored{k}") for k in range(3)]
        dve_step, act_step = s.sem("dve_step"), s.sem("act_step")
        block = ctx.enter_context(nc.Block())

        rows = lambda t: P if t < QT else N_DEC
        units = [(c, t) for c in range(NC + 1) for t in (QT, *range(QT))]

        def dests(c, t):
            name, at = (CHUNKS[c][2], CHUNKS[c][3]) if c < NC else ("g", 0)
            k = (c * TT + (t + 1) % TT) % 3
            if c == NC:
                n = rows(t)
                return [(d["g"][t * P:t * P + n, :], y[0:n, k, 0:48])]
            if t < QT:
                out = d[name if name in ("q", "qd", "ga", "gb") else name + "_p"]
                return [(out[t * P:(t + 1) * P, at:at + CW], y[:, k, :])]
            if name == "win":
                return [(d["win_s"][:, WINDOW - DEC_T:WINDOW, P * j:P * (j + 1)], y[32 * j:32 * j + 32, k, 0:P])
                        for j in range(4)]
            out = d[name][SEQ:TOKENS, :] if name in ("q", "qd", "ga", "gb") else d[name + "_s"]
            return [(out[:, at + P * j:at + P * (j + 1)], y[32 * j:32 * j + 32, k, 0:P]) for j in range(4)]

        stores = [0] * 3
        store_level = []
        for n, (c, t) in enumerate(units):
            stores[n % 3] += 16 * len(dests(c, t))
            store_level.append(stores[n % 3])

        @block.sync
        def _(sp):
            for t in range(TT):
                src = d["x_prompt"][t * P:(t + 1) * P, :] if t < QT else d["x_sample"]
                sp.dma_start(x[0:rows(t), t, :], src).then_inc(x_in[t], 16)
            sp.dma_start(ident[:], d["ident"]).then_inc(gains_in, 16)
            with nc.allow_non_contiguous_dma("a column of gains"):
                sp.dma_start(gain[:], d["attn_norm"].rearrange("(k p) -> p k", p=P)).then_inc(gains_in, 16)
            sp.dma_start(tab[0:BUCKETS, :], d["rel_bias_table"]).then_inc(table_in, 16)
            sp.dma_start(hot[:], d["bucket_hot"]).then_inc(table_in, 16)
            w_view = d["w_in"].rearrange("(k p) n -> p k n", p=P)
            for c in range(2):
                sp.dma_start(w[:, c, :, :], w_view[:, :, CHUNKS[c][0]:CHUNKS[c][0] + CW]).then_inc(w_in[c], 16)
            for j, name in enumerate(("nsa_q_gain", "diff_q_gain", "diff_k_gain", "nsa_k_gain")):
                sp.dma_start(heads_gain[:, j, :], spread(d[name], P)).then_inc(heads_in, 16)
            sp.dma_start(wg[:], w_view[:, :, G_N:G_N + 48]).then_inc(wg_in, 16)
            sp.wait_ge(bias_row, 4)
            for h in range(24):
                sp.dma_start(d["toep"][h:h + 1, :, :],
                             bass.AP(tensor=brow, offset=h * BROW + BTOP - 384, ap=[[BROW, 1], [-1, P], [1, STRIP]])
                             ).then_inc(bias_out, 16)
            sp.dma_start(d["decb"], bass.AP(tensor=brow, offset=DEC_T - 1, ap=[[BROW, 24], [-1, DEC_T], [1, DECW]])
                         ).then_inc(bias_out, 16)
            n_normed = 0
            for n, (c, t) in enumerate(units):
                if t == QT and c + 2 < NC:
                    sp.wait_ge(tile_done, TT * c + 1)
                    at = CHUNKS[c + 2][0]
                    sp.dma_start(w[:, c % 2, :, :], w_view[:, :, at:at + CW]).then_inc(w_in[c % 2], 16)
                if c < NC and CHUNKS[c][1] in ("query", "key", "key_value"):
                    n_normed += 1
                    sp.wait_ge(y_ready, n_normed)
                else:
                    sp.wait_ge(bank_free[t], c + 2)
                for dst, src in dests(c, t):
                    sp.dma_start(dst, src).then_inc(stored[n % 3], 16)
            sp.wait_ge(bias_out, 16 * 25)
            for k in range(3):
                sp.wait_ge(stored[k], stores[k])

        def x_tile(sc, t):
            return x[0:rows(t), t, :]

        @block.scalar
        def _(act):
            act.wait_ge(ssum_set, 1)
            for t in range(TT):
                act.wait_ge(x_in[t], 16)
                if t:
                    act.wait_ge(x_sq, t)
                nc.scalar.activation(xf[0:rows(t), :, :].rearrange("p a b -> p (a b)"), x[0:rows(t), t, :], ACT.Square,
                                     accum_out=ssum[0:rows(t), t:t + 1]).then_inc(x_sq, 1)
            act.wait_ge(x_rstd, 1)
            nc.scalar.activation(rstd[:], ssum[:], ACT.Sqrt).then_inc(x_sq, 1)
            act.wait_ge(x_rstd, 2)
            for t in range(2, TT):
                nc.scalar.activation(x[0:rows(t), t, :], x[0:rows(t), t, :], ACT.Copy,
                                     scale=rstd[0:rows(t), t:t + 1]).then_inc(x_scaled, 1)
            act.wait_ge(w_in[0], 16)
            nc.scalar.activation(wh[:, 0, :, :], w[:, 0, :, :], ACT.Copy).then_inc(first_hi, 1)
            for k in range(KT):
                act.wait_ge(x_copied, k + 1)
                nc.scalar.activation(xh[:, k, :], xf[:, k % 2, :], ACT.Copy).then_inc(x_hi, 1)

            def split(c):
                act.wait_ge(w_in[c % 2], 16 * (c // 2 + 1))
                if c >= 2:
                    act.wait_ge(tile_done, TT * (c - 1))
                nc.scalar.activation(wh[:, c % 2, :, :], w[:, c % 2, :, :], ACT.Copy).then_inc(w_hi, 1)

            split(1)
            act.wait_ge(wg_in, 16)
            nc.scalar.activation(wgh[:], wg[:], ACT.Copy).then_inc(w_hi, 1)
            n_sq = 0
            for n, (c, t) in enumerate(units):
                kind = CHUNKS[c][1] if c < NC else "gate"
                cols = 48 if c == NC else (CW if t < QT else P)
                rws = rows(t) if c == NC else P
                if kind in ("query", "key", "key_value"):
                    a, b = (rws, cols) if kind != "key_value" else ((P, KVW) if t < QT else (64, P))
                    act.wait_ge(tile_done, n + 1)
                    if n_sq >= 2:
                        act.wait_ge(summed, 2 * (n_sq - 1))
                    nc.scalar.activation(sq[0:a, n_sq % 2, 0:b], ps[0:a, t, 0:b], ACT.Square).then_inc(squared, 1)
                    act.wait_ge(summed, 2 * n_sq + 2)
                    nc.scalar.activation(stat[0:a, n_sq % 2, 1, 0:b // DK], stat[0:a, n_sq % 2, 0, 0:b // DK],
                                         ACT.Sqrt).then_inc(rooted, 1)
                    n_sq += 1
                if kind == "gate":
                    act.wait_ge(tile_done, n + 1)
                    if n >= 3:
                        act.wait_ge(stored[n % 3], store_level[n - 3])
                    nc.scalar.activation(y[0:rws, n % 3, 0:cols], ps[0:rws, t, 0:cols],
                                         ACT.Sigmoid).then_inc(bank_free[t], 1)
                if t == QT - 1 and c + 2 < NC:
                    split(c + 2)

        @block.vector
        def _(dve):
            step = Chain(dve, dve_step)
            for t in range(TT):
                nc.vector.nop().then_inc(bank_free[t], 1)
            nc.vector.nop().then_inc(w_split, 1)
            nc.vector.memset(ssum[:], 1.0).then_inc(ssum_set, 1)
            nc.vector.memset(tab[BUCKETS:BUCKETS + 1, :], NEG).then_inc(mask_row, 1)
            dve.wait_ge(x_sq, TT)
            nc.vector.tensor_scalar(ssum[:], ssum[:], 1.0 / D_MODEL, EPS, ALU.mult, ALU.add).then_inc(x_rstd, 1)
            dve.wait_ge(x_sq, TT + 1)
            nc.vector.reciprocal(rstd[:], rstd[:]).then_inc(x_rstd, 1)
            dve.wait_ge(x_rstd, 2)
            for t in range(2):
                nc.vector.tensor_scalar(x[:, t, :], x[:, t, :], rstd[:, t:t + 1], None, ALU.mult).then_inc(x_scaled, 1)
            dve.wait_ge(gains_in, 16 * 2)

            def gained(k):
                dve.wait_ge(x_turned, k + 1)
                if k >= 2:
                    dve.wait_ge(x_ready, k - 1)
                nc.vector.tensor_scalar(xf[:, k % 2, :], pt[:, k % 2, :], gain[:, k:k + 1], None,
                                        ALU.mult).then_inc(x_copied, 1)

            gained(0)
            for k in range(KT):
                if k + 1 < KT:
                    gained(k + 1)
                dve.wait_ge(x_hi, k + 1)
                nc.vector.tensor_tensor(xl[:, k, :], xf[:, k % 2, :], xh[:, k, :].bitcast(F32),
                                        ALU.subtract).then_inc(x_ready, 1)
            dve.wait_ge(x_turned, KT + 1)
            for k in range(KT):
                ins = nc.vector.tensor_scalar(xsam[:, k, :], pt[:, 0, N_DEC * k:N_DEC * (k + 1)], gain[:, k:k + 1], None,
                                              ALU.mult)
            ins.then_inc(x_ready, 1)
            for j in range(4):
                dve.wait_ge(bias_mm, j + 1)
                nc.vector.tensor_copy(brow[:, 389 * j:389 * (j + 1)], ps[0:24, j, 0:389]).then_inc(bias_row, 1)
            def split(c):
                dve.wait_ge(w_hi, c + 1 if c >= 2 else 1)
                nc.vector.tensor_tensor(wl[:, c % 2, :, :], w[:, c % 2, :, :], wh[:, c % 2, :, :].bitcast(F32),
                                        ALU.subtract).then_inc(w_split, 1)

            split(1)
            dve.wait_ge(w_hi, 2)
            nc.vector.tensor_tensor(wgl[:], wg[:], wgh[:].bitcast(F32), ALU.subtract).then_inc(gates_split, 1)
            dve.wait_ge(heads_in, 64)
            for j in range(2):
                step(nc.vector.tensor_scalar(heads_gain[:, j, :], heads_gain[:, j, :], SCALE, None, ALU.mult))
            n_sq = 0
            for n, (c, t) in enumerate(units):
                kind = CHUNKS[c][1] if c < NC else "gate"
                cols = CW if t < QT else P
                k = n % 3
                if kind != "gate":
                    dve.wait_ge(tile_done, n + 1)
                    if n >= 3:
                        dve.wait_ge(stored[k], store_level[n - 3])
                if kind in ("query", "key", "key_value"):
                    a, b = (P, cols) if kind != "key_value" else ((P, KVW) if t < QT else (64, P))
                    g = b // DK
                    m = n_sq % 2
                    dve.wait_ge(squared, n_sq + 1)
                    nc.vector.tensor_reduce(stat[0:a, m, 0, 0:g], sq[0:a, m, 0:b].rearrange("p (g e) -> p g e", e=DK),
                                            AX.X, ALU.add).then_inc(summed, 1)
                    dve.wait_ge(summed, 2 * n_sq + 1)
                    nc.vector.tensor_scalar(stat[0:a, m, 0, 0:g], stat[0:a, m, 0, 0:g], 1.0 / DK, EPS,
                                            ALU.mult, ALU.add).then_inc(summed, 1)
                    if kind == "key_value":
                        raw = (slice(0, P), slice(KVW, CW)) if t < QT else (slice(64, P), slice(0, P))
                        nc.vector.tensor_copy(y[raw[0], k, raw[1]], ps[raw[0], t, raw[1]]).then_inc(dve_step, 1)
                        step.n += 1
                    dve.wait_ge(rooted, n_sq + 1)
                    step(nc.vector.reciprocal(stat[0:a, m, 2, 0:g], stat[0:a, m, 1, 0:g]))
                    row = {"q": 0, "qd": 1, "diff": 2, "nsa": 3, "win": 3}[CHUNKS[c][2]]
                    yv = y[0:a, k, 0:b].rearrange("p (g e) -> p g e", e=DK)
                    nc.vector.tensor_tensor(yv, ps[0:a, t, 0:b].rearrange("p (g e) -> p g e", e=DK),
                                                   stat[0:a, m, 2, 0:g].unsqueeze(2).to_broadcast([a, g, DK]),
                                            ALU.mult).then_inc(bank_free[t], 1)
                    dve.wait_ge(bank_free[t], c + 2)
                    nc.vector.tensor_tensor(yv, yv, heads_gain[0:a, row:row + 1, :].to_broadcast([a, g, DK]),
                                            ALU.mult).then_inc(y_ready, 1)
                    n_sq += 1
                elif kind == "plain":
                    nc.vector.tensor_copy(y[:, k, 0:cols], ps[:, t, 0:cols]).then_inc(bank_free[t], 1)
                if t == QT - 1 and c + 2 < NC:
                    split(c + 2)

        @block.gpsimd
        def _(pool):
            pool.wait_ge(first_hi, 1)
            nc.gpsimd.tensor_tensor(wl[:, 0, :, :], w[:, 0, :, :], wh[:, 0, :, :].bitcast(F32), ALU.subtract).then_inc(first_split, 1)

        @block.tensor
        def _(pe):
            pe.wait_ge(table_in, 32)
            pe.wait_ge(mask_row, 1)
            for j in range(4):
                pe.matmul(ps[0:24, j, 0:389], tab[:], hot[:, 389 * j:389 * (j + 1)], start=True, stop=True).then_inc(bias_mm, 1)
            pe.wait_ge(gains_in, 16 * 2)
            pe.wait_ge(x_scaled, TT)
            for k in range(KT):
                if k >= 2:
                    pe.wait_ge(x_copied, k - 1)
                for t in range(QT):
                    ins = pe.transpose(pt[:, k % 2, P * t:P * (t + 1)], x[:, t, P * k:P * (k + 1)], ident[:])
                ins.then_inc(x_turned, 1)
            pe.wait_ge(x_copied, KT)
            for k in range(KT):
                ins = pe.transpose(pt[:, 0, N_DEC * k:N_DEC * (k + 1)], x[0:N_DEC, QT, P * k:P * (k + 1)],
                                   ident[0:N_DEC, 0:N_DEC])
            ins.then_inc(x_turned, 1)
            pe.wait_ge(bias_row, 4)
            pe.wait_ge(x_ready, KT + 1)

            def chunk(u, c, width, hi, lo, raw):
                pe.wait_ge(bank_free[QT], c + 1)
                for k in range(KT):
                    for j in range(4 if width == CW else 1):
                        n = P if width == CW else width
                        ins = pe.matmul(ps[32 * j:32 * j + 32, QT, 0:n], xsam[:, k, :], raw(k)[:, n * j:n * (j + 1)],
                                        start=k == 0, stop=k == KT - 1)
                ins.then_inc(tile_done, 1)
                for t in range(QT):
                    pe.wait_ge(bank_free[t], c + 1)
                    for k in range(KT):
                        xk = slice(P * t, P * (t + 1))
                        pe.matmul(ps[:, t, 0:width], xh[:, k, xk], hi(k), start=k == 0, stop=False)
                        pe.matmul(ps[:, t, 0:width], xh[:, k, xk], lo(k), start=False, stop=False)
                        ins = pe.matmul(ps[:, t, 0:width], xl[:, k, xk], hi(k), start=False, stop=k == KT - 1)
                    ins.then_inc(tile_done, 1)

            def full(u, c):
                chunk(u, c, CW, lambda k: wh[:, u, k, :], lambda k: wl[:, u, k, :], lambda k: w[:, u, k, :])


            pe.wait_ge(first_split, 1)
            with pe.Fori(0, NC // 2) as i:
                for u in range(2):
                    pe.wait_ge(w_split, 2 * i + u + 1)
                    full(u, 2 * i + u)
            pe.wait_ge(w_split, NC)
            full(0, NC - 1)
            pe.wait_ge(gates_split, 1)
            chunk(0, NC, 48, lambda k: wgh[:, k, :], lambda k: wgl[:, k, :], lambda k: wg[:, k, :])


def bucket_of(dist):
    exact = BUCKETS // 2
    if dist < exact:
        return dist
    return min(exact + int(math.log(dist / exact) / math.log(MAX_DIST / exact) * (BUCKETS - exact)), BUCKETS - 1)


def bucket_hot():
    hot = np.zeros((BUCKETS + 1, BROW), np.float32)
    for i in range(BROW):
        dist = BTOP - i
        hot[BUCKETS if dist < 0 else bucket_of(dist), i] = 1.0
    return hot


CH = 64
CHP = SEQ // CMP_STRIDE
JP = CMP_STRIDE // 2
CHUNKS_PER_PAGE = PAGE // CMP_STRIDE
XW = GROUPS * P + 2


def compress(nc, d):
    with ExitStack() as ctx:
        s = Space(nc, ctx, "cm")
        raw = s.sb("raw", [P, 2, CMP_STRIDE, 2 * KVW])
        laid = s.sb("laid", [P, 2, GROUPS, CMP_STRIDE * DK])
        xh = s.sb("xh", [P, JP, XW], F32R)
        xl = s.sb("xl", [P, JP, XW], F32R)
        w1h = s.sb("w1h", [P, 2, 2 * JP, CMP_HID], F32R)
        w1l = s.sb("w1l", [P, 2, 2 * JP, CMP_HID], F32R)
        w2 = s.sb("w2", [P, 2, 2, DK])
        pe_t = s.sb("pe_t", [P, 2, 2 * JP])
        pe_row = s.sb("pe_row", [1, 4 * P])
        pe_h = s.sb("pe_h", [P, 4])
        hid = s.sb("hid", [P, 2, 2, CW])
        ident = s.sb("ident", [P, P])
        gain = s.sb("gain", [P, DK])
        table = s.sb("table", [1, DEC_B * N_PAGES], I32)
        sq = s.sb("sq", [P, KVW])
        stat = s.sb("stat", [P, 3, GROUPS])
        out = s.sb("out", [P, 2, KVW])
        pt = s.ps("pt", [P, 4, CW])
        ph = s.ps("ph", [P, 2, CW])
        pc = s.ps("pc", [P, 2, CW])

        consts_in, table_in = s.sem("consts_in"), s.sem("table_in")
        w1_in = [s.sem(f"w1_in{k}") for k in range(2)]
        w1_hi, w1_lo, pe_mm, pe_ready, pads = (s.sem(n) for n in ("w1_hi", "w1_lo", "pe_mm", "pe_ready", "pads"))
        raw_in = [s.sem(f"raw_in{u}") for u in range(2)]
        laid_out, pe_row_ready = s.sem("laid_out"), s.sem("pe_row_ready")
        turned, x_hi, x_lo = s.sem("turned"), s.sem("x_hi"), s.sem("x_lo")
        hid_mm, hid_ready, row_mm = s.sem("hid_mm"), s.sem("hid_ready"), s.sem("row_mm")
        squared, summed, rooted, step_sem, out_ready = (
            s.sem(n) for n in ("squared", "summed", "rooted", "dve_step", "out_ready"))
        stored = [s.sem(f"stored{k}") for k in range(2)]
        block = ctx.enter_context(nc.Block())

        T_UNIT = 2 * GROUPS
        N_UNITS = DEC_B
        w1 = [d[f"cmp_w1_{x}"].rearrange("(k p) n -> p k n", p=P) for x in "kv"]
        raw_w1 = [laid[:, k, :, :].rearrange("p g c -> p (g c)").rearrange("p (k n) -> p k n", n=CMP_HID) for k in range(2)]
        nsa_chunks = d["cache_nsa"].rearrange("n (c j) e -> n c j e", j=CMP_STRIDE)
        nsa_p_chunks = d["nsa_p"].rearrange("(c j) e -> c j e", j=CMP_STRIDE)

        @block.sync
        def _(sp):
            sp.dma_start(table[:], d["page_table"]).then_inc(table_in, 16)
            sp.dma_start(ident[:], d["ident"]).then_inc(consts_in, 16)
            sp.dma_start(gain[:], spread(d["nsa_k_gain"], P)).then_inc(consts_in, 16)
            for k, x in enumerate("kv"):
                sp.dma_start(w2[:, k, :, :], d[f"cmp_w2_{x}"].rearrange("(h p) n -> p h n", p=P)).then_inc(consts_in, 16)
                with nc.allow_non_contiguous_dma("the position embedding, by contraction row"):
                    sp.dma_start(pe_t[:, k, :], d[f"cmp_pe_{x}"].rearrange("l e -> (l e)").rearrange("(k p) -> p k", p=P)
                                 ).then_inc(consts_in, 16)
            for k in range(2):
                sp.dma_start(raw_w1[k], w1[k]).then_inc(w1_in[k], 16)
            sp.wait_ge(table_in, 16)

            def store(n, k, kn):
                sp.wait_ge(out_ready, n + 3)
                sp.dma_start(d["kc_s" if k == 0 else "vc_s"][bass.ds(kn * P, P), :], out[:, k, :]).then_inc(stored[k], 16)

            def load(pair, u):
                if pair >= 2:
                    sp.wait_ge(laid_out, 2 * (pair - 1))
                for b in range(2):
                    for pg in range(N_PAGES):
                        page = sp.value_load(table[0:1, bass.ds((2 * pair + b) * N_PAGES + pg, 1)],
                                             min_val=0, max_val=d["cache_nsa"].shape[0] - 1)
                        at = CH * b + CHUNKS_PER_PAGE * pg
                        sp.dma_start(raw[at:at + CHUNKS_PER_PAGE, u, :, :],
                                     nsa_chunks[bass.ds(page, 1), :, :, 0:2 * KVW].rearrange("n c j e -> (n c) j e")).then_inc(raw_in[u], 16)

            load(0, 0)
            load(1, 1)
            for pair in range(DEC_B // 2):
                for k in range(2):
                    store(2 * pair + k, k, pair)
                if pair + 2 < DEC_B // 2:
                    load(pair + 2, pair % 2)
                elif pair + 2 == DEC_B // 2:
                    sp.wait_ge(laid_out, 2 * (pair + 1))
                    sp.dma_start(raw[0:CHP, 0, :, :], nsa_p_chunks[:, :, 0:2 * KVW]).then_inc(raw_in[0], 16)
            for k, name in enumerate(("kc_p", "vc_p")):
                sp.wait_ge(out_ready, N_UNITS + k + 3)
                sp.dma_start(d[name], out[0:CHP, k, :]).then_inc(stored[k], 16)
            for k in range(2):
                sp.wait_ge(stored[k], 16 * (DEC_B // 2 + 2))

        FILL = 16 * 2 * N_PAGES
        PROMPT = [(N_UNITS + k, 0, k, CHP) for k in range(2)]

        def loop_units(i):
            return [(4 * i + 2 * u + k, u, k, P) for u in range(2) for k in range(2)]

        @block.scalar
        def _(act):
            for k in range(2):
                act.wait_ge(w1_in[k], 16)
                nc.scalar.activation(w1h[:, k, :, :], raw_w1[k], ACT.Copy).then_inc(w1_hi, 1)
            act.wait_ge(pe_ready, 1)
            act.wait_ge(pads, 2)

            def high_parts(n, r, jh):
                for g in range(GROUPS):
                    m = GROUPS * jh + g
                    act.wait_ge(turned, T_UNIT * n + m + 1)
                    if m == 0:
                        act.wait_ge(hid_mm, 2 * n + 1)
                    nc.scalar.activation(xh[:, 4 * jh:4 * jh + 4, r * g:r * (g + 1)],
                                         pt[:, m % 4, 0:4 * r].rearrange("p (j c) -> p j c", j=4), ACT.Copy).then_inc(x_hi, 1)

            def gelu(n, k, r):
                for ht in range(2):
                    act.wait_ge(hid_mm, 2 * n + ht + 2)
                    nc.scalar.activation(hid[:, k, ht, 0:4 * r], ph[:, ht, 0:4 * r], ACT.Gelu_apprx_tanh,
                                         bias=pe_h[:, 2 * k + ht:2 * k + ht + 1]).then_inc(hid_ready, 1)

            def norm(n, kn, r):
                act.wait_ge(row_mm, n + 1)
                nc.scalar.activation(sq[0:r, :], pc[0:r, 0, 0:KVW], ACT.Square).then_inc(squared, 1)
                act.wait_ge(summed, 2 * kn + 2)
                nc.scalar.activation(stat[0:r, 1, :], stat[0:r, 0, :], ACT.Sqrt).then_inc(rooted, 1)

            def run(units, key_no):
                for n, u, k, r in units:
                    high_parts(n, r, 0)
                    if k == 1:
                        norm(n - 1, key_no(u), r)
                    high_parts(n, r, 1)
                    gelu(n, k, r)

            with act.Fori(0, 2) as i:
                run(loop_units(i), lambda u: 2 * i + u)
            run(PROMPT, lambda u: DEC_B // 2)

        @block.vector
        def _(dve):
            nc.vector.nop().then_inc(x_lo, 1)
            for k in range(2):
                nc.vector.nop().then_inc(out_ready, 1)
                nc.vector.nop().then_inc(stored[k], 16)
            nc.vector.memset(xh[:, :, GROUPS * P:XW].bitcast(F32), 0.0).then_inc(pads, 1)
            nc.vector.memset(xl[:, :, GROUPS * P:XW].bitcast(F32), 0.0).then_inc(pads, 1)
            for k in range(2):
                dve.wait_ge(w1_hi, k + 1)
                nc.vector.tensor_tensor(w1l[:, k, :, :], raw_w1[k], w1h[:, k, :, :].bitcast(F32),
                                        ALU.subtract).then_inc(w1_lo, 1)
            dve.wait_ge(pe_mm, 1)
            nc.vector.tensor_copy(pe_row[:].rearrange("p (k n) -> p k n", k=2), pc[0:1, :, 0:CMP_HID]).then_inc(pe_row_ready, 1)
            dve.wait_ge(pe_mm, 2)
            nc.vector.tensor_copy(pe_h[:], ph[:, 0, 0:4]).then_inc(pe_ready, 1)

            dve.wait_ge(w1_lo, 2)

            def lay_out(n, u, k, r, level):
                if k == 0:
                    dve.wait_ge(raw_in[u], level)
                nc.vector.tensor_copy(laid[0:r, k, :, :].rearrange("p g (j e) -> p g j e", e=DK),
                                      raw[0:r, u, :, KVW * k:KVW * (k + 1)].rearrange("p j (g e) -> p g j e", e=DK)
                                      ).then_inc(laid_out, 1)

            def low_parts(n, r, jh):
                for g in range(GROUPS):
                    m = GROUPS * jh + g
                    dve.wait_ge(x_hi, T_UNIT * n + m + 1)
                    view = (slice(None), slice(4 * jh, 4 * jh + 4), slice(r * g, r * (g + 1)))
                    nc.vector.tensor_tensor(xl[view], pt[:, m % 4, 0:4 * r].rearrange("p (j c) -> p j c", j=4),
                                            xh[view].bitcast(F32), ALU.subtract).then_inc(x_lo, 1)

            def rows(n, k, kn, r, step):
                dve.wait_ge(row_mm, n + 1)
                dve.wait_ge(stored[k], 16 * kn + 16)
                if k == 1:
                    nc.vector.tensor_copy(out[0:r, 1, :], pc[0:r, 1, 0:KVW]).then_inc(out_ready, 1)
                    return
                dve.wait_ge(squared, kn + 1)
                nc.vector.tensor_reduce(stat[0:r, 0, :], sq[0:r, :].rearrange("p (g e) -> p g e", e=DK),
                                        AX.X, ALU.add).then_inc(summed, 1)
                dve.wait_ge(summed, 2 * kn + 1)
                nc.vector.tensor_scalar(stat[0:r, 0, :], stat[0:r, 0, :], 1.0 / DK, EPS, ALU.mult, ALU.add).then_inc(summed, 1)
                dve.wait_ge(rooted, kn + 1)
                step(nc.vector.reciprocal(stat[0:r, 2, :], stat[0:r, 1, :]))
                view = out[0:r, 0, :].rearrange("p (g e) -> p g e", e=DK)
                step(nc.vector.tensor_tensor(view, pc[0:r, 0, 0:KVW].rearrange("p (g e) -> p g e", e=DK),
                                             stat[0:r, 2, :].unsqueeze(2).to_broadcast([r, GROUPS, DK]), ALU.mult))
                nc.vector.tensor_tensor(view, view, gain[0:r, :].unsqueeze(1).to_broadcast([r, GROUPS, DK]),
                                        ALU.mult).then_inc(out_ready, 1)

            def run(units, key_no, step, level):
                for j, (n, u, k, r) in enumerate(units):
                    lay_out(n, u, k, r, level)
                    low_parts(n, r, 0)
                    if j:
                        rows(n - 1, 1 - k, kn, r, step)
                    kn = key_no(u)
                    low_parts(n, r, 1)
                rows(n, k, kn, r, step)

            dve.wait_ge(consts_in, 16 * 6)
            with dve.Fori(0, 2) as i:
                run(loop_units(i), lambda u: 2 * i + u, Chain(dve, step_sem, 4 * i), FILL * i + FILL)
            run(PROMPT, lambda u: DEC_B // 2, Chain(dve, step_sem, 8), 2 * FILL + 16)

        @block.tensor
        def _(pe):
            pe.nop().then_inc(hid_mm, 1)
            pe.wait_ge(consts_in, 16 * 6)
            for k in range(2):
                pe.wait_ge(w1_in[k], 16)
                for kt in range(2 * JP):
                    ins = pe.matmul(pc[0:1, k, 0:CMP_HID], pe_t[:, k, kt:kt + 1], raw_w1[k][:, kt, :],
                                    start=kt == 0, stop=kt == 2 * JP - 1)
            ins.then_inc(pe_mm, 1)
            pe.wait_ge(pe_row_ready, 1)
            for x in range(4):
                ins = pe.matmul(ph[:, 0, x:x + 1], pe_row[0:1, P * x:P * (x + 1)], ident[0:1, 0:1], start=True, stop=True)
            ins.then_inc(pe_mm, 1)
            pe.wait_ge(pe_ready, 1)
            pe.wait_ge(w1_lo, 2)

            def turn(n, u, k, r, jh):
                for g in range(GROUPS):
                    m = GROUPS * jh + g
                    if jh:
                        pe.wait_ge(x_lo, T_UNIT * n + m - 4 + 2)
                    for j in range(4):
                        jp = 4 * jh + j
                        ins = pe.transpose(pt[:, m % 4, r * j:r * (j + 1)],
                                           laid[0:r, k, g, P * jp:P * (jp + 1)],
                                           ident[0:r, 0:r])
                    ins.then_inc(turned, 1)

            def hidden(n, k, r):
                for ht in range(2):
                    col = slice(P * ht, P * (ht + 1))
                    for jp in range(JP):
                        if ht == 0 and jp % 4 == 0:
                            pe.wait_ge(x_lo, T_UNIT * n + GROUPS * (jp // 4 + 1) + 1)
                        for half in range(2):
                            mh, ml = xh[:, jp, half:half + 4 * r], xl[:, jp, half:half + 4 * r]
                            kt = JP * half + jp
                            o = ph[:, ht, 0:4 * r]
                            pe.matmul(o, w1h[:, k, kt, col], mh, start=jp == 0 and half == 0, stop=False)
                            pe.matmul(o, w1h[:, k, kt, col], ml, start=False, stop=False)
                            ins = pe.matmul(o, w1l[:, k, kt, col], mh, start=False, stop=jp == JP - 1 and half == 1)
                    ins.then_inc(hid_mm, 1)

            def second(n, k, r):
                pe.wait_ge(hid_ready, 2 * n + 2)
                pe.wait_ge(out_ready, n + 1)
                for g in range(GROUPS):
                    for ht in range(2):
                        ins = pe.matmul(pc[0:r, k, DK * g:DK * (g + 1)], hid[:, k, ht, r * g:r * (g + 1)], w2[:, k, ht, :],
                                        start=ht == 0, stop=ht == 1)
                ins.then_inc(row_mm, 1)

            def run(units):
                for j, (n, u, k, r) in enumerate(units):
                    if j == 0:
                        pe.wait_ge(x_lo, T_UNIT * n + 1)
                    pe.wait_ge(laid_out, n + 1)
                    turn(n, u, k, r, 0)
                    if j:
                        second(*prev)
                    turn(n, u, k, r, 1)
                    hidden(n, k, r)
                    prev = (n, k, r)
                second(*prev)

            with pe.Fori(0, 2) as i:
                run(loop_units(i))
            run(PROMPT)


CHP = SEQ // CMP_STRIDE
HEADS_AT_ONCE = 4
LAM_INIT = 0.8 - 0.6 * math.exp(-0.3 * 0)


def lambda_steps(nc, dve, act_exp_done, lam, lv, step, ready):
    for j in range(2):
        step(nc.vector.tensor_tensor(lv[:, j, :], lv[:, 2 * j, :] if j == 0 else lv[:, 2, :],
                                     lv[:, 1, :] if j == 0 else lv[:, 3, :], ALU.mult))
    nc.vector.tensor_reduce(lam[:, 1:3], lv[:, 0:2, :], AX.X, ALU.add).then_inc(ready, 1)
    dve.wait_ge(act_exp_done, 1)
    step(nc.vector.tensor_tensor(lam[:, 0:1], lam[:, 2:3], lam[:, 1:2], ALU.subtract))
    step(nc.vector.tensor_scalar(lam[:, 0:1], lam[:, 0:1], -LAM_INIT, None, ALU.add))


def prompt_attention(nc, d):
    with ExitStack() as ctx:
        s = Space(nc, ctx, "pa")
        q = s.sb("q", [P, 2, QT, HPG * DK])
        ks = s.sb("ks", [P, 2, QT, 2, DK])
        kw = s.sb("kw", [P, 2, QT, 2, DK])
        kc = s.sb("kc", [CHP, 2, 2, DK])
        vs = s.sb("vs", [P, 2, QT, DK])
        vw = s.sb("vw", [P, 2, QT, DK])
        vc = s.sb("vc", [CHP, 2, DK])
        strip = s.sb("strip", [P, 2, HPG, STRIP])
        gates = s.sb("gates", [P, 2, QT, HPG * 3])
        dq = s.sb("dq", [P, HEADS_AT_ONCE, QT, P])
        dk = s.sb("dk", [P, HEADS_AT_ONCE, QT, P])
        dv = s.sb("dv", [P, HEADS_AT_ONCE, QT, DV])
        dstrip = s.sb("dstrip", [P, HEADS_AT_ONCE, SEQ])
        q_t = s.sb("q_t", [P, 2, SEQ])
        ks_t = s.sb("ks_t", [P, SEQ])
        kw_t = s.sb("kw_t", [P, SEQ])
        kc_t = s.sb("kc_t", [P, CHP])
        sc = s.sb("sc", [P, 4, 2, SEQ])
        p_t = s.sb("p_t", [P, 2, 2, SEQ])
        nmax = s.sb("nmax", [P, 4, 2])
        rsum = s.sb("rsum", [P, 8, 2, 3])
        maps = s.sb("maps", [P, 2])
        coef = s.sb("coef", [P, 4, 6])
        part = s.sb("part", [P, 2, 6 * DK])
        oa = s.sb("oa", [P, 2, QT, HPG * DK])
        ob = s.sb("ob", [P, QT, DHEADS, DV])
        osq = s.sb("osq", [P, DHEADS, DV])
        ssum = s.sb("ssum", [P, QT * DHEADS])
        ident = s.sb("ident", [P, P])
        lam = s.sb("lam", [P, 4])
        lv = s.sb("lv", [P, 4, DD])
        gain = s.sb("gain", [P, DV])
        ps_s = s.ps("ps_s", [P, 4, CW])
        ps_t = s.ps("ps_t", [P, 2, CW])
        ps_o = s.ps("ps_o", [P, 2, CW])

        consts_in, begun, begun_keys = s.sem("consts_in"), s.sem("begun"), s.sem("begun_keys")
        g_in = [s.sem(f"g_in{u}") for u in range(2)]
        h_in = [s.sem(f"h_in{u}") for u in range(HEADS_AT_ONCE)]
        keys_mm, q_copied, k_copied = s.sem("keys_mm"), s.sem("q_copied"), s.sem("k_copied")
        scores_mm, scored, probs, turned, values_mm = (
            s.sem(n) for n in ("scores_mm", "scored", "probs", "turned", "values_mm"))
        p_copied = [s.sem(f"p_copied{k}") for k in range(2)]
        combined, step_sem, lam_dot, lam_exp = s.sem("combined"), s.sem("dve_step"), s.sem("lam_dot"), s.sem("lam_exp")
        oa_out = [s.sem(f"oa_out{u}") for u in range(2)]
        window_kept, pool_step = s.sem("window_kept"), s.sem("pool_step")
        o_sq, o_root, ob_ready, ob_out = s.sem("o_sq"), s.sem("o_root"), s.sem("ob_ready"), s.sem("ob_out")
        block = ctx.enter_context(nc.Block())

        HP = HPG // 2
        DU, DM = QT, QT
        NU, NM = HP * QT * 3, HP * QT
        N_BASE, M_BASE = DHEADS * DU, DHEADS * DM
        G_LOADS, H_LOADS = 12, 4

        class Unit:
            def __init__(self, lhs, rhs, bias, width, values, out, clamp, m, br, nbr):
                self.lhs, self.rhs, self.bias, self.width, self.values, self.out = lhs, rhs, bias, width, values, out
                self.clamp, self.m, self.br, self.nbr = clamp, m, br, nbr

        HALF = [slice(DK * x, DK * (x + 1)) for x in range(2)]

        def group_units(u, m0):
            out = []
            for hp in range(HP):
                for t in range(QT):
                    m = m0 + QT * hp + t
                    lhs = [q_t[x, hp, P * t:P * (t + 1)] for x in HALF]
                    n = P * (t + 1)
                    first = P * (QT - 1 - t)
                    c0 = first + CMP_BLOCK - 1
                    two = [strip[:, u, 2 * hp + x, :] for x in range(2)]
                    cb = [x[:, c0:c0 + CMP_STRIDE * (CHP - 1) + 1:CMP_STRIDE] for x in two]
                    sb = [x[:, first:SEQ] for x in two]
                    o = lambda br: [ps_o[:, m % 2, DK * (3 * x + br):DK * (3 * x + br + 1)] for x in range(2)]
                    out.append(Unit(lhs, [kc_t[x, :] for x in HALF], cb, CHP, [vc[:, u, :]], o(0), 1e29, m, 0, 3))
                    out.append(Unit(lhs, [ks_t[x, 0:n] for x in HALF], sb, n, [vs[:, u, k, :] for k in range(t + 1)],
                                    o(1), 3e38, m, 1, 3))
                    out.append(Unit(lhs, [kw_t[x, 0:n] for x in HALF], sb, n, [vw[:, u, k, :] for k in range(t + 1)],
                                    o(2), 3e38, m, 2, 3))
            return out

        def head_units(u, m0):
            return [Unit([q_t[x, 0, P * t:P * (t + 1)] for x in HALF], [ks_t[x, 0:P * (t + 1)] for x in HALF],
                         [dstrip[:, u, P * (QT - 1 - t):SEQ]] * 2, P * (t + 1), [dv[:, u, k, :] for k in range(t + 1)],
                         [ps_o[:, t % 2, DV * x:DV * (x + 1)] for x in range(2)], 3e38, m0 + t, 0, 1) for t in range(QT)]

        HEAD_PASS = [x for k in range(HEADS_AT_ONCE) for x in head_units(k, DM * k)]
        GROUP_PASS = [x for k in range(2) for x in group_units(k, NM * k)]

        @block.sync
        def _(sp):
            sp.dma_start(ident[:], d["ident"]).then_inc(consts_in, 16)
            for j, name in enumerate(("lambda_q1", "lambda_k1", "lambda_q2", "lambda_k2")):
                sp.dma_start(lv[:, j, :], spread(d[name], P)).then_inc(consts_in, 16)
            sp.dma_start(gain[:], spread(d["diff_subln"], P)).then_inc(consts_in, 16)

            def tok(ap):
                return ap.rearrange("(t p) c -> p t c", p=P)

            def load_group(g, u):
                q_cols, cols = bass.ds(g * HPG * DK, HPG * DK), lambda slot: bass.ds(g * DK + slot * KVW, DK)
                pairs = [(q[:, u, :, :], tok(d["q"][0:SEQ, q_cols])), (vs[:, u, :, :], tok(d["nsa_p"][:, cols(3)])),
                         (vw[:, u, :, :], tok(d["win_p"][:, cols(1)])), (vc[:, u, :], d["vc_p"][:, cols(0)]),
                         (strip[:, u, :, :], d["toep"][bass.ds(g * HPG, HPG), :, :].rearrange("h p x -> p h x")),
                         (gates[:, u, :, :], tok(d["g"][0:SEQ, bass.ds(g * HPG * 3, HPG * 3)]))]
                for k in range(2):
                    pairs += [(ks[:, u, :, k, :], tok(d["nsa_p"][:, cols(2)])), (kw[:, u, :, k, :], tok(d["win_p"][:, cols(0)])),
                              (kc[:, u, k, :], d["kc_p"][:, cols(0)])]
                assert len(pairs) == G_LOADS
                for dst, src in pairs:
                    sp.dma_start(dst, src).then_inc(g_in[u], 16)

            def load_head(h, u):
                cols = lambda slot: bass.ds(h * P + slot * 1024, P)
                for dst, src in ((dq[:, u, :, :], tok(d["qd"][0:SEQ, cols(0)])), (dk[:, u, :, :], tok(d["diff_p"][:, cols(0)])),
                                 (dv[:, u, :, :], tok(d["diff_p"][:, cols(1)])),
                                 (dstrip[:, u, :], d["toep"][bass.ds(h + HEADS, 1), :, 0:SEQ].rearrange("h p x -> (h p) x"))):
                    sp.dma_start(dst, src).then_inc(h_in[u], 16)

            for h in range(HEADS_AT_ONCE):
                load_head(h, h)
            load_group(0, 0)
            load_group(1, 1)
            for h in range(HEADS_AT_ONCE, DHEADS):
                sp.wait_ge(combined, DM * (h - HEADS_AT_ONCE + 1) + 2)
                load_head(h, h % HEADS_AT_ONCE)
            for g in range(GROUPS):
                sp.wait_ge(combined, M_BASE + NM * (g + 1) + 2)
                sp.dma_start(tok(d["oa"][0:SEQ, HPG * DK * g:HPG * DK * (g + 1)]), oa[:, g % 2, :, :]).then_inc(oa_out[g % 2], 16)
                if g + 2 < GROUPS:
                    load_group(g + 2, g % 2)
            for u in range(2):
                sp.wait_ge(oa_out[u], 48)
            for t in range(QT):
                sp.wait_ge(ob_ready, t + 1)
                sp.dma_start(d["ob"][P * t:P * (t + 1), :], ob[:, t, :, :].rearrange("p h e -> p (h e)")).then_inc(ob_out, 16)
            sp.wait_ge(ob_out, 16 * QT)

        @block.gpsimd
        def _(pool):
            pool.wait_ge(combined, 2 * DM + 2)
            pool.dma_start(d["win_s"][:, 0:WINDOW - DEC_T, :], d["cache_win"][:, DEC_T:WINDOW, :]).then_inc(window_kept, 16)
            pool.wait_ge(combined, M_BASE + 2)
            step = Chain(pool, pool_step)
            for t in range(QT):
                step(nc.gpsimd.tensor_tensor(osq[:], ob[:, t, :, :], ob[:, t, :, :], ALU.mult))
                w = DV
                while w > 1:
                    w //= 2
                    step(nc.gpsimd.tensor_tensor(osq[:, :, 0:w], osq[:, :, 0:w], osq[:, :, w:2 * w], ALU.add))
                step(nc.gpsimd.tensor_scalar(ssum[:, DHEADS * t:DHEADS * (t + 1)], osq[:, :, 0], 1.0 / DV, EPS, ALU.mult, ALU.add))
                step(nc.gpsimd.tensor_tensor(ob[:, t, :, :], ob[:, t, :, :], gain[:].unsqueeze(1).to_broadcast([P, DHEADS, DV]),
                                             ALU.mult))
            nc.gpsimd.nop().then_inc(o_sq, 1)
            pool.wait_ge(window_kept, 16)

        @block.tensor
        def _(pe):
            pe.wait_ge(consts_in, 96)

            def turn_head(u, h, level, n):
                pe.wait_ge(h_in[u], level)
                pe.wait_ge(scored, 2 * n + 4)
                for k, src in enumerate((dq, dk)):
                    for t in range(QT):
                        ins = pe.transpose(ps_s[:, k, P * t:P * (t + 1)], src[:, u, t, :], ident[:])
                    ins.then_inc(keys_mm, 1)
                pe.wait_ge(q_copied, h + 1)
                pe.wait_ge(k_copied, h + 1)

            def turn_group(u, g, level, n, n_turned):
                pe.wait_ge(g_in[u], level)
                pe.wait_ge(scored, 2 * n + 4)
                for hp in range(2):
                    for t in range(QT):
                        ins = pe.transpose(ps_s[:, 2 * hp, P * t:P * (t + 1)], q[:, u, t, P * hp:P * (hp + 1)], ident[:])
                    ins.then_inc(keys_mm, 1)
                    for t in range(QT):
                        k = (ks, kw)[hp][:, u, t, :, :].rearrange("p a e -> p (a e)")
                        ins = pe.transpose(ps_s[:, 2 * hp + 1, P * t:P * (t + 1)], k, ident[:])
                    ins.then_inc(keys_mm, 1)
                pe.wait_ge(p_copied[0], n_turned + 1)
                pe.sem_inc(begun_keys, 1)
                pe.transpose(ps_t[:, 0, 0:CHP], kc[:, u, :, :].rearrange("p a e -> p (a e)"),
                             ident[0:CHP, 0:CHP]).then_inc(keys_mm, 1)
                pe.wait_ge(q_copied, DHEADS + 2 * g + 2)
                pe.wait_ge(k_copied, DHEADS + 3 * g + 3)

            def scores(x, j, n):
                pe.wait_ge(scored, 2 * n + 2)
                for a in range(2):
                    ins = pe.matmul(ps_s[:, 2 * (j % 2) + a, 0:x.width], x.lhs[a], x.rhs[a], start=True, stop=True)
                ins.then_inc(scores_mm, 1)

            def turn(x, j, n):
                for a in range(2):
                    pe.wait_ge(probs, 2 * n + a + 1)
                    pe.wait_ge(p_copied[a], n + 1)
                    for k, v in enumerate(x.values):
                        r = v.shape[0]
                        ins = pe.transpose(ps_t[0:r, a, P * k:P * (k + 1)], sc[:, j % 4, a, P * k:P * k + r], ident[:])
                    ins.then_inc(turned, 1)

            def values(x, j, n, m0):
                if x.br == 0:
                    pe.wait_ge(combined, m0 + x.m + 1)
                for a in range(2):
                    pe.wait_ge(p_copied[a], n + 2)
                    for k, v in enumerate(x.values):
                        r = v.shape[0]
                        ins = pe.matmul(x.out[a], p_t[0:r, j % 2, a, P * k:P * (k + 1)], v, start=k == 0,
                                        stop=k == len(x.values) - 1)
                ins.then_inc(values_mm, 1)

            def run(units, n0, m0, setup):
                for j in range(len(units) + 3):
                    setup(j)
                    if j < len(units):
                        scores(units[j], j, n0 + j)
                    if 2 <= j < len(units) + 2:
                        turn(units[j - 2], j - 2, n0 + (j - 2))
                    if j >= 3:
                        values(units[j - 3], j - 3, n0 + (j - 3), m0)

            with pe.Fori(0, DHEADS // HEADS_AT_ONCE) as i:
                n0 = DU * HEADS_AT_ONCE * i

                def next_head(j):
                    k = j // DU
                    if j % DU == 0 and k < HEADS_AT_ONCE:
                        turn_head(k, HEADS_AT_ONCE * i + k, 16 * H_LOADS * i + 16 * H_LOADS, n0 + j)

                run(HEAD_PASS, n0, DM * HEADS_AT_ONCE * i, next_head)
            with pe.Fori(0, GROUPS // 2) as i:
                n0 = N_BASE + 2 * NU * i

                def next_group(j):
                    if j in (0, NU):
                        turn_group(j // NU, 2 * i + j // NU, 16 * G_LOADS * i + 16 * G_LOADS, n0 + j, n0 + (j - 2 if j else 0))

                run(GROUP_PASS, n0, M_BASE + 2 * NM * i, next_group)

        @block.scalar
        def _(act):
            act.wait_ge(lam_dot, 1)
            nc.scalar.activation(lam[:, 1:3], lam[:, 1:3], ACT.Exp).then_inc(lam_exp, 1)

            def exps(x, j, n):
                for a in range(2):
                    act.wait_ge(scored, 2 * n + a + 5)
                    nc.scalar.activation(sc[:, j % 4, a, 0:x.width], sc[:, j % 4, a, 0:x.width], ACT.Exp, scale=-1.0,
                                         bias=nmax[:, j % 4, a:a + 1], accum_out=rsum[:, x.m % 8, a, x.br:x.br + 1]
                                         ).then_inc(probs, 1)

            def copy(x, j, n):
                act.wait_ge(turned, 2 * n + 9)
                act.wait_ge(values_mm, n + 1)
                r, w = x.values[0].shape[0], P * len(x.values)
                nc.scalar.activation(p_t[0:r, j % 2, 0, 0:w], ps_t[0:r, 0, 0:w], ACT.Copy).then_inc(p_copied[0], 1)

            def run(units, n0, setup):
                for j in range(len(units) + 2):
                    setup(j)
                    if j < len(units):
                        exps(units[j], j, n0 + j)
                    if j >= 2:
                        copy(units[j - 2], j - 2, n0 + (j - 2))

            with act.Fori(0, DHEADS // HEADS_AT_ONCE) as i:
                def next_head(j):
                    if j % DU == 0 and j // DU < HEADS_AT_ONCE:
                        act.wait_ge(keys_mm, 2 * HEADS_AT_ONCE * i + 2 * (j // DU) + 1)
                        nc.scalar.activation(q_t[:, 0, :], ps_s[:, 0, :], ACT.Copy).then_inc(q_copied, 1)

                run(HEAD_PASS, DU * HEADS_AT_ONCE * i, next_head)
            with act.Fori(0, GROUPS // 2) as i:
                def next_group(j):
                    if j in (0, NU):
                        for hp in range(2):
                            act.wait_ge(keys_mm, 10 * i + 2 * DHEADS + 5 * (j // NU) + 2 * hp + 1)
                            nc.scalar.activation(q_t[:, hp, :], ps_s[:, 2 * hp, :], ACT.Copy).then_inc(q_copied, 1)

                run(GROUP_PASS, N_BASE + 2 * NU * i, next_group)
            act.wait_ge(o_sq, 1)
            nc.scalar.activation(ssum[:], ssum[:], ACT.Sqrt).then_inc(o_root, 1)

        @block.vector
        def _(dve):
            nc.vector.nop().then_inc(scored, 4)
            nc.vector.nop().then_inc(combined, 2)
            nc.vector.nop().then_inc(turned, 8)
            nc.vector.nop().then_inc(values_mm, 2)
            for k in range(2):
                nc.vector.nop().then_inc(p_copied[k], 1)
                nc.vector.nop().then_inc(oa_out[k], 16)
            step = Chain(dve, step_sem)
            dve.wait_ge(consts_in, 96)
            lambda_steps(nc, dve, lam_exp, lam, lv, step, lam_dot)
            step(nc.vector.tensor_scalar(gain[:], gain[:], 1.0 - LAM_INIT, None, ALU.mult))
            step(nc.vector.memset(maps[:], 1.0))
            step(nc.vector.tensor_copy(maps[:, 1:2], lam[:, 0:1]))
            done = step.n

            def score(x, j, n):
                dve.wait_ge(scores_mm, n + 1)
                dve.wait_ge(turned, 2 * n + 2)
                dve.sem_inc(begun, 1)
                for a in range(2):
                    nc.vector.tensor_tensor_reduce(out=sc[:, j % 4, a, 0:x.width], in0=ps_s[:, 2 * (j % 2) + a, 0:x.width],
                                                   in1=x.bias[a], scale=-1.0, scalar=x.clamp, op0=ALU.add, op1=ALU.min,
                                                   accum_out=nmax[:, j % 4, a:a + 1]).then_inc(scored, 1)

            def copy(x, j, n):
                dve.wait_ge(turned, 2 * n + 10)
                dve.wait_ge(values_mm, n + 1)
                r, w = x.values[0].shape[0], P * len(x.values)
                nc.vector.tensor_copy(p_t[0:r, j % 2, 1, 0:w], ps_t[0:r, 1, 0:w]).then_inc(p_copied[1], 1)

            def scales(x, n, width, weights, chain):
                dve.wait_ge(probs, 2 * n + 2)
                out = coef[:, x.m % 4, 0:width]
                chain(nc.vector.tensor_scalar(out.rearrange("p (h b) -> p h b", h=2), rsum[:, x.m % 8, :, 0:width // 2],
                                              TINY, None, ALU.max))
                chain(nc.vector.reciprocal(out, out))
                chain(nc.vector.tensor_tensor(out, out, weights, ALU.mult))

            def group_scales(x, n, chain):
                u, hp, t = x.m // NM, x.m % NM // QT, x.m % QT
                scales(x, n, 6, gates[:, u, t, 6 * hp:6 * hp + 6], chain)

            def combine_group(x, n, chain):
                u, hp, t = x.m // NM, x.m % NM // QT, x.m % QT
                dve.wait_ge(values_mm, n + 3)
                chain(nc.vector.tensor_tensor(part[:, x.m % 2, :].rearrange("p (b e) -> p b e", e=DK),
                                              ps_o[:, x.m % 2, 0:6 * DK].rearrange("p (b e) -> p b e", e=DK),
                                              coef[:, x.m % 4, :].unsqueeze(2).to_broadcast([P, 6, DK]), ALU.mult))
                nc.vector.tensor_reduce(oa[:, u, t, P * hp:P * (hp + 1)].rearrange("p (h e) -> p h e", h=2),
                                        part[:, x.m % 2, :].rearrange("p (h b e) -> p h e b", h=2, e=DK),
                                        AX.X, ALU.add).then_inc(combined, 1)

            def combine_head(x, n, h, chain):
                k, t = x.m % 2, x.m % QT
                dve.wait_ge(values_mm, n + 3)
                chain(nc.vector.tensor_scalar(part[:, x.m % 2, 0:DV], ps_o[:, k, DV:2 * DV], coef[:, x.m % 4, 1:2], None, ALU.mult))
                out = ob[:, t, bass.ds(h, 1), :].rearrange("p a e -> p (a e)")
                nc.vector.scalar_tensor_tensor(out=out, in0=ps_o[:, k, 0:DV], scalar=coef[:, x.m % 4, 0:1],
                                               in1=part[:, x.m % 2, 0:DV], op0=ALU.mult, op1=ALU.add).then_inc(combined, 1)

            def run(units, n0, setup, scale, combine):
                LAG = 4
                for j in range(len(units) + LAG):
                    setup(j)
                    if j < len(units):
                        score(units[j], j, n0 + j)
                    if 2 <= j < len(units) + 2:
                        copy(units[j - 2], j - 2, n0 + (j - 2))
                    if 3 <= j < len(units) + 3 and units[j - 3].br == units[j - 3].nbr - 1:
                        scale(units[j - 3], n0 + (j - 3))
                    if j >= LAG:
                        x = units[j - LAG]
                        if x.br == x.nbr - 1:
                            combine(x, n0 + (j - LAG))

            with dve.Fori(0, DHEADS // HEADS_AT_ONCE) as i:
                chain = Chain(dve, step_sem, 4 * DM * HEADS_AT_ONCE * i + done)

                def next_head(j):
                    if j % DU == 0 and j // DU < HEADS_AT_ONCE:
                        dve.wait_ge(keys_mm, 2 * HEADS_AT_ONCE * i + 2 * (j // DU) + 2)
                        nc.vector.tensor_copy(ks_t[:], ps_s[:, 1, :]).then_inc(k_copied, 1)

                run(HEAD_PASS, DU * HEADS_AT_ONCE * i, next_head, lambda x, n: scales(x, n, 2, maps[:], chain),
                    lambda x, n: combine_head(x, n, HEADS_AT_ONCE * i + x.m // DM, chain))
            done += 4 * M_BASE
            with dve.Fori(0, GROUPS // 2) as i:
                chain = Chain(dve, step_sem, 4 * 2 * NM * i + done)

                def next_group(j):
                    if j in (0, NU):
                        u = j // NU
                        for k, dst in enumerate((ks_t, kw_t)):
                            dve.wait_ge(keys_mm, 10 * i + 2 * DHEADS + 5 * u + 2 * k + 2)
                            nc.vector.tensor_copy(dst[:], ps_s[:, 2 * k + 1, :]).then_inc(k_copied, 1)
                        dve.wait_ge(keys_mm, 10 * i + 2 * DHEADS + 5 * u + 5)
                        nc.vector.tensor_copy(kc_t[:], ps_t[:, 0, 0:CHP]).then_inc(k_copied, 1)
                        dve.wait_ge(oa_out[u], 16 * i + 16)

                run(GROUP_PASS, N_BASE + 2 * NU * i, next_group, lambda x, n: group_scales(x, n, chain),
                    lambda x, n: combine_group(x, n, chain))
            done += 4 * GROUPS * NM
            step = Chain(dve, step_sem, done)
            dve.wait_ge(o_root, 1)
            step(nc.vector.reciprocal(ssum[:], ssum[:]))
            for t in range(QT):
                nc.vector.tensor_tensor(ob[:, t, :, :], ob[:, t, :, :],
                                        ssum[:, DHEADS * t:DHEADS * (t + 1)].unsqueeze(2).to_broadcast([P, DHEADS, DV]),
                                        ALU.mult).then_inc(ob_ready, 1)


PAIRS = DEC_B // 2
ROWS = P // 2
NCOL = PAST + DEC_T
CMPS = ROWS

C_GROUP, C_STACK, C_IDX, C_WIN, C_MAP, C_NSA, C_DIFF = 0, 128, 192, 209, 213, 215, 471
C_ALL = 983


def decode_constants():
    c = np.zeros((P, C_ALL), np.float32)
    for r in range(P):
        b, x = divmod(r, ROWS)
        h, t = divmod(x, DEC_T)
        for y in range(ROWS):
            c[r, C_GROUP + ROWS * b + y] = float(x // (HPG * DEC_T) == y // (HPG * DEC_T) and y % DEC_T == t)
        c[r, C_STACK + 32 * b + x % 32] = 1.0
        c[r, C_IDX:C_IDX + N_SLC] = np.arange(N_SLC)
        c[r, C_WIN:C_WIN + DEC_T] = [NEG if j <= t else 0.0 for j in range(DEC_T)]
        c[r, C_MAP + x // 32] = 1.0
        g = h // HPG
        c[r, C_NSA + DK * g:C_NSA + DK * (g + 1)] = 1.0
        half, dh = (r // 32) % 2, (r % 32) // DEC_T
        if dh // 4 == half:
            c[r, C_DIFF + DV * (dh % 4):C_DIFF + DV * (dh % 4 + 1)] = 1.0
    return c


def select_weights():
    c0 = np.arange(CMPS)[:, None] * CMP_STRIDE
    s0 = np.arange(N_SLC)[None, :] * SEL_BLOCK
    shared = np.clip(np.minimum(c0 + CMP_BLOCK, s0 + SEL_BLOCK) - np.maximum(c0, s0), 0, None)
    return (shared / CMP_BLOCK).astype(np.float32)


CHAIN = 24


def decode_attention(nc, d):
    with ExitStack() as ctx:
        s = Space(nc, ctx, "de")
        sel = s.sb("sel", [P, 2, N_PAGES, 2 * KVW])
        win = s.sb("win", [P, 2, WINDOW // P, 2 * KVW])
        dk = s.sb("dk", [P, 2, 2, DHEADS * P])
        dv = s.sb("dv", [P, 2, N_PAGES, DHEADS * DV])
        sel_n = s.sb("sel_n", [DEC_T, 2, 2 * KVW])
        win_n = s.sb("win_n", [DEC_T, 2, 2 * KVW])
        dk_n = s.sb("dk_n", [DEC_T, 2, DHEADS * P])
        dv_n = s.sb("dv_n", [DEC_T, 2, DHEADS * DV])
        kc = s.sb("kc", [P, KVW])
        vc = s.sb("vc", [P, KVW])
        qn = s.sb("qn", [2 * DEC_T, D_MODEL])
        qd = s.sb("qd", [2 * DEC_T, D_MODEL])
        gates = s.sb("gates", [P, 3])
        qb = s.sb("qb", [P, 2, 2, ROWS])
        qdb = s.sb("qdb", [P, DHEADS, 2, ROWS])
        slot = s.sb("slot", [P, 3, CW])
        s_cmp = s.sb("s_cmp", [P, CMPS])
        s_sel = s.sb("s_sel", [P, NCOL])
        s_win = s.sb("s_win", [P, WINDOW + DEC_T])
        s_dif = s.sb("s_dif", [P, NCOL])
        qp = s_dif[0:2 * DEC_T, 0:D_MODEL]
        b_nsa = s.sb("b_nsa", [P, DECW])
        b_win = s.sb("b_win", [P, WINDOW + DEC_T])
        b_dif = s.sb("b_dif", [P, NCOL])
        con = s.sb("con", [P, C_ALL])
        selw = s.sb("selw", [CMPS, N_SLC])
        nm = s.sb("nm", [P, 4, 4])
        rs = s.sb("rs", [P, 4])
        rr = s.sb("rr", [P, 8])
        cm = s.sb("cm", [P, 3, P])
        cd = s.sb("cd", [P, 64])
        gm = s.sb("gm", [P, P])
        pg = s.sb("pg", [CMPS, P])
        pick = s.sb("pick", [P, 3, N_SLC])
        part = s.sb("part", [P, CW])
        o_n = s.sb("o_n", [P, DK])
        o_d = s.sb("o_d", [P, DV])
        table = s.sb("table", [1, DEC_B * N_PAGES], I32)
        ident = s.sb("ident", [P, P])
        lam = s.sb("lam", [P, 4])
        lv = part[:, 0:4 * DD].rearrange("p (v e) -> p v e", e=DD)
        gain = s.sb("gain", [P, DV])
        ps_t = s.ps("ps_t", [P, 3, CW])
        ps_s = s.ps("ps_s", [P, 2, CW])
        ps_n = s.ps("ps_n", [P, CW])
        ps_d = s.ps("ps_d", [P, CW])
        Q_AT, PG_AT, IMP_AT = 256, 384, 256

        consts_in, table_in, b_ready, begun, begun_pe = (
            s.sem(n) for n in ("consts_in", "table_in", "b_ready", "begun", "begun_pe"))
        begun_sp, begun_pool = s.sem("begun_sp"), s.sem("begun_pool")
        q_in, new_in = s.sem("q_in"), s.sem("new_in")
        sel_in = [s.sem(f"sel_in{k}") for k in range(N_PAGES)]
        win_in = [s.sem(f"win_in{k}") for k in range(WINDOW // P)]
        dk_in = [s.sem(f"dk_in{k}") for k in range(2)]
        dv_in = [s.sem(f"dv_in{k}") for k in range(N_PAGES)]
        q_laid, q_turned, q_ready = s.sem("q_laid"), s.sem("q_turned"), s.sem("q_ready")
        turned, scores_mm, scored = s.sem("turned"), s.sem("scores_mm"), s.sem("scored")
        copied = [s.sem(f"copied{k}") for k in range(2)]
        max_ready, probs, coef_ready = s.sem("max_ready"), s.sem("probs"), s.sem("coef_ready")
        pg_mm, pg_copied, imp_mm = s.sem("pg_mm"), s.sem("pg_copied"), s.sem("imp_mm")
        nsa_mm, diff_mm, nsa_read, diff_read = s.sem("nsa_mm"), s.sem("diff_mm"), s.sem("nsa_read"), s.sem("diff_read")
        o_sq, o_root, nsa_out, diff_out = s.sem("o_sq"), s.sem("o_root"), s.sem("nsa_out"), s.sem("diff_out")
        nsa_stored, diff_stored = s.sem("nsa_stored"), s.sem("diff_stored")
        o_n_free, o_d_free = s.sem("o_n_free"), s.sem("o_d_free")
        step_sem, lam_dot, lam_exp = s.sem("dve_step"), s.sem("lam_dot"), s.sem("lam_exp")
        block = ctx.enter_context(nc.Block())

        STEPS = ([("sel", k, 0) for k in range(N_PAGES)] + [("win", k, 0) for k in range(WINDOW // P)]
                 + [("sel_n", 0, 0), ("win_n", 0, 0), ("cmp", 0, 0)] + [("dif_n", 0, k) for k in range(4)]
                 + [("dif", k, m) for k in range(N_PAGES) for m in range(4)]
                 + [("p_sel", 0, 0), ("p_sel", 1, 0), ("p_few", 0, 0), ("p_win", 0, 0), ("p_dif", 0, 0), ("p_dif_n", 0, 0)])
        N = len(STEPS)
        assert N % 3 == 0
        EVEN, ODD = (N + 1) // 2, N // 2
        AT = {x: k for k, x in reversed(list(enumerate(STEPS)))}
        SEL0, SEL1, WIN0, FEW, DIF0, DIF1 = range(6)
        LAST = [AT["sel", 3, 0], AT["sel", 7, 0], AT["win", 3, 0], AT["dif_n", 0, 3], AT["dif", 3, 3], AT["dif", 7, 3]]
        GROUP_OF = {}
        for g, (kind, a, b) in enumerate((("sel", 0, 4), ("sel", 4, 8), ("win", 0, 4), (None, 0, 0), ("dif", 0, 4), ("dif", 4, 8))):
            for k in range(a, b):
                GROUP_OF[kind, k] = g
        F_CMP, F_SEL, F_WIN, F_DIF = 0, 64, 68, 72
        TURN_CREDIT = N
        IMP_1, IMP_2 = LAST[FEW] + 6, LAST[FEW] + 9
        READ_AT = {last + 2 + (last + 1) % 2: g for g, last in enumerate(LAST)}
        GROUP_AT, SHARE_AT, CHOOSE_AT, SCALE_AT, SCALE_D_AT = IMP_1 - 1, IMP_1 + 1, IMP_2 + 2, IMP_2 + 6, LAST[DIF1] + 3
        assert all(x % 2 for x in (GROUP_AT, SHARE_AT, CHOOSE_AT, SCALE_AT, SCALE_D_AT, *READ_AT))

        def score_place(kind, k):
            if kind in ("sel", "win", "dif"):
                return GROUP_OF[kind, k] % 2, P * (k % 4)
            return FEW % 2, {"cmp": F_CMP, "sel_n": F_SEL, "win_n": F_WIN, "dif_n": F_DIF}[kind]

        def pieces(j):
            kind = STEPS[j][0]
            if kind in ("sel_n", "win_n", "dif_n"):
                return [(slice(0, P), slice(0, 4 * DEC_T))]
            if kind == "cmp":
                return [(slice(0, P), slice(0, 2 * P))]
            if kind == "p_few":
                return [(slice(0, DEC_T), slice(0, 4 * ROWS)), (slice(0, ROWS), slice(4 * ROWS, 5 * ROWS)),
                        (slice(ROWS, P), slice(5 * ROWS, 6 * ROWS))]
            if kind == "p_dif_n":
                return [(slice(0, DEC_T), slice(0, 64))]
            return [(slice(0, P), slice(0, CW))]

        @block.sync
        def _(sp):
            sp.dma_start(table[:], d["page_table"]).then_inc(table_in, 16)
            sp.dma_start(ident[:], d["ident"]).then_inc(consts_in, 16)
            for j, name in enumerate(("lambda_q1", "lambda_k1", "lambda_q2", "lambda_k2")):
                sp.dma_start(lv[:, j, :], spread(d[name], P)).then_inc(consts_in, 16)
            sp.dma_start(gain[:], spread(d["diff_subln"], P)).then_inc(consts_in, 16)
            sp.dma_start(con[:], d["decode_constants"]).then_inc(consts_in, 16)
            sp.dma_start(selw[:], d["select_weights"]).then_inc(consts_in, 16)
            for b in range(2):
                rows = slice(ROWS * b, ROWS * (b + 1))
                sp.dma_start(b_nsa[rows, :], d["decb"][0:HEADS].rearrange("h t k -> (h t) k")).then_inc(consts_in, 16)
                sp.dma_start(b_win[rows, :], d["decb"][0:HEADS, :, PAST - WINDOW:NCOL].rearrange("h t k -> (h t) k")
                             ).then_inc(consts_in, 16)
                for m in range(2):
                    sp.dma_start(b_dif[rows.start + 32 * m:rows.start + 32 * m + 32, :],
                                 d["decb"][HEADS:24, :, 0:NCOL].rearrange("h t k -> (h t) k")).then_inc(consts_in, 16)
            sp.wait_ge(table_in, 16)
            n_phys = d["cache_nsa"].shape[0]

            with sp.Fori(0, PAIRS) as i:
                def page(b, k):
                    return sp.value_load(table[0:1, bass.ds((2 * i + b) * N_PAGES + k, 1)], min_val=0, max_val=n_phys - 1)

                tok = bass.ds(2 * DEC_T * i + SEQ, 2 * DEC_T)
                new = bass.ds(2 * DEC_T * i, 2 * DEC_T)
                sp.wait_ge(turned, N * i + LAST[FEW] + 1)
                for dst, src in ((qn[:], d["q"][tok, :]), (qd[:], d["qd"][tok, :]), (kc[:], d["kc_s"][bass.ds(P * i, P), :])):
                    sp.dma_start(dst, src).then_inc(q_in, 16)
                sp.wait_ge(nsa_mm, i + 1)
                sp.sem_inc(begun_sp, 1)
                for k in range(N_PAGES):
                    for b in range(2):
                        sp.dma_start(sel[:, b, k, :], d["cache_nsa"][bass.ds(page(b, k), 1), :, 2 * KVW:4 * KVW]
                                     .rearrange("n p e -> (n p) e")).then_inc(sel_in[k], 16)
                for k in range(WINDOW // P):
                    for b in range(2):
                        sp.dma_start(win[:, b, k, :], d["cache_win"][bass.ds(2 * i + b, 1), P * k:P * (k + 1), :]
                                     .rearrange("n p e -> (n p) e")).then_inc(win_in[k], 16)
                sp.wait_ge(diff_mm, i + 1)
                sp.dma_start(vc[:], d["vc_s"][bass.ds(P * i, P), :]).then_inc(new_in, 16)
                for dst, src in ((sel_n, d["nsa_s"][new, 2 * KVW:4 * KVW]), (dk_n, d["diff_s"][new, 0:1024]),
                                 (dv_n, d["diff_s"][new, 1024:2048])):
                    sp.dma_start(dst[:], src.rearrange("(b t) e -> t b e", b=2)).then_inc(new_in, 16)
                sp.dma_start(win_n[:], d["win_s"][bass.ds(2 * i, 2), WINDOW - DEC_T:WINDOW, :].rearrange("b t e -> t b e")
                             ).then_inc(new_in, 16)
                with nc.allow_non_contiguous_dma("three gates of a head"):
                    for b in range(2):
                        sp.dma_start(gates[ROWS * b:ROWS * (b + 1), :],
                                     d["g"][bass.ds(2 * DEC_T * i + SEQ + DEC_T * b, DEC_T), :]
                                     .rearrange("t (h c) -> h t c", c=3)).then_inc(new_in, 16)

                def load_k(k):
                    first = N * i + AT["dif", k - 2, 3] + 1 + TURN_CREDIT if k >= 2 else N * i + AT["dif", k + 6, 3] + 1
                    sp.wait_ge(turned, first)
                    sp.sem_inc(begun_sp, 1)
                    for b in range(2):
                        sp.dma_start(dk[:, k % 2, b, :], d["cache_diff"][bass.ds(page(b, k), 1), :, 0:1024]
                                     .rearrange("n p e -> (n p) e")).then_inc(dk_in[k % 2], 16)

                def load_v(k):
                    for b in range(2):
                        sp.dma_start(dv[:, b, k, :], d["cache_diff"][bass.ds(page(b, k), 1), :, 1024:2048]
                                     .rearrange("n p e -> (n p) e")).then_inc(dv_in[k], 16)

                load_k(0)
                load_k(1)
                for k in range(N_PAGES):
                    load_v(k)
                    if k + 2 < N_PAGES:
                        load_k(k + 2)

        @block.gpsimd
        def _(pool):
            with pool.Fori(0, PAIRS) as i:
                pool.wait_ge(nsa_out, i + 2)
                pool.sem_inc(begun_pool, 1)
                for b in range(2):
                    pool.dma_start(d["oa"][bass.ds(2 * DEC_T * i + SEQ + DEC_T * b, DEC_T), :].rearrange("t (h e) -> h t e", e=DK),
                                   o_n[ROWS * b:ROWS * (b + 1), :]).then_inc(nsa_stored, 16)
                pool.wait_ge(diff_out, i + 2)
                pool.sem_inc(begun_pool, 1)
                for b in range(2):
                    for half in range(2):
                        at = ROWS * b + 32 * half + 16 * half
                        pool.dma_start(d["ob"][bass.ds(2 * DEC_T * i + SEQ + DEC_T * b, DEC_T), 512 * half:512 * (half + 1)]
                                       .rearrange("t (h e) -> h t e", e=DV), o_d[at:at + 16, :]).then_inc(diff_stored, 16)
                pool.wait_ge(nsa_stored, 32 * i + 32)
                pool.sem_inc(o_n_free, 1)
                pool.wait_ge(diff_stored, 64 * i + 64)
                pool.sem_inc(o_d_free, 1)
            pool.wait_ge(nsa_stored, 32 * PAIRS)
            pool.wait_ge(diff_stored, 64 * PAIRS)

        @block.tensor
        def _(pe):
            pe.wait_ge(consts_in, 16 * 16)

            def stand():
                pe.sem_inc(begun_pe, 1)

            def turn(i, j):
                kind, k, m = STEPS[j]
                bank = ps_t[:, j % 3, :]
                if kind in ("sel", "win"):
                    src, arrived = (sel, sel_in) if kind == "sel" else (win, win_in)
                    pe.wait_ge(arrived[k], 32 * i + 32)
                    for b in range(2):
                        for g in range(2):
                            c = 2 * b + g
                            ins = pe.transpose(bank[:, P * c:P * (c + 1)], src[:, b, k, P * g:P * (g + 1)], ident[:])
                elif kind in ("sel_n", "win_n", "dif_n"):
                    src = {"sel_n": sel_n, "win_n": win_n, "dif_n": dk_n}[kind]
                    if kind == "sel_n":
                        pe.wait_ge(new_in, 112 * i + 112)
                        stand()
                    for b in range(2):
                        for g in range(2):
                            c = 2 * b + g
                            ins = pe.transpose(bank[:, DEC_T * c:DEC_T * (c + 1)],
                                               src[:, b, P * (2 * m + g):P * (2 * m + g + 1)], ident[0:DEC_T, 0:DEC_T])
                elif kind == "cmp":
                    for g in range(2):
                        ins = pe.transpose(bank[:, P * g:P * (g + 1)], kc[:, P * g:P * (g + 1)], ident[:])
                elif kind == "dif":
                    if m == 0:
                        pe.wait_ge(dk_in[k % 2], 128 * i + 32 * (k // 2) + 32)
                    for b in range(2):
                        for g in range(2):
                            c, h = 2 * b + g, 2 * m + g
                            ins = pe.transpose(bank[:, P * c:P * (c + 1)], dk[:, k % 2, b, P * h:P * (h + 1)], ident[:])
                elif kind == "p_sel" or kind == "p_win":
                    pr, which = (s_sel, 1) if kind == "p_sel" else (s_win, 2)
                    if kind == "p_sel" and k == 0:
                        pe.wait_ge(coef_ready, 5 * i + 4)
                    for x in range(4):
                        cols = slice(P * (4 * k + x), P * (4 * k + x + 1))
                        ins = pe.matmul(bank[:, P * x:P * (x + 1)], pr[:, cols], cm[:, which, :], start=True, stop=True)
                elif kind == "p_few":
                    for x, (pr, which, first) in enumerate(((s_sel, 1, PAST), (s_win, 2, WINDOW))):
                        pe.matmul(bank[0:DEC_T, P * x:P * (x + 1)], pr[:, first:first + DEC_T], cm[:, which, :], start=True, stop=True)
                    for b in range(2):
                        rows = slice(ROWS * b, ROWS * (b + 1))
                        ins = pe.matmul(bank[rows, 2 * P + ROWS * b:2 * P + ROWS * (b + 1)], s_cmp[:], cm[:, 0, rows],
                                        start=True, stop=True)
                elif kind == "p_dif":
                    pe.wait_ge(coef_ready, 5 * i + 5)
                    for x in range(N_PAGES):
                        ins = pe.matmul(bank[:, 64 * x:64 * (x + 1)], s_dif[:, P * x:P * (x + 1)], cd[:], start=True, stop=True)
                else:
                    ins = pe.matmul(bank[0:DEC_T, 0:64], s_dif[:, PAST:NCOL], cd[:], start=True, stop=True)
                ins.then_inc(turned, 1)

            def multiply(i, j):
                kind, k, m = STEPS[j]
                tile = slot[:, j % 3, :]
                pe.wait_ge(copied[j % 2], (ODD if j % 2 else EVEN) * i + j // 2 + 1)
                ins = None
                if kind in ("sel", "win", "sel_n", "win_n", "cmp", "dif", "dif_n"):
                    bank, at = score_place(kind, k)
                    n = {"cmp": CMPS, "sel_n": DEC_T, "win_n": DEC_T, "dif_n": DEC_T}.get(kind, P)
                    group = {("sel", 0): SEL0, ("sel", 4): SEL1, ("win", 0): WIN0, ("sel_n", 0): FEW, ("dif", 0): DIF0,
                             ("dif", 4): DIF1}.get((kind, k))
                    if group is not None and m == 0:
                        pe.wait_ge(scored, 6 * i + group + 1)
                    for g in range(2):
                        for b in range(2):
                            lhs = qdb[:, 2 * m + g, b, :] if kind in ("dif", "dif_n") else qb[:, g, b, :]
                            c = (2 * b + g) * n
                            if kind == "cmp":
                                c = P * g + CMPS * b
                            first = g == 0 and m == 0
                            last = g == 1 and (kind not in ("dif", "dif_n") or m == 3)
                            ins = pe.matmul(ps_s[ROWS * b:ROWS * (b + 1), bank, at:at + n], lhs, tile[:, c:c + n],
                                            start=first, stop=last)
                    if j in LAST:
                        ins.then_inc(scores_mm, 1)
                elif kind in ("p_sel", "p_win"):
                    if kind == "p_sel" and k == 0:
                        pe.wait_ge(nsa_read, i + 1)
                    for x in range(4):
                        v = sel[:, :, 4 * k + x, KVW:2 * KVW] if kind == "p_sel" else win[:, :, x, KVW:2 * KVW]
                        for b in range(2):
                            ins = pe.matmul(ps_n[ROWS * b:ROWS * (b + 1), 0:KVW], tile[:, P * x + ROWS * b:P * x + ROWS * (b + 1)],
                                            v[:, b, :], start=kind == "p_sel" and k == 0 and x == 0,
                                            stop=kind == "p_win" and x == 3)
                    if kind == "p_win":
                        ins.then_inc(nsa_mm, 1)
                elif kind == "p_few":
                    for x in range(3):
                        for b in range(2):
                            rows = slice(ROWS * b, ROWS * (b + 1)) if x == 2 else slice(0, DEC_T)
                            v = (sel_n[:, b, KVW:2 * KVW], win_n[:, b, KVW:2 * KVW], vc[rows, :])[x]
                            ins = pe.matmul(ps_n[ROWS * b:ROWS * (b + 1), 0:KVW], tile[rows, P * x + ROWS * b:P * x + ROWS * (b + 1)],
                                            v, start=False, stop=False)
                elif kind == "p_dif":
                    pe.wait_ge(diff_read, i + 1)
                    for x in range(N_PAGES):
                        pe.wait_ge(dv_in[x], 32 * i + 32)
                        for b in range(2):
                            for half in range(2):
                                o = 64 * b + 32 * half
                                ins = pe.matmul(ps_d[o:o + 32, :], tile[:, 64 * x + 32 * b:64 * x + 32 * b + 32],
                                                dv[:, b, x, CW * half:CW * (half + 1)], start=x == 0, stop=False)
                else:
                    stand()
                    for b in range(2):
                        for half in range(2):
                            o = 64 * b + 32 * half
                            ins = pe.matmul(ps_d[o:o + 32, :], tile[0:DEC_T, 32 * b:32 * b + 32],
                                            dv_n[:, b, CW * half:CW * (half + 1)], start=False, stop=True)
                    ins.then_inc(diff_mm, 1)

            with pe.Fori(0, PAIRS) as i:
                pe.wait_ge(q_in, 48 * i + 48)
                pe.wait_ge(q_laid, i + 1)
                stand()
                for x in range(16):
                    src = qp if x < 8 else qd
                    ins = pe.transpose(ps_n[:, Q_AT + 8 * x:Q_AT + 8 * x + 8], src[:, P * (x % 8):P * (x % 8 + 1)],
                                       ident[0:2 * DEC_T, 0:2 * DEC_T])
                ins.then_inc(q_turned, 1)
                pe.wait_ge(q_ready, i + 1)
                for j in range(N + 2):
                    if j < N:
                        turn(i, j)
                    if j >= 2:
                        multiply(i, j - 2)
                    if j - 2 == IMP_1:
                        pe.wait_ge(coef_ready, 5 * i + 1)
                        stand()
                        pe.matmul(ps_n[0:CMPS, PG_AT:PG_AT + P], s_cmp[:], gm[:], start=True, stop=True).then_inc(pg_mm, 1)
                    if j - 2 == IMP_2:
                        pe.wait_ge(pg_copied, i + 1)
                        stand()
                        pe.matmul(ps_n[:, IMP_AT:IMP_AT + N_SLC], pg[:], selw[:], start=True, stop=True).then_inc(imp_mm, 1)

        @block.scalar
        def _(act):
            act.wait_ge(lam_dot, 1)
            nc.scalar.activation(lam[:, 1:3], lam[:, 1:3], ACT.Exp).then_inc(lam_exp, 1)
            with act.Fori(0, PAIRS) as i:
                def exp(kind, tile, level):
                    act.wait_ge(max_ready, 4 * i + level)
                    nc.scalar.activation(tile, tile, ACT.Exp, scale=-1.0, bias=nm[:, kind, 3:4],
                                         accum_out=rs[:, kind:kind + 1]).then_inc(probs, 1)

                for j in range(0, N, 2):
                    act.wait_ge(turned, N * i + j + 1 + TURN_CREDIT)
                    todo = pieces(j)
                    for x, (rows, cols) in enumerate(todo):
                        ins = nc.scalar.activation(slot[rows, j % 3, cols], ps_t[rows, j % 3, cols], ACT.Copy)
                    ins.then_inc(copied[0], 1)
                    if j == LAST[FEW] + 2:
                        exp(0, s_cmp[:], 1)
                        exp(2, s_win[:], 2)
                    if j == LAST[FEW] + 12:
                        exp(1, s_sel[:], 3)
                    if j == LAST[DIF1] + 2:
                        exp(3, s_dif[:], 4)
                act.wait_ge(o_sq, 2 * i + 2)
                nc.scalar.activation(rr[:, 7:8], rr[:, 6:7], ACT.Sqrt).then_inc(o_root, 1)

        @block.vector
        def _(dve):
            def stand():
                dve.sem_inc(begun, 1)

            nc.vector.nop().then_inc(turned, TURN_CREDIT)
            nc.vector.nop().then_inc(scored, 2)
            for x in (nsa_mm, diff_mm, nsa_read, diff_read, nsa_out, diff_out, o_n_free, o_d_free):
                nc.vector.nop().then_inc(x, 1)
            step = Chain(dve, step_sem)
            step(nc.vector.memset(qb[:], 0.0))
            step(nc.vector.memset(qdb[:], 0.0))
            dve.wait_ge(consts_in, 16 * 16)
            lambda_steps(nc, dve, lam_exp, lam, lv, step, lam_dot)
            step(nc.vector.tensor_scalar(gain[:], gain[:], 1.0 - LAM_INIT, None, ALU.mult))
            step(nc.vector.scalar_tensor_tensor(out=lam[:, 3:4], in0=con[:, C_MAP + 1:C_MAP + 2], scalar=lam[:, 0:1],
                                                in1=con[:, C_MAP:C_MAP + 1], op0=ALU.mult, op1=ALU.add))
            step(nc.vector.tensor_tensor(b_win[:, 0:DEC_T], b_win[:, 0:DEC_T], con[:, C_WIN:C_WIN + DEC_T], ALU.add))
            done = step.n

            with dve.Fori(0, PAIRS) as i:
                chain = Chain(dve, step_sem, CHAIN * i + done)

                def lowest(kind, piece, out, in0, in1, last=None):
                    stand()
                    ins = nc.vector.tensor_tensor_reduce(out=out, in0=in0, in1=in1, scale=-1.0, scalar=3e38 if kind else 1e29,
                                                         op0=ALU.add, op1=ALU.min,
                                                         accum_out=nm[:, kind, piece:piece + 1])
                    if last is None:
                        chain(ins)
                    else:
                        ins.then_inc(last, 1)

                def least(kind, n):
                    nc.vector.tensor_reduce(nm[:, kind, 3:4], nm[:, kind, 0:n], AX.X, ALU.min).then_inc(max_ready, 1)

                def read(group):
                    dve.wait_ge(scores_mm, 6 * i + group + 1)
                    bank = ps_s[:, group % 2, :]
                    if group in (SEL0, SEL1):
                        cols = slice(CW * group, CW * (group + 1))
                        nc.vector.tensor_tensor(s_sel[:, cols], bank, b_nsa[:, cols], ALU.add).then_inc(scored, 1)
                    elif group == WIN0:
                        lowest(2, 0, s_win[:, 0:WINDOW], bank, b_win[:, 0:WINDOW], scored)
                    elif group == FEW:
                        dve.wait_ge(scored, 6 * i + 2 + WIN0 + 1)
                        c0 = CMP_BLOCK - 1
                        lowest(0, 3, s_cmp[:], bank[:, F_CMP:F_CMP + CMPS], b_nsa[:, c0:c0 + CMP_STRIDE * (CMPS - 1) + 1:CMP_STRIDE])
                        nc.vector.nop().then_inc(max_ready, 1)
                        lowest(2, 1, s_win[:, WINDOW:], bank[:, F_WIN:F_WIN + DEC_T], b_win[:, WINDOW:])
                        least(2, 2)
                        lowest(3, 2, s_dif[:, PAST:], bank[:, F_DIF:F_DIF + DEC_T], b_dif[:, PAST:])
                        nc.vector.tensor_tensor(s_sel[:, PAST:], bank[:, F_SEL:F_SEL + DEC_T], b_nsa[:, PAST:NCOL],
                                                ALU.add).then_inc(scored, 1)
                    else:
                        k = group - DIF0
                        cols = slice(CW * k, CW * (k + 1))
                        lowest(3, k, s_dif[:, cols], bank, b_dif[:, cols], scored)

                def inverse(kind):
                    chain(nc.vector.tensor_scalar(rr[:, kind:kind + 1], rs[:, kind:kind + 1], TINY, None, ALU.max))
                    chain(nc.vector.reciprocal(rr[:, kind:kind + 1], rr[:, kind:kind + 1]))

                dve.wait_ge(q_in, 48 * i + 48)
                for gp in range(2):
                    ins = nc.vector.tensor_copy(qp[:, 512 * gp:512 * (gp + 1)].rearrange("p (h g e) -> p h g e", h=HPG, g=2),
                                                qn[:, 512 * gp:512 * (gp + 1)].rearrange("p (g h e) -> p h g e", g=2, h=HPG))
                ins.then_inc(q_laid, 1)
                dve.wait_ge(q_turned, i + 1)
                for gp in range(2):
                    for g2 in range(2):
                        half, g = slice(DK * g2, DK * (g2 + 1)), 2 * gp + g2
                        nc.vector.tensor_copy(
                            qb[half, gp, :, 16 * g:16 * (g + 1)].rearrange("p b (h t) -> p h b t", t=DEC_T),
                            ps_n[half, Q_AT + 32 * gp:Q_AT + 32 * (gp + 1)].rearrange("p (h b t) -> p h b t", h=HPG, t=DEC_T))
                for m in range(2):
                    half = slice(DD * m, DD * (m + 1))
                    base = qdb[half, 0, 0, 32 * m:32 * m + 1]
                    out = bass.AP(tensor=base.tensor, offset=base.offset,
                                  ap=[list(base.ap[0]), [2 * ROWS + DEC_T, DHEADS], [ROWS, 2], [1, DEC_T]])
                    ins = nc.vector.tensor_copy(out, ps_n[half, Q_AT + 64:Q_AT + 128].rearrange("p (h b t) -> p h b t", h=DHEADS, t=DEC_T))
                ins.then_inc(q_ready, 1)

                for j in range(1, N, 2):
                    dve.wait_ge(turned, N * i + j + 1 + TURN_CREDIT)
                    for rows, cols in pieces(j):
                        ins = nc.vector.tensor_copy(slot[rows, j % 3, cols], ps_t[rows, j % 3, cols])
                    ins.then_inc(copied[1], 1)
                    if j in READ_AT:
                        read(READ_AT[j])
                    if j == GROUP_AT:
                        dve.wait_ge(probs, 4 * i + 1)
                        inverse(0)
                        nc.vector.tensor_scalar(gm[:], con[:, C_GROUP:C_GROUP + P], rr[:, 0:1], None, ALU.mult).then_inc(coef_ready, 1)
                    if j == SHARE_AT:
                        dve.wait_ge(pg_mm, i + 1)
                        nc.vector.tensor_copy(pg[:], ps_n[0:CMPS, PG_AT:PG_AT + P]).then_inc(pg_copied, 1)
                    if j == CHOOSE_AT:
                        dve.wait_ge(imp_mm, i + 1)
                        dve.wait_ge(scored, 6 * i + 2 + FEW + 1)
                        free = slice(1, N_SLC - 2)
                        imp = ps_n[:, IMP_AT:IMP_AT + N_SLC]
                        idx = con[:, C_IDX:C_IDX + N_SLC]
                        chain(nc.vector.tensor_reduce(rr[:, 4:5], imp[:, free], AX.X, ALU.min))
                        chain(nc.vector.scalar_tensor_tensor(out=pick[:, 0, free], in0=imp[:, free], scalar=rr[:, 4:5],
                                                             in1=idx[:, free], op0=ALU.is_equal, op1=ALU.mult))
                        chain(nc.vector.tensor_reduce(rr[:, 5:6], pick[:, 0, free], AX.X, ALU.max))
                        chain(nc.vector.tensor_scalar(pick[:, 1, :], idx, rr[:, 5:6], NEG, ALU.is_equal, ALU.mult))
                        view = s_sel[:, 0:PAST].rearrange("p (n e) -> p n e", e=SEL_BLOCK)
                        lowest(1, 0, view, view, pick[:, 1, 0:N_SLC - 1].unsqueeze(2).to_broadcast([P, N_SLC - 1, SEL_BLOCK]))
                        lowest(1, 1, s_sel[:, PAST:], s_sel[:, PAST:], pick[:, 1, N_SLC - 1:N_SLC].to_broadcast([P, DEC_T]))
                        least(1, 2)
                    if j == SCALE_AT:
                        dve.wait_ge(probs, 4 * i + 3)
                        dve.wait_ge(new_in, 112 * i + 112)
                        dve.wait_ge(coef_ready, 5 * i + 1)
                        inverse(1)
                        inverse(2)
                        chain(nc.vector.tensor_tensor(rr[:, 0:3], rr[:, 0:3], gates[:], ALU.mult))
                        for k in range(3):
                            nc.vector.tensor_scalar(cm[:, k, :], ident[:], rr[:, k:k + 1], None,
                                                    ALU.mult).then_inc(coef_ready, 1)
                    if j == SCALE_D_AT:
                        dve.wait_ge(scored, 6 * i + 2 + DIF1 + 1)
                        least(3, 3)
                        dve.wait_ge(probs, 4 * i + 4)
                        inverse(3)
                        chain(nc.vector.tensor_tensor(rr[:, 3:4], rr[:, 3:4], lam[:, 3:4], ALU.mult))
                        nc.vector.tensor_scalar(cd[:], con[:, C_STACK:C_STACK + 64], rr[:, 3:4], None, ALU.mult).then_inc(coef_ready, 1)
                dve.wait_ge(nsa_mm, i + 2)
                chain(nc.vector.tensor_tensor(part[:, 0:KVW], ps_n[:, 0:KVW], con[:, C_NSA:C_NSA + KVW], ALU.mult))
                nc.vector.nop().then_inc(nsa_read, 1)
                dve.wait_ge(o_n_free, i + 1)
                nc.vector.tensor_reduce(o_n[:], part[:, 0:KVW].rearrange("p (g e) -> p e g", e=DK), AX.X, ALU.add).then_inc(nsa_out, 1)
                dve.wait_ge(nsa_out, i + 2)
                dve.wait_ge(diff_mm, i + 2)
                chain(nc.vector.tensor_tensor(part[:], ps_d[:], con[:, C_DIFF:C_DIFF + CW], ALU.mult))
                nc.vector.nop().then_inc(diff_read, 1)
                dve.wait_ge(o_d_free, i + 1)
                chain(nc.vector.tensor_reduce(o_d[:], part[:].rearrange("p (h e) -> p e h", e=DV), AX.X, ALU.add))
                chain(nc.vector.tensor_tensor(part[:, 0:DV], o_d[:], o_d[:], ALU.mult))
                nc.vector.tensor_reduce(rr[:, 6:7], part[:, 0:DV], AX.X, ALU.add).then_inc(o_sq, 1)
                dve.wait_ge(o_sq, 2 * i + 1)
                nc.vector.tensor_scalar(rr[:, 6:7], rr[:, 6:7], 1.0 / DV, EPS, ALU.mult, ALU.add).then_inc(o_sq, 1)
                dve.wait_ge(o_root, i + 1)
                chain(nc.vector.reciprocal(rr[:, 7:8], rr[:, 7:8]))
                nc.vector.scalar_tensor_tensor(out=o_d[:], in0=o_d[:], scalar=rr[:, 7:8], in1=gain[:],
                                               op0=ALU.mult, op1=ALU.mult).then_inc(diff_out, 1)
                assert chain.n == CHAIN, chain.n


HALF = D_FF // 2
FT = HALF // P
WS = 2048
PAIR = TOKENS // 2


def finish(nc, d):
    with ExitStack() as ctx:
        s = Space(nc, ctx, "fi")
        h = s.sb("h", [P, TT, D_MODEL])
        th = s.sb("th", [P, KT, TOKENS], F32R)
        tl = s.sb("tl", [P, KT, TOKENS], F32R)
        fh = s.sb("fh", [P, FT, TOKENS], F32R)
        fl = s.sb("fl", [P, FT, TOKENS], F32R)
        yt = s.sb("yt", [P, KT, TOKENS])
        w = s.sb("w", [P, 2, WS])
        wh = s.sb("wh", [P, 2, WS], F32R)
        wl = s.sb("wl", [P, 2, WS], F32R)
        buf = s.sb("buf", [P, 2, 4, CW])
        more = yt[:].rearrange("p a c -> p (a c)")[:, 0:8 * CW].rearrange("p (u j c) -> p u j c", u=2, j=4)
        places = [buf[:, 0], buf[:, 1], more[:, 0], more[:, 1]]
        relu = buf[:, 0, 0:2, :].rearrange("p a b -> p (a b)")[:, 0:TOKENS]
        sqr = buf[:, 1, 0:2, :].rearrange("p a b -> p (a b)")[:, 0:TOKENS]
        ident = s.sb("ident", [P, P])
        gain = s.sb("gain", [P, D_MODEL])
        ssum = s.sb("ssum", [P, TT])
        rstd = s.sb("rstd", [P, TT])
        ps = s.ps("ps", [P, 8, CW])

        h_in, consts_in = s.sem("h_in"), s.sem("consts_in")
        o_in = [s.sem(f"o_in{k}") for k in range(4)]
        w_in = [s.sem(f"w_in{k}") for k in range(2)]
        w_hi, w_split = s.sem("w_hi"), s.sem("w_split")
        merged, turned, t_hi, t_lo = s.sem("merged"), s.sem("turned"), s.sem("t_hi"), s.sem("t_lo")
        o_done, up_done, down_done, h_added = s.sem("o_done"), s.sem("up_done"), s.sem("down_done"), s.sem("h_added")
        h_sq, h_rstd = s.sem("h_sq"), s.sem("h_rstd")
        relued, f_hi, f_lo, y_added = (s.sem(n) for n in ("relued", "f_hi", "f_lo", "y_added"))
        f_made = [s.sem(f"f_made{f}") for f in range(2)]
        y_turned, y_ready, y_out = s.sem("y_turned"), s.sem("y_ready"), s.sem("y_out")
        step_sem, zeroed, y_zeroed, second_part = (s.sem(n) for n in ("dve_step", "zeroed", "y_zeroed", "second_part"))
        block = ctx.enter_context(nc.Block())

        rows = lambda t: P if t < QT else N_DEC
        units = [(t, k) for t in range(TT) for k in range(2)]
        NO = 4
        NU = HALF // 256
        w_o = d["w_o"].rearrange("(k p) n -> p k n", p=P)
        w_up = d["w_up"].rearrange("(k p) n -> p k n", p=P)
        w_down = d["w_down"].rearrange("(k p) n -> p k n", p=P)

        def piece(n):
            if n < NO:
                return w_o[:, :, 256 * n:256 * (n + 1)], KT
            half, c = divmod(n - NO, 2 * NU)
            if c < NU:
                return w_up[:, :, HALF * half + 256 * c:HALF * half + 256 * (c + 1)], KT
            return w_down[:, FT * half:FT * (half + 1), P * (c - NU):P * (c - NU + 1)], FT

        N_ALL = NO + 4 * NU

        @block.sync
        def _(sp):
            def load(n):
                if n >= 2:
                    sp.wait_ge(w_split, n - 1)
                src, k = piece(n)
                sp.dma_start(w[:, n % 2, :].rearrange("p (k c) -> p k c", k=k), src).then_inc(w_in[n % 2], 16)

            for u, (t, k) in enumerate(units):
                if u >= 4:
                    sp.wait_ge(turned, u - 3)
                cols = slice(CW * k, CW * (k + 1))
                for j, name in enumerate(("ga", "oa", "gb", "ob")):
                    sp.dma_start(places[u % 4][0:rows(t), j, :], d[name][P * t:P * t + rows(t), cols]).then_inc(o_in[u % 4], 16)
                if u == 0:
                    sp.dma_start(ident[:], d["ident"]).then_inc(consts_in, 16)
                    sp.dma_start(gain[:], spread(d["mlp_norm"], P)).then_inc(consts_in, 16)
                if u == 3:
                    load(0)
                    load(1)
            for t in range(TT):
                src = d["x_prompt"][P * t:P * (t + 1), :] if t < QT else d["x_sample"]
                sp.dma_start(h[0:rows(t), t, :], src).then_inc(h_in, 16)
            for n in range(2, N_ALL):
                load(n)
            for t in range(TT):
                sp.wait_ge(y_ready, t + 1)
                dst = d["y_prompt"][P * t:P * (t + 1), :] if t < QT else d["y_sample"]
                sp.dma_start(dst, h[0:rows(t), t, :]).then_inc(y_out, 16)
            sp.wait_ge(y_out, 16 * TT)

        @block.gpsimd
        def _(pool):
            for u, (t, k) in enumerate(units):
                b = places[u % 4][0:rows(t)]
                pool.wait_ge(o_in[u % 4], 64 * (u // 4 + 1))
                nc.gpsimd.tensor_tensor(b[:, 2, :], b[:, 2, :], b[:, 3, :], ALU.mult).then_inc(second_part, 1)
            pool.wait_ge(turned, len(units))
            nc.gpsimd.memset(yt[:], 0.0).then_inc(y_zeroed, 1)
            pool.wait_ge(w_hi, 5)
            nc.gpsimd.tensor_tensor(wl[:, 0, :], w[:, 0, :], wh[:, 0, :].bitcast(F32), ALU.subtract).then_inc(w_split, 1)

        @block.scalar
        def _(act):
            def split(n):
                act.wait_ge(w_in[n % 2], 16 * (n // 2 + 1))
                if n >= 2:
                    act.wait_ge(o_done, TT * (n - 1))
                nc.scalar.activation(wh[:, n % 2, :], w[:, n % 2, :], ACT.Copy).then_inc(w_hi, 1)

            def split_ahead(u, n, done, level):
                act.wait_ge(w_in[u], 8 * n + (16 if u == 0 else 8))
                act.wait_ge(done, level)
                nc.scalar.activation(wh[:, u, :], w[:, u, :], ACT.Copy).then_inc(w_hi, 1)

            def high_parts(u):
                t, k = units[u % len(units)]
                act.wait_ge(turned, u + 1)
                nc.scalar.activation(th[:, 4 * k:4 * k + 4, P * t:P * t + rows(t)],
                                     ps[:, 6 + u % 2, 0:4 * rows(t)].rearrange("p (k c) -> p k c", k=4),
                                     ACT.Copy).then_inc(t_hi, 1)

            for u in range(len(units)):
                high_parts(u)
                if u == 5:
                    split(0)
            split(1)
            split(2)
            split(3)
            for t in range(TT):
                act.wait_ge(h_added, TT * (NO - 1) + t + 1)
                if t == 0:
                    act.wait_ge(zeroed, 1)
                else:
                    act.wait_ge(h_sq, t)
                nc.scalar.activation(buf[0:rows(t), 0, 0:2, :].rearrange("p a b -> p (a b)"), h[0:rows(t), t, :],
                                     ACT.Square, accum_out=ssum[0:rows(t), t:t + 1]).then_inc(h_sq, 1)
            act.wait_ge(h_rstd, 1)
            nc.scalar.activation(rstd[:], ssum[:], ACT.Sqrt).then_inc(h_sq, 1)
            split(4)
            for u in range(len(units)):
                high_parts(len(units) + u)
            split(5)
            for half in range(2):
                first = NO + 2 * NU * half
                with act.Fori(0, NU // 2) as i:
                    for u in range(2):
                        at = NU * half + 2 * i + u
                        for f in range(2):
                            act.wait_ge(up_done, 2 * at + f + 1)
                            nc.scalar.activation(relu.rearrange("p (a c) -> p a c", a=2), ps[:, 2 * f:2 * f + 2, 0:PAIR],
                                                 ACT.Relu).then_inc(relued, 1)
                            act.wait_ge(f_made[f], at + 2)
                            nc.scalar.activation(fh[:, bass.ds(4 * i + 2 * u + f, 1), :].rearrange("p a c -> p (a c)"),
                                                 sqr, ACT.Copy).then_inc(f_hi, 1)
                        split_ahead(u, first + 2 * i + u + 2, up_done, 2 * at + 2)
                last = 1 if half else 0
                with act.Fori(0, NU // 2 - last) as i:
                    for u in range(2):
                        split_ahead(u, first + NU + 2 * i + u + 2, down_done, NU * half + 2 * i + u + 1)

        @block.vector
        def _(dve):
            step = Chain(dve, step_sem)

            def split(n):
                dve.wait_ge(w_hi, n + 1)
                nc.vector.tensor_tensor(wl[:, n % 2, :], w[:, n % 2, :], wh[:, n % 2, :].bitcast(F32),
                                        ALU.subtract).then_inc(w_split, 1)

            def low_parts(u):
                t, k = units[u % len(units)]
                dve.wait_ge(t_hi, u + 1)
                view = (slice(None), slice(4 * k, 4 * k + 4), slice(P * t, P * t + rows(t)))
                nc.vector.tensor_tensor(tl[view], ps[:, 6 + u % 2, 0:4 * rows(t)].rearrange("p (k c) -> p k c", k=4),
                                        th[view].bitcast(F32), ALU.subtract).then_inc(t_lo, 1)

            nc.vector.memset(ssum[:], 1.0).then_inc(zeroed, 1)
            nc.vector.nop().then_inc(f_lo, 1)
            for f in range(2):
                nc.vector.nop().then_inc(f_made[f], 1)
                nc.vector.nop().then_inc(y_added, 1)
            for u, (t, k) in enumerate(units):
                b = places[u % 4][0:rows(t)]
                dve.wait_ge(o_in[u % 4], 64 * (u // 4 + 1))
                step(nc.vector.tensor_tensor(b[:, 0, :], b[:, 0, :], b[:, 1, :], ALU.mult))
                dve.wait_ge(second_part, u + 1)
                nc.vector.tensor_tensor(b[:, 0, :], b[:, 0, :], b[:, 2, :], ALU.add).then_inc(merged, 1)
                if u >= 1:
                    low_parts(u - 1)
                if u == 8:
                    split(0)
            low_parts(len(units) - 1)
            split(1)
            dve.wait_ge(h_in, 16 * TT)
            for n in range(NO):
                for t in range(TT):
                    dve.wait_ge(o_done, TT * n + t + 1)
                    hv = h[0:rows(t), t, 256 * n:256 * (n + 1)]
                    nc.vector.tensor_tensor(hv, ps[0:rows(t), t, 0:256], hv, ALU.add).then_inc(h_added, 1)
                if n + 2 < NO:
                    split(n + 2)
            dve.wait_ge(h_sq, TT)
            nc.vector.tensor_scalar(ssum[:], ssum[:], 1.0 / D_MODEL, EPS, ALU.mult, ALU.add).then_inc(h_rstd, 1)
            dve.wait_ge(h_sq, TT + 1)
            step(nc.vector.reciprocal(rstd[:], rstd[:]))
            for u, (t, k) in enumerate(units):
                n = len(units) + u
                if u >= 2:
                    dve.wait_ge(turned, n - 1)
                nc.vector.scalar_tensor_tensor(out=buf[0:rows(t), u % 2, 0, :], in0=h[0:rows(t), t, CW * k:CW * (k + 1)],
                                               scalar=rstd[0:rows(t), t:t + 1], in1=gain[0:rows(t), CW * k:CW * (k + 1)],
                                               op0=ALU.mult, op1=ALU.mult).then_inc(merged, 1)
                if u >= 1:
                    low_parts(n - 1)
            low_parts(2 * len(units) - 1)
            dve.wait_ge(y_zeroed, 1)
            dve.wait_ge(w_split, 5)
            split(5)

            def split_dyn(u, n):
                dve.wait_ge(w_hi, n + 1)
                nc.vector.tensor_tensor(wl[:, u, :], w[:, u, :], wh[:, u, :].bitcast(F32), ALU.subtract).then_inc(w_split, 1)

            for half in range(2):
                first = NO + 2 * NU * half
                with dve.Fori(0, NU // 2) as i:
                    for u in range(2):
                        for f in range(2):
                            at = 2 * (NU * half + 2 * i + u) + f
                            dve.wait_ge(relued, at + 1)
                            dve.wait_ge(f_lo, at + 1)
                            nc.vector.scalar_tensor_tensor(out=sqr.rearrange("p (a c) -> p a c", a=2),
                                                           in0=ps[:, 2 * f:2 * f + 2, 0:PAIR], scalar=0.0,
                                                           in1=relu.rearrange("p (a c) -> p a c", a=2),
                                                           op0=ALU.max, op1=ALU.mult).then_inc(f_made[f], 1)
                            dve.wait_ge(f_hi, at + 1)
                            ft = bass.ds(4 * i + 2 * u + f, 1)
                            nc.vector.tensor_tensor(fl[:, ft, :].rearrange("p a c -> p (a c)"), sqr,
                                                    fh[:, ft, :].rearrange("p a c -> p (a c)").bitcast(F32),
                                                    ALU.subtract).then_inc(f_lo, 1)
                        split_dyn(u, first + 2 * i + u + 2)

                def add_y(i, u):
                    dve.wait_ge(down_done, NU * half + 2 * i + u + 1)
                    y = yt[:, bass.ds(2 * i + u, 1), :].rearrange("p b (a c) -> p (b a) c", a=2)
                    nc.vector.tensor_tensor(y, ps[:, 4 + 2 * u:6 + 2 * u, 0:PAIR], y, ALU.add).then_inc(y_added, 1)

                last = 1 if half else 0
                with dve.Fori(0, NU // 2 - last) as i:
                    for u in range(2):
                        add_y(i, u)
                        split_dyn(u, first + NU + 2 * i + u + 2)
                if half:
                    for u in range(2):
                        add_y(NU // 2 - 1, u)
            for t in range(TT):
                for k in range(2):
                    dve.wait_ge(y_turned, 2 * t + k + 1)
                    hv = h[0:rows(t), t, CW * k:CW * (k + 1)]
                    ins = nc.vector.tensor_tensor(hv, ps[0:rows(t), k + 2 * (t % 2), :], hv, ALU.add)
                    if k == 0:
                        ins.then_inc(step_sem, 1)
                ins.then_inc(y_ready, 1)

        @block.tensor
        def _(pe):
            pe.wait_ge(consts_in, 32)

            def turn(u):
                t, k = units[u % len(units)]
                pe.wait_ge(merged, u + 1)
                if u >= 2:
                    pe.wait_ge(t_lo, u - 1)
                n = rows(t)
                src = places[u % 4] if u < len(units) else places[u % 2]
                for j in range(4):
                    ins = pe.transpose(ps[:, 6 + u % 2, n * j:n * (j + 1)], src[0:n, 0, P * j:P * (j + 1)],
                                       ident[0:n, 0:n])
                ins.then_inc(turned, 1)

            for u in range(len(units)):
                turn(u)
            pe.wait_ge(t_lo, len(units))
            for n in range(NO):
                pe.wait_ge(w_split, n + 1)
                hi = wh[:, n % 2, :].rearrange("p (k c) -> p k c", k=KT)
                lo = wl[:, n % 2, :].rearrange("p (k c) -> p k c", k=KT)
                for t in range(TT):
                    if n:
                        pe.wait_ge(h_added, TT * (n - 1) + t + 1)
                    tok = slice(P * t, P * t + rows(t))
                    out = ps[0:rows(t), t, 0:256]
                    for k in range(KT):
                        pe.matmul(out, th[:, k, tok], hi[:, k, :], start=k == 0, stop=False)
                        pe.matmul(out, th[:, k, tok], lo[:, k, :], start=False, stop=False)
                        ins = pe.matmul(out, tl[:, k, tok], hi[:, k, :], start=False, stop=k == KT - 1)
                    ins.then_inc(o_done, 1)
            for u in range(len(units)):
                turn(len(units) + u)
            pe.wait_ge(t_lo, 2 * len(units))

            def product(out, kts, hi, lo, a_hi, a_lo):
                for k in range(kts):
                    for b in range(2):
                        tok = slice(PAIR * b, PAIR * (b + 1))
                        o = out[:, b, 0:PAIR]
                        pe.matmul(o, hi[:, k, :], a_hi[:, k, tok], start=k == 0, stop=False)
                        pe.matmul(o, hi[:, k, :], a_lo[:, k, tok], start=False, stop=False)
                        ins = pe.matmul(o, lo[:, k, :], a_hi[:, k, tok], start=False, stop=k == kts - 1)
                return ins

            for half in range(2):
                first = NO + 2 * NU * half
                with pe.Fori(0, NU // 2) as i:
                    for u in range(2):
                        at = NU * half + 2 * i + u
                        pe.wait_ge(w_split, first + 2 * i + u + 1)
                        hi = wh[:, u, :].rearrange("p (k c) -> p k c", k=KT)
                        lo = wl[:, u, :].rearrange("p (k c) -> p k c", k=KT)
                        for f in range(2):
                            pe.wait_ge(f_made[f], at + 1)
                            col = slice(P * f, P * (f + 1))
                            product(ps[:, 2 * f:2 * f + 2, :], KT, hi[:, :, col], lo[:, :, col], th, tl).then_inc(up_done, 1)
                pe.wait_ge(f_lo, 2 * NU * (half + 1) + 1)
                with pe.Fori(0, NU // 2) as i:
                    for u in range(2):
                        at = NU * half + 2 * i + u
                        pe.wait_ge(w_split, first + NU + 2 * i + u + 1)
                        pe.wait_ge(y_added, at + 1)
                        hi = wh[:, u, :].rearrange("p (k c) -> p k c", k=FT)
                        lo = wl[:, u, :].rearrange("p (k c) -> p k c", k=FT)
                        product(ps[:, 4 + 2 * u:6 + 2 * u, :], FT, hi, lo, fh, fl).then_inc(down_done, 1)
            pe.wait_ge(y_added, 2 * NU + 2)
            for t in range(TT):
                if t >= 2:
                    pe.wait_ge(y_ready, t - 1)
                for k in range(2):
                    for j in range(4):
                        ins = pe.transpose(ps[0:rows(t), k + 2 * (t % 2), P * j:P * (j + 1)],
                                           yt[:, 4 * k + j, P * t:P * t + rows(t)], ident[:])
                    ins.then_inc(y_turned, 1)


def build(nc, d):
    project(nc, d)
    compress(nc, d)
    prompt_attention(nc, d)
    decode_attention(nc, d)
    finish(nc, d)


VIEWS = {
    "x_prompt": ("x_prompt", (SEQ, D_MODEL)), "x_sample": ("x_sample", (N_DEC, D_MODEL)),
    "cache_nsa_kv": ("cache_nsa", (-1, PAGE, 4 * KVW)), "cache_diff_kv": ("cache_diff", (-1, PAGE, 2 * D_MODEL)),
    "cache_nsa_win": ("cache_win", (DEC_B, WINDOW, 2 * KVW)), "page_table": ("page_table", (1, DEC_B * N_PAGES)),
    "rel_bias_table": ("rel_bias_table", (BUCKETS, HEADS + DHEADS)),
    "w_in": ("w_in", (D_MODEL, N_IN)), "w_o": ("w_o", (D_MODEL, D_MODEL)),
    "w_up": ("w_up", (D_MODEL, D_FF)), "w_down": ("w_down", (D_FF, D_MODEL)),
    **{f"cmp_pe_{x}": (f"cmp_pe_{x}", (CMP_BLOCK, DK)) for x in "kv"},
    **{f"cmp_w1_{x}": (f"cmp_w1_{x}", (CMP_BLOCK * DK, CMP_HID)) for x in "kv"},
    **{f"cmp_w2_{x}": (f"cmp_w2_{x}", (CMP_HID, DK)) for x in "kv"},
    **{x: (x, (-1,)) for x in ("attn_norm", "nsa_q_gain", "nsa_k_gain", "diff_q_gain", "diff_k_gain", "lambda_q1",
                               "lambda_k1", "lambda_q2", "lambda_k2", "diff_subln", "mlp_norm")},
}
SCRATCH = {
    **{x: (TOKENS, D_MODEL) for x in ("q", "qd", "ga", "gb", "oa", "ob")}, "g": (TOKENS, 3 * HEADS),
    "toep": (HEADS + DHEADS, P, STRIP), "decb": (HEADS + DHEADS, DEC_T, DECW),
    "kc_s": (DEC_B * PAST // CMP_STRIDE, KVW), "vc_s": (DEC_B * PAST // CMP_STRIDE, KVW), "kc_p": (CHP, KVW), "vc_p": (CHP, KVW),
}
OUTPUTS = (
    ("y_prompt", (SEQ, D_MODEL), (1, SEQ, D_MODEL)), ("y_sample", (N_DEC, D_MODEL), (DEC_B, DEC_T, D_MODEL)),
    ("nsa_p", (SEQ, 4 * KVW), (1, 1, SEQ, 4, GROUPS, DK)), ("diff_p", (SEQ, 2 * D_MODEL), (1, 1, SEQ, 2, DHEADS, DV)),
    ("win_p", (SEQ, 2 * KVW), (1, 1, SEQ, 2, GROUPS, DK)),
    ("nsa_s", (N_DEC, 4 * KVW), (1, DEC_B, DEC_T, 4, GROUPS, DK)), ("diff_s", (N_DEC, 2 * D_MODEL), (1, DEC_B, DEC_T, 2, DHEADS, DV)),
    ("win_s", (DEC_B, WINDOW, 2 * KVW), (1, DEC_B, WINDOW, 2, GROUPS, DK)),
)


def kernel(**inputs):
    import concourse.bacc as bacc
    from concourse.bass_utils import run_bass_kernel_spmd

    nc = bacc.Bacc("TRN2", target_bir_lowering=False, num_devices=1)
    arrays, d = {}, {}

    def give(name, a):
        arrays[f"in_{name}"] = np.ascontiguousarray(a)
        d[name] = nc.dram_tensor(f"in_{name}", a.shape, mybir.dt.from_np(a.dtype), kind="ExternalInput").ap()

    for source, (name, shape) in VIEWS.items():
        give(name, np.asarray(inputs[source]).reshape(shape))
    for name, a in (("ident", np.eye(P, dtype=np.float32)), ("bucket_hot", bucket_hot()),
                    ("decode_constants", decode_constants()), ("select_weights", select_weights())):
        give(name, a)
    for name, shape in SCRATCH.items():
        d[name] = nc.dram_tensor(f"scratch_{name}", shape, F32, kind="Internal").ap()
    for name, shape, _ in OUTPUTS:
        d[name] = nc.dram_tensor(f"out_{name}", shape, F32, kind="ExternalOutput").ap()
    build(nc, d)
    result = run_bass_kernel_spmd(nc, [arrays], core_ids=[0]).results[0]
    return tuple(result[f"out_{name}"].reshape(shape) for name, _, shape in OUTPUTS)
```
